# Optimizing a Trainium2 kernel written in Bass

```python
import math
import jax, jax.numpy as jnp
from jax import lax
import numpy as np

D_MODEL = 1024
BATCH = 1
SEQ = 256
DEPTH = 2
DEC_BATCH = 8
DEC_SEQ = 8
PAST_LEN = 2048
PAGE_SIZE = 128

SSD_HEAD_DIM = 64
SSD_WIDTH = D_MODEL
SSD_HEADS = SSD_WIDTH // SSD_HEAD_DIM
SSD_GROUPS = 2
SSD_STATE = 128
CONV_WIDTH = 4
CONV_DIM = SSD_WIDTH + 2 * SSD_GROUPS * SSD_STATE
SSD_CHUNK = 128
RET_HEADS = 4
RET_WIDTH = D_MODEL
RET_V_DIM = RET_WIDTH // RET_HEADS
RET_QK_DIM = RET_V_DIM // 2
RET_CHUNK = 128
ROPE_BASE = 10000.0
MIX_WIDTH = SSD_WIDTH + RET_WIDTH
IN_SIZES = (SSD_WIDTH, CONV_DIM, SSD_HEADS, RET_HEADS * RET_QK_DIM, RET_HEADS * RET_QK_DIM, RET_WIDTH, RET_WIDTH)
IN_DIM = SSD_WIDTH + CONV_DIM + SSD_HEADS + 2 * RET_HEADS * RET_QK_DIM + 2 * RET_WIDTH
N_MEM = 256
XA_HEADS = 4
XA_HEAD_DIM = D_MODEL // XA_HEADS
N_EGROUPS = 4
EXPERTS_PER_GROUP = 4
N_EXPERTS = N_EGROUPS * EXPERTS_PER_GROUP
TOP_K = 2
EXPERT_FF = D_MODEL // 2
RMS_EPS = 1e-6

kernel_name = 'hymba_ssd_retention_hmoe_decode_step'

def _rms(x):
    xf = x.astype(jnp.float32)
    return (xf * lax.rsqrt(jnp.mean(xf * xf, axis=-1, keepdims=True) + RMS_EPS)).astype(x.dtype)

def rmsnorm(x, gain):
    return _rms(x) * gain

def _chunk_len(L, c):
    return c if L % c == 0 else L

def _causal_mask(n):
    return jnp.tril(jnp.ones((n, n), dtype=bool))

def retention_log_decay():
    return jnp.log(1.0 - jnp.exp2(-5.0 - jnp.arange(RET_HEADS, dtype=jnp.float32)))

def causal_conv(xbc, prev, w, b):
    L = xbc.shape[1]
    xp = jnp.concatenate([prev.astype(xbc.dtype), xbc], axis=1)
    out = b + xp[:, 0:L] * w[0]
    for j in range(1, CONV_WIDTH):
        out = out + xp[:, j:j + L] * w[j]
    return out, xp[:, L:]

def ssd_scan(x, dt, A, Bm, Cm, state0):
    b, L, H, P = x.shape
    G, N = Bm.shape[2], Bm.shape[3]
    HG = H // G
    cl = _chunk_len(L, SSD_CHUNK)
    nc = L // cl
    f32 = jnp.float32
    xdt = (x.astype(f32) * dt[..., None]).reshape(b, nc, cl, G, HG, P)
    a = (dt * A).reshape(b, nc, cl, G, HG)
    Bc = Bm.astype(f32).reshape(b, nc, cl, G, N)
    Cc = Cm.astype(f32).reshape(b, nc, cl, G, N)
    a_cum = jnp.cumsum(a, axis=2)
    a_t = jnp.moveaxis(a_cum, 2, -1)
    seg = a_t[..., :, None] - a_t[..., None, :]
    Lmat = jnp.exp(jnp.where(_causal_mask(cl), seg, -jnp.inf))
    CB = jnp.einsum('bclgn,bcsgn->bcgls', Cc, Bc)
    y_diag = jnp.einsum('bcgls,bcghls,bcsghp->bclghp', CB, Lmat, xdt)
    decay_to_end = jnp.exp(a_cum[:, :, -1:] - a_cum)
    chunk_states = jnp.einsum('bclgn,bclgh,bclghp->bcghpn', Bc, decay_to_end, xdt)
    chunk_decay = jnp.exp(a_cum[:, :, -1])
    s0 = state0.astype(f32).reshape(b, G, HG, P, N)

    def step(s, inp):
        cs, cd = inp
        return cd[..., None, None] * s + cs, s

    s_final, s_in = lax.scan(step, s0, (jnp.moveaxis(chunk_states, 1, 0), jnp.moveaxis(chunk_decay, 1, 0)))
    s_in = jnp.moveaxis(s_in, 0, 1)
    y_off = jnp.einsum('bclgn,bcghpn,bclgh->bclghp', Cc, s_in, jnp.exp(a_cum))
    y = (y_diag + y_off).reshape(b, L, H, P)
    return y, s_final.reshape(b, H, P, N)

def rotary(x, pos):
    half = x.shape[-1] // 2
    inv = ROPE_BASE ** (-jnp.arange(half, dtype=jnp.float32) / half)
    ang = pos[:, None] * inv[None, :]
    cos = jnp.cos(ang)[None, :, None, :]
    sin = jnp.sin(ang)[None, :, None, :]
    x1, x2 = x[..., :half], x[..., half:]
    return jnp.concatenate([x1 * cos - x2 * sin, x1 * sin + x2 * cos], axis=-1)

def retention_chunkwise(q, k, v, state0, log_gamma):
    b, L, H, dk = q.shape
    dv = v.shape[-1]
    cl = _chunk_len(L, RET_CHUNK)
    nc = L // cl
    q = q.reshape(b, nc, cl, H, dk)
    k = k.reshape(b, nc, cl, H, dk)
    v = v.reshape(b, nc, cl, H, dv)
    idx = jnp.arange(cl, dtype=jnp.float32)
    rel = idx[:, None] - idx[None, :]
    decay = jnp.exp(jnp.where(_causal_mask(cl), rel[None] * log_gamma[:, None, None], -jnp.inf))
    scores = jnp.einsum('bclhd,bcshd->bchls', q, k) * decay
    o_intra = jnp.einsum('bchls,bcshe->bclhe', scores, v)
    k_end = k * jnp.exp((cl - 1 - idx)[:, None] * log_gamma)[:, :, None]
    chunk_kv = jnp.einsum('bclhd,bclhe->bchde', k_end, v)
    chunk_decay = jnp.exp(cl * log_gamma)[:, None, None]

    def step(s, kv):
        return chunk_decay * s + kv, s

    s_final, s_in = lax.scan(step, state0.astype(jnp.float32), jnp.moveaxis(chunk_kv, 1, 0))
    s_in = jnp.moveaxis(s_in, 0, 1)
    q_start = q * jnp.exp((idx + 1.0)[:, None] * log_gamma)[:, :, None]
    o_cross = jnp.einsum('bclhd,bchde->bclhe', q_start, s_in)
    return (o_intra + o_cross).reshape(b, L, H, dv), s_final

def parallel_mixer(h, conv_prev, ssm_prev, ret_prev, pos0, w_in, conv_w, conv_b, dt_bias, a_log, d_skip,
                   ssd_gain, ret_gain, w_out):
    b, L, _ = h.shape
    proj = h @ w_in
    offs = np.cumsum(np.array(IN_SIZES))[:-1].tolist()
    z, xbc, dt_raw, q, k, v, g = jnp.split(proj, offs, axis=-1)
    xbc, conv_new = causal_conv(xbc, conv_prev, conv_w, conv_b)
    xbc = jax.nn.silu(xbc)
    xs, Bm, Cm = jnp.split(xbc, [SSD_WIDTH, SSD_WIDTH + SSD_GROUPS * SSD_STATE], axis=-1)
    xs = xs.reshape(b, L, SSD_HEADS, SSD_HEAD_DIM)
    Bm = Bm.reshape(b, L, SSD_GROUPS, SSD_STATE)
    Cm = Cm.reshape(b, L, SSD_GROUPS, SSD_STATE)
    dt = jax.nn.softplus(dt_raw.astype(jnp.float32) + dt_bias)
    A = -jnp.exp(a_log.astype(jnp.float32))
    y, ssm_new = ssd_scan(xs, dt, A, Bm, Cm, ssm_prev)
    y = (y + d_skip[:, None] * xs).reshape(b, L, SSD_WIDTH) * jax.nn.silu(z)
    y_ssd = _rms(y.reshape(b, L, SSD_GROUPS, SSD_WIDTH // SSD_GROUPS)).reshape(b, L, SSD_WIDTH) * ssd_gain
    pos = (pos0 + jnp.arange(L)).astype(jnp.float32)
    q = rotary(q.reshape(b, L, RET_HEADS, RET_QK_DIM), pos)
    k = rotary(k.reshape(b, L, RET_HEADS, RET_QK_DIM), pos) * (RET_QK_DIM ** -0.5)
    v = v.reshape(b, L, RET_HEADS, RET_V_DIM)
    o, ret_new = retention_chunkwise(q, k, v, ret_prev, retention_log_decay())
    y_ret = _rms(o).reshape(b, L, RET_WIDTH) * ret_gain * jax.nn.silu(g)
    out = jnp.concatenate([y_ssd, y_ret], axis=-1) @ w_out
    return out, conv_new, ssm_new, ret_new

def mem_proj(mem, w):
    b, m, _ = mem.shape
    return (mem @ w).reshape(b, m, XA_HEADS, XA_HEAD_DIM)

def cross_attend(h, mem_k, mem_v, w_q, w_o):
    b, L, _ = h.shape
    q = (h @ w_q).reshape(b, L, XA_HEADS, XA_HEAD_DIM)
    s = jnp.einsum('blhd,bmhd->bhlm', q, mem_k).astype(jnp.float32) * (XA_HEAD_DIM ** -0.5)
    p = jax.nn.softmax(s, axis=-1).astype(mem_v.dtype)
    o = jnp.einsum('bhlm,bmhd->blhd', p, mem_v).reshape(b, L, D_MODEL)
    return o @ w_o

def hier_moe(h, w_rg, b_rg, w_re, b_re, w_gate, w_up, w_down):
    shp = h.shape
    hf = h.reshape(-1, shp[-1])
    g_logits = (hf @ w_rg).astype(jnp.float32) + b_rg
    g_idx = jnp.argmax(g_logits, axis=-1)
    g_prob = jnp.max(jax.nn.softmax(g_logits, axis=-1), axis=-1)
    e_logits = ((hf @ w_re).astype(jnp.float32) + b_re).reshape(-1, N_EGROUPS, EXPERTS_PER_GROUP)
    e_logits = jnp.einsum('tg,tge->te', jax.nn.one_hot(g_idx, N_EGROUPS, dtype=jnp.float32), e_logits)
    e_prob = jax.nn.softmax(e_logits, axis=-1)
    top_p, top_i = lax.top_k(e_prob, TOP_K)
    weight = g_prob[:, None] * top_p / jnp.sum(top_p, axis=-1, keepdims=True)
    expert_id = g_idx[:, None] * EXPERTS_PER_GROUP + top_i
    gates = jnp.einsum('tk,tke->te', weight, jax.nn.one_hot(expert_id, N_EXPERTS, dtype=jnp.float32))
    y = jnp.zeros(hf.shape, jnp.float32)
    for e in range(N_EXPERTS):
        a = jax.nn.silu(hf @ w_gate[e]) * (hf @ w_up[e])
        y = y + gates[:, e:e + 1] * (a @ w_down[e])
    return y.reshape(shp).astype(h.dtype)

def trunk(x, pos0, mem_k, mem_v, conv_prev, ssm_prev, ret_prev, norm_mix, w_in, conv_w, conv_b, dt_bias, a_log,
          d_skip, ssd_gain, ret_gain, w_out, norm_mem, w_mq, w_mo, norm_ffn, w_rg, b_rg, w_re, b_re, w_gate, w_up,
          w_down, norm_final):
    convs, ssms, rets = [], [], []
    for i in range(DEPTH):
        m, c_new, s_new, r_new = parallel_mixer(rmsnorm(x, norm_mix[i]), conv_prev[i], ssm_prev[i], ret_prev[i],
                                                pos0, w_in[i], conv_w[i], conv_b[i], dt_bias[i], a_log[i],
                                                d_skip[i], ssd_gain[i], ret_gain[i], w_out[i])
        x = x + m
        x = x + cross_attend(rmsnorm(x, norm_mem[i]), mem_k[i], mem_v[i], w_mq[i], w_mo[i])
        x = x + hier_moe(rmsnorm(x, norm_ffn[i]), w_rg[i], b_rg[i], w_re[i], b_re[i], w_gate[i], w_up[i], w_down[i])
        convs.append(c_new)
        ssms.append(s_new)
        rets.append(r_new)
    return rmsnorm(x, norm_final), jnp.stack(ssms), jnp.stack(convs), jnp.stack(rets)

def setup_inputs(seed: int = 0) -> dict:
    key = jax.random.key(seed)
    k = jax.random.split(key, 32)
    f32 = jnp.float32

    def nrm(kk, shape, scale):
        return scale * jax.random.normal(kk, shape, f32)

    def gain(kk, shape):
        return 1.0 + 0.01 * jax.random.normal(kk, shape, f32)

    dt0 = jnp.exp(jax.random.uniform(k[12], (DEPTH, SSD_HEADS), f32, math.log(1e-3), math.log(1e-1)))
    return {
        'x_prompt': nrm(k[0], (BATCH, SEQ, D_MODEL), 1.0),
        'x_sample': nrm(k[1], (DEC_BATCH, DEC_SEQ, D_MODEL), 1.0),
        'mem_prompt': nrm(k[2], (BATCH, N_MEM, D_MODEL), 1.0),
        'state_ssm': nrm(k[3], (DEPTH, DEC_BATCH, SSD_HEADS, SSD_HEAD_DIM, SSD_STATE), 0.1),
        'state_conv': nrm(k[4], (DEPTH, DEC_BATCH, CONV_WIDTH - 1, CONV_DIM), 1.0),
        'state_ret': nrm(k[5], (DEPTH, DEC_BATCH, RET_HEADS, RET_QK_DIM, RET_V_DIM), 1.0),
        'cache_mem_k': nrm(k[6], (DEPTH, DEC_BATCH, N_MEM, XA_HEADS, XA_HEAD_DIM), 1.0),
        'cache_mem_v': nrm(k[7], (DEPTH, DEC_BATCH, N_MEM, XA_HEADS, XA_HEAD_DIM), 1.0),
        'norm_mix': gain(k[8], (DEPTH, D_MODEL)),
        'w_in': nrm(k[9], (DEPTH, D_MODEL, IN_DIM), D_MODEL ** -0.5),
        'conv_w': nrm(k[10], (DEPTH, CONV_WIDTH, CONV_DIM), CONV_WIDTH ** -0.5),
        'conv_b': nrm(k[11], (DEPTH, CONV_DIM), 0.01),
        'dt_bias': dt0 + jnp.log(-jnp.expm1(-dt0)),
        'a_log': jnp.log(jax.random.uniform(k[13], (DEPTH, SSD_HEADS), f32, 1.0, 16.0)),
        'd_skip': gain(k[14], (DEPTH, SSD_HEADS)),
        'ssd_gain': gain(k[15], (DEPTH, SSD_WIDTH)),
        'ret_gain': gain(k[16], (DEPTH, RET_WIDTH)),
        'w_out': nrm(k[17], (DEPTH, MIX_WIDTH, D_MODEL), MIX_WIDTH ** -0.5),
        'norm_mem': gain(k[18], (DEPTH, D_MODEL)),
        'w_mq': nrm(k[19], (DEPTH, D_MODEL, D_MODEL), D_MODEL ** -0.5),
        'w_mk': nrm(k[20], (DEPTH, D_MODEL, D_MODEL), D_MODEL ** -0.5),
        'w_mv': nrm(k[21], (DEPTH, D_MODEL, D_MODEL), D_MODEL ** -0.5),
        'w_mo': nrm(k[22], (DEPTH, D_MODEL, D_MODEL), D_MODEL ** -0.5),
        'norm_ffn': gain(k[23], (DEPTH, D_MODEL)),
        'w_rg': nrm(k[24], (DEPTH, D_MODEL, N_EGROUPS), D_MODEL ** -0.5),
        'b_rg': nrm(k[25], (DEPTH, N_EGROUPS), 0.01),
        'w_re': nrm(k[26], (DEPTH, D_MODEL, N_EXPERTS), D_MODEL ** -0.5),
        'b_re': nrm(k[27], (DEPTH, N_EXPERTS), 0.01),
        'w_gate': nrm(k[28], (DEPTH, N_EXPERTS, D_MODEL, EXPERT_FF), D_MODEL ** -0.5),
        'w_up': nrm(k[29], (DEPTH, N_EXPERTS, D_MODEL, EXPERT_FF), D_MODEL ** -0.5),
        'w_down': nrm(k[30], (DEPTH, N_EXPERTS, EXPERT_FF, D_MODEL), EXPERT_FF ** -0.5),
        'norm_final': gain(k[31], (D_MODEL,)),
    }

def reference(x_prompt, x_sample, mem_prompt, state_ssm, state_conv, state_ret, cache_mem_k, cache_mem_v,
              norm_mix, w_in, conv_w, conv_b, dt_bias, a_log, d_skip, ssd_gain, ret_gain, w_out,
              norm_mem, w_mq, w_mk, w_mv, w_mo, norm_ffn, w_rg, b_rg, w_re, b_re, w_gate, w_up, w_down,
              norm_final):
    weights = (norm_mix, w_in, conv_w, conv_b, dt_bias, a_log, d_skip, ssd_gain, ret_gain, w_out,
               norm_mem, w_mq, w_mo, norm_ffn, w_rg, b_rg, w_re, b_re, w_gate, w_up, w_down, norm_final)
    bp = x_prompt.shape[0]
    mem_k_prompt = jnp.stack([mem_proj(mem_prompt, w_mk[i]) for i in range(DEPTH)])
    mem_v_prompt = jnp.stack([mem_proj(mem_prompt, w_mv[i]) for i in range(DEPTH)])
    conv0 = jnp.zeros((DEPTH, bp, CONV_WIDTH - 1, CONV_DIM), x_prompt.dtype)
    ssm0 = jnp.zeros((DEPTH, bp, SSD_HEADS, SSD_HEAD_DIM, SSD_STATE), jnp.float32)
    ret0 = jnp.zeros((DEPTH, bp, RET_HEADS, RET_QK_DIM, RET_V_DIM), jnp.float32)
    y_prompt, ssm_prompt, conv_prompt, ret_prompt = trunk(x_prompt, 0, mem_k_prompt, mem_v_prompt,
                                                          conv0, ssm0, ret0, *weights)
    y_sample, ssm_sample, conv_sample, ret_sample = trunk(x_sample, PAST_LEN, cache_mem_k, cache_mem_v,
                                                          state_conv, state_ssm, state_ret, *weights)
    return (y_prompt, y_sample, ssm_prompt, conv_prompt, ret_prompt, mem_k_prompt, mem_v_prompt,
            ssm_sample, conv_sample, ret_sample)


_drawn_inputs = setup_inputs


def setup_inputs(seed=0):
    import zlib

    import numpy as np

    out = dict(_drawn_inputs(seed))
    spreads = {}
    factors = {'d_skip': 16.261,
     'ssd_gain': 7.585,
     'ret_gain': 10.089,
     'norm_mem': 11.372,
     'b_rg': 12.684,
     'norm_final': 33.337,
     'conv_b': 2.822,
     'norm_ffn': 6.303,
     'b_re': 8.0}
    for name, (base, spread) in spreads.items():
        noise = np.random.default_rng([zlib.crc32(name.encode()), seed]).standard_normal(out[name].shape)
        drawn = base * np.exp(spread * noise) if base else spread * noise
        out[name] = __import__('jax').numpy.asarray(drawn.astype(out[name].dtype))
    for name, factor in factors.items():
        out[name] = (out[name] * factor).astype(out[name].dtype)
    return out
```

```python
from contextlib import ExitStack

import numpy as np

import concourse.bass as bass
from concourse import mybir

F32 = mybir.dt.float32
ACT = mybir.ActivationFunctionType
ALU = mybir.AluOpType
AX = mybir.AxisListType

P = 128
DEPTH = 2
D = 1024
KD = D // P
SEQ = 256
DB, DS = 8, 8
NS = DB * DS
T = SEQ + NS
PAST = 2048
H, HD, G, N = 16, 64, 2, 128
CW = 4
CC = 12
RH, DK, DV = 4, 128, 256
M = 256
XH = 4
EG, EPG = 4, 4
E = 16
FC = 4
EPS = 1e-6
ROPE_BASE = 10000.0
BANK = 512

TOK0 = [0, 128, 256]
TOKN = [128, 128, 64]

SLAB = KD * P
QUAD = 4 * SLAB
RING = 4
Q_V, Q_K, Q_Q, Q_XBC, Q_DT, Q_Z, Q_G = 0, 2, 3, 4, 7, 8, 10
Q_STATE = 12
Q_OUT = 16
Q_MK, Q_MV, Q_MQ = 20, 22, 24
Q_KC, Q_VC = 26, 30
Q_MO = 34
Q_MOE = 36
QUADS = Q_MOE + 3 * E
REVS = QUADS // RING
assert QUADS % RING == 0 and Q_MOE % RING == 0

XW = CW - 1 + SEQ + DB * (CW - 1 + DS)
XS0 = CW - 1 + SEQ
XOUT = XW - (CW - 1)


def layout_of(sizes):
    at, n = {}, 0
    for name, size in sizes:
        at[name] = n
        n += size
    return at, n


CONSTS = [("ident", P), ("ones", P), ("rot", P), ("cos", T), ("sin", T), ("causal", P), ("causal_s", NS),
          ("decay", RH * P), ("decay_s", RH * NS), ("qdecay", RH * P), ("qdecay_s", RH * NS),
          ("kend", RH), ("kend_s", RH), ("own", DB), ("restart", T), ("rank", EPG), ("eps", 1)]
CAT, CN = layout_of(CONSTS)
PARAMS = [("norm_mix", KD), ("norm_mem", KD), ("norm_ffn", KD), ("norm_final", KD), ("ssd_gain", KD),
          ("ret_gain", KD), ("d_skip", KD), ("conv_b", CC), ("conv_w", CC * CW), ("dt_bias", 1), ("a_log", 1),
          ("route_b", EG + E), ("route_w", KD * (EG + E))]
PAT, PN = layout_of(PARAMS)


def gammas():
    return 1.0 - 2.0 ** (-5.0 - np.arange(RH))


def constants():
    c = np.zeros((P, CN), np.float64)

    def put(name, a):
        c[:a.shape[0], CAT[name]:CAT[name] + a.shape[1]] = a

    put("ident", np.eye(P))
    put("ones", np.ones((P, P)))
    half = DK // 2
    rot = np.zeros((P, P))
    for m in range(half):
        rot[m + half, m] = -1.0
        rot[m, m + half] = 1.0
    put("rot", rot)
    pos = np.concatenate([np.arange(SEQ), np.tile(PAST + np.arange(DS), DB)]).astype(np.float32)
    inv = (np.float32(ROPE_BASE) ** (-np.arange(half, dtype=np.float32) / np.float32(half))).astype(np.float32)
    ang = (pos[None, :] * inv[:, None]).astype(np.float32).astype(np.float64)
    put("cos", np.tile(np.cos(ang), (2, 1)))
    put("sin", np.tile(np.sin(ang), (2, 1)))
    s, l = np.arange(P)[:, None], np.arange(P)[None, :]
    put("causal", (l >= s) * 1.0)
    ss, ls = np.arange(NS)[:, None], np.arange(NS)[None, :]
    same = (ss // DS == ls // DS) & (ls >= ss)
    put("causal_s", same * 1.0)
    scale = DK ** -0.5
    lg = np.log(gammas())
    put("decay", np.concatenate([np.where(l >= s, np.exp((l - s) * g), 0.0) * scale for g in lg], 1))
    put("decay_s", np.concatenate([np.where(same, np.exp((ls - ss) * g), 0.0) * scale for g in lg], 1))
    put("qdecay", np.tile(np.concatenate([np.exp((np.arange(P) + 1) * g) for g in lg])[None], (P, 1)))
    put("qdecay_s", np.tile(np.concatenate([np.exp((np.arange(NS) % DS + 1) * g) for g in lg])[None], (P, 1)))
    put("kend", np.stack([np.exp((P - 1 - np.arange(P)) * g) for g in lg], 1) * scale)
    put("kend_s", np.stack([np.exp((DS - 1 - np.arange(NS) % DS) * g) for g in lg], 1) * scale)
    put("own", (np.arange(NS)[:, None] // DS == np.arange(DB)[None]) * 1.0)
    start = np.ones(T)
    start[[0, P] + [SEQ + b * DS for b in range(DB)]] = 0.0
    put("restart", np.tile(start[None], (H, 1)))
    put("rank", np.tile(np.arange(EPG, 0, -1.0)[None], (P, 1)))
    put("eps", np.full((P, 1), EPS))
    return c.astype(np.float32)


def build(nc, stream, params, consts, x_in, mem_in, y_out, st_out, conv_out, mk_out, mv_out):
    with ExitStack() as ctx:
        def sb(name, *shape):
            return ctx.enter_context(nc.sbuf_tensor(name, [P, *shape], F32))

        def sem(name):
            return ctx.enter_context(nc.semaphore(name))

        ring = sb("ring", RING, QUAD)
        cst = sb("cst", CN)
        par = sb("par", DEPTH, PN)
        x = sb("x", KD, T)
        h = sb("h", KD, T)
        work_n = 21572
        work = sb("work", work_n)
        states_out = sb("states_out", 2, 2048)
        rstd = sb("rstd", T)
        dt_row = sb("dt_row", T)
        acum_row = sb("acum_row", T)
        dt_tok = sb("dt_tok", 3, H)
        acum_tok = sb("acum_tok", 3, H)
        cbm = sb("cbm", G, P)
        last = sb("last", H)
        last_s = sb("last_s", H, DB)
        last_own = sb("last_own", H, DB)
        decay_end = sb("decay_end", H)
        keep = sb("keep", H)
        conv_tail = sb("conv_tail", CC, (CW - 1) * (1 + DB))
        psum = ctx.enter_context(nc.psum_tensor("psum", [P, 8, BANK], F32))

        def view(tensor, at, *shape):
            n = int(np.prod(shape))
            v = tensor[:, at:at + n]
            if len(shape) == 1:
                return v
            names = "abcd"[:len(shape)]
            return v.rearrange(f"p ({' '.join(names)}) -> p {' '.join(names)}",
                               **{k: s for k, s in zip(names, shape)})

        zv = view(work, 0, KD, T)
        raw = view(work, 2560, CC, XW)
        gate = view(work, 2560, KD, T)
        decays = view(work, 5120, 3, BANK)
        xbc = view(work, 6724, CC, T)
        kq = view(work, 10564, 2 * RH, T)
        v_tok = view(work, 13124, 3, D)
        x_tok = view(work, 16196, 3, D)
        conv_acc = view(work, 16196, 2, XOUT)
        dt_tmp = view(work, 16196 + 2 * XOUT, 6, T)
        b_tok = view(work, 19268, 3, G * N)
        k_tok = view(work, 20036, 3, RH * DK)
        rot_tmp = view(work, 20036, 2, T)
        rstd6 = view(work, 13124, 6, T)
        hflat = h[:].rearrange("p a b -> p (a b)")
        c_dec_s = hflat[:, 0:1024].rearrange("p (h t) -> p h t", h=H)
        q_dec_s = hflat[:, 1024:1280].rearrange("p (h t) -> p h t", h=RH)
        k_own = hflat[:, 1280:1792]
        b_own = hflat[:, 1792:2048]
        rows = hflat[:, 2048:2560]
        mem = view(work, 0, KD, M)
        k_mem = view(work, 2048, KD, M)
        vt_mem = view(work, 4096, KD, M)
        v_mem = view(work, 6144, 2, D)
        q_p = view(work, 8192, KD, SEQ)
        q_own = view(work, 10240, KD, DB, NS)
        prob = view(work, 14336, 3, XH, M)
        prob_t = view(work, 17408, XH, 2, T)
        xmax = view(work, 19968, 3, XH)
        xsum = view(work, 19980, 3, XH)
        gates_all = view(work, 0, E, T)
        silu_gate = view(work, 5120, 2, T)
        hidden = view(work, 5760, FC, T)
        gate_row = view(work, 7040, T)
        one_row = view(work, 7360, 2, T)
        logits = view(work, 8000, 3, EG + E)
        R0 = 8100
        gmax = view(work, R0, 3)
        gsel = view(work, R0 + 10, 3, EG)
        gtmp = view(work, R0 + 30, 3, EG)
        gden = view(work, R0 + 50, 3)
        epick = view(work, R0 + 60, 3, EG, EPG)
        el = view(work, R0 + 120, 3, EPG)
        e1 = view(work, R0 + 140, 3, EPG)
        e2 = view(work, R0 + 160, 3, EPG)
        m1 = view(work, R0 + 180, 3)
        m2 = view(work, R0 + 190, 3)
        mt = view(work, R0 + 200, 3)
        w1 = view(work, R0 + 210, 3)
        w2 = view(work, R0 + 220, 3)
        gates_tok = view(work, R0 + 240, 3, EG, EPG)

        def k_(name, n, rows_=P, at=0):
            return cst[0:rows_, CAT[name] + at:CAT[name] + at + n]

        ident, ones = k_("ident", P), k_("ones", P)

        s_const = sem("s_const")
        loaded = [sem(f"s_loaded{s}") for s in range(RING)]
        freed = [sem(f"s_freed{s}") for s in range(RING)]
        s_sq = sem("s_sq")
        s_sum = sem("s_sum")
        s_rstd = sem("s_rstd")
        s_h = sem("s_h")
        s_proj = sem("s_proj")
        s_evac = sem("s_evac")
        s_rot = sem("s_rot")
        s_rotated = sem("s_rotated")
        s_dtv = sem("s_dtv")
        s_dta = sem("s_dta")
        s_conv = sem("s_conv")
        s_raw_free = sem("s_raw_free")
        s_silu = sem("s_silu")
        s_t = sem("s_t")
        s_tout = sem("s_tout")
        s_cb = sem("s_cb")
        s_rows = sem("s_rows")
        s_bc = sem("s_bc")
        s_diff = sem("s_diff")
        s_exp = sem("s_exp")
        s_lm = sem("s_lm")
        s_y = sem("s_y")
        s_yout = sem("s_yout")
        s_dec = sem("s_dec")
        s_dece = sem("s_dece")
        s_xdec = sem("s_xdec")
        s_cs = sem("s_cs")
        s_csout = sem("s_csout")
        s_score = sem("s_score")
        s_decayed = sem("s_decayed")
        s_o = sem("s_o")
        s_oout = sem("s_oout")
        s_kv = sem("s_kv")
        s_kvout = sem("s_kvout")
        s_own = sem("s_own")
        s_batch = sem("s_batch")
        s_newst = sem("s_newst")
        s_store = [sem(f"s_store{i}") for i in range(2)]
        s_gated = sem("s_gated")
        s_sq6 = sem("s_sq6")
        s_sum6 = sem("s_sum6")
        s_rstd6 = sem("s_rstd6")
        s_mix = sem("s_mix")
        s_wout = sem("s_wout")
        s_xadd = sem("s_xadd")
        s_mem = sem("s_mem")
        s_mkv = sem("s_mkv")
        s_mkvout = sem("s_mkvout")
        s_vt = sem("s_vt")
        s_vtout = sem("s_vtout")
        s_mkstore = sem("s_mkstore")
        s_mvstore = sem("s_mvstore")
        s_qzero = sem("s_qzero")
        s_q = sem("s_q")
        s_qout = sem("s_qout")
        s_xs = sem("s_xs")
        s_xmax = sem("s_xmax")
        s_xexp = sem("s_xexp")
        s_prob = sem("s_prob")
        s_pt = sem("s_pt")
        s_ptout = sem("s_ptout")
        s_xo = sem("s_xo")
        s_xoout = sem("s_xoout")
        s_route = sem("s_route")
        s_rv = sem("s_rv")
        s_ra = sem("s_ra")
        s_gt = sem("s_gt")
        s_grow = sem("s_grow")
        s_orow = sem("s_orow")
        s_gb = sem("s_gb")
        s_gbout = sem("s_gbout")
        s_gate = sem("s_gate")
        s_up = sem("s_up")
        s_sg = sem("s_sg")
        s_hid = sem("s_hid")
        s_down = sem("s_down")
        s_added = sem("s_added")
        s_tstore = sem("s_tstore")
        s_ystore = sem("s_ystore")

        block = ctx.enter_context(nc.Block())
        NNORM = 3
        gam = gammas()

        def quad(eng, L, q):
            eng.wait_ge(loaded[q % RING], 16 * (L * REVS + q // RING + 1))
            return ring[:, q % RING, :]

        def tok(t):
            return slice(TOK0[t], TOK0[t] + TOKN[t])

        def heads_of(t):
            hb = BANK // TOKN[t]
            return hb, H // hb

        @block.sync
        def _(sp):
            sp.dma_start(x[:], x_in).then_inc(s_const, 16)
            sp.dma_start(cst[:], consts).then_inc(s_const, 16)
            sp.dma_start(par[:], params.rearrange("l p n -> p l n")).then_inc(s_const, 16)
            for n in range(DEPTH * REVS):
                for s in range(RING):
                    if n >= 1:
                        sp.wait_ge(freed[s], n)
                    sp.dma_start(ring[:, s, :], stream[n * RING + s]).then_inc(loaded[s], 16)

        @block.tensor
        def _(pe):
            def sums(L, k):
                pe.wait_ge(s_sq, L * NNORM + k + 1)
                for j in range(KD):
                    mm = pe.matmul(psum[:, 7, 0:T], ones, h[:, j, :], start=(j == 0), stop=(j == KD - 1))
                mm.then_inc(s_sum, 1)

            def transposes(outs_ins):
                for o, i in outs_ins:
                    mm = pe.transpose(o, i, ident[0:i.shape[0], 0:i.shape[0]])
                return mm

            def mixer(L):
                sums(L, 0)
                pe.wait_ge(s_h, L * NNORM + 1)
                n_proj = 0

                def project(q0, chunks):
                    nonlocal n_proj
                    for c in range(chunks):
                        w = quad(pe, L, q0 + c // 4)
                        if n_proj >= 4:
                            pe.wait_ge(s_evac, L * 45 + n_proj - 3)
                        for j in range(KD):
                            a = (c % 4) * SLAB + j * P
                            mm = pe.matmul(psum[:, n_proj % 4, 0:T], w[:, a:a + P], h[:, j, :],
                                           start=(j == 0), stop=(j == KD - 1))
                        mm.then_inc(s_proj, 1)
                        n_proj += 1
                        if c % 4 == 3:
                            pe.drain().then_inc(freed[(q0 + c // 4) % RING], 1)

                project(Q_V, 8)
                project(Q_K, 4)
                project(Q_Q, 4)
                project(Q_XBC, 12)
                w = quad(pe, L, Q_DT)
                pe.wait_ge(s_evac, L * 45 + n_proj - 3)
                for j in range(KD):
                    mm = pe.matmul(psum[0:H, n_proj % 4, 0:T], w[:, j * H:(j + 1) * H], h[:, j, :],
                                   start=(j == 0), stop=(j == KD - 1))
                mm.then_inc(s_proj, 1)
                n_proj += 1
                for j in range(2 * RH):
                    pe.wait_ge(s_evac, L * 45 + 8 + j + 1)
                    if j >= 2:
                        pe.wait_ge(s_rotated, L * 8 + j - 1)
                    pe.matmul(psum[:, 4 + j % 2, 0:T], k_("rot", P), kq[:, j, :], start=True, stop=True)\
                        .then_inc(s_rot, 1)
                nt = 0

                def turn(group, n):
                    nonlocal nt
                    if nt >= 2:
                        pe.wait_ge(s_tout, L * 19 + nt - 1)
                    b = 6 + nt % 2
                    transposes([(psum[0:n, b, i * P:(i + 1) * P], src) for i, src in enumerate(group)])\
                        .then_inc(s_t, 1)
                    nt += 1

                for t in range(3):
                    for half in range(2):
                        turn([zv[:, 4 * half + i, tok(t)] for i in range(4)], TOKN[t])
                project(Q_Z, 8)
                pe.wait_ge(s_silu, (L + 1) * CC)
                for t in range(3):
                    for half in range(2):
                        turn([xbc[:, 4 * half + i, tok(t)] for i in range(4)], TOKN[t])
                for t in range(3):
                    turn([xbc[:, 8 + i, tok(t)] for i in range(2)], TOKN[t])
                pe.wait_ge(s_rotated, (L + 1) * 8)
                for t in range(3):
                    turn([kq[:, i, tok(t)] for i in range(4)], TOKN[t])
                pe.wait_ge(s_dtv, (L + 1) * 4)
                pe.wait_ge(s_tout, L * 19 + nt - 1)
                b = 6 + nt % 2
                for t in range(3):
                    for i, src in enumerate((dt_row, acum_row)):
                        mm = pe.transpose(psum[0:TOKN[t], b, (3 * i + t) * H:(3 * i + t + 1) * H],
                                          src[0:H, tok(t)], ident[0:H, 0:H])
                mm.then_inc(s_t, 1)
                nt += 1
                project(Q_G, 8)
                pe.wait_ge(s_evac, (L + 1) * 45)
                pe.wait_ge(s_tout, (L + 1) * 19)

                nb = 0
                for t in range(3):
                    n = TOKN[t]
                    hb, banks = heads_of(t)
                    for g in range(G):
                        mm = pe.matmul(psum[0:n, 4, g * P:g * P + n], xbc[:, 8 + g, tok(t)], xbc[:, 10 + g, tok(t)],
                                       start=True, stop=True)
                    mm.then_inc(s_cb, 1)
                    for i in range(banks):
                        pe.wait_ge(s_rows, L * 10 + nb + 1)
                        pe.matmul(psum[:, 5, 0:BANK], ones[0:H, :], rows[0:H, :], start=True, stop=True)\
                            .then_inc(s_bc, 1)
                        pe.wait_ge(s_lm, L * 10 + nb + 1)
                        nb += 1
                        for hh in range(hb):
                            hd = i * hb + hh
                            c = hd // 2 if t == 2 else (hd // 2) % 2
                            o = psum[(hd % 2) * HD:(hd % 2) * HD + HD, 6, c * n:c * n + n]
                            first = hd < 2 if t == 2 else True
                            mm = pe.matmul(o, x_tok[0:n, t, hd * HD:(hd + 1) * HD],
                                           decays[0:n, 0, hh * n:(hh + 1) * n],
                                           start=first, stop=(t == 0), skip_group_check=True)
                            if t == 1:
                                mm = pe.matmul(o, states_out[:, 0, hd * HD:(hd + 1) * HD],
                                               decays[:, 1, hh * n:(hh + 1) * n],
                                               start=False, stop=True, skip_group_check=True)
                        mm.then_inc(s_y, 1)
                        if t < 2:
                            pe.wait_ge(s_yout, L * 8 + t * 4 + i + 1)
                    pe.wait_ge(s_xdec, L * 3 + t + 1)
                    if t < 2:
                        for g in range(G):
                            mm = pe.matmul(psum[:, g, 0:BANK], b_tok[0:n, t, g * N:(g + 1) * N],
                                           x_tok[0:n, t, g * BANK:(g + 1) * BANK], start=True, stop=True)
                        mm.then_inc(s_cs, 1)
                        pe.wait_ge(s_csout, L * 2 + t + 1)

                for t in range(3):
                    n = TOKN[t]
                    if t > 0:
                        pe.wait_ge(s_oout, L * 2 + t)
                    for r in range(RH):
                        mm = pe.matmul(psum[0:n, 4, r * n:(r + 1) * n], kq[:, r, tok(t)], kq[:, RH + r, tok(t)],
                                       start=True, stop=True)
                    mm.then_inc(s_score, 1)
                    pe.wait_ge(s_decayed, L * 3 + t + 1)
                    if t < 2:
                        for r in range(RH):
                            for e in range(2):
                                o = psum[:, 2 + r // 2, (r % 2) * 2 * P + e * P:(r % 2) * 2 * P + (e + 1) * P]
                                mm = pe.matmul(o, v_tok[:, t, r * DV + e * P:r * DV + (e + 1) * P],
                                               decays[:, 0, r * P:(r + 1) * P], start=True, stop=(t == 0),
                                               skip_group_check=True)
                                if t == 1:
                                    mm = pe.matmul(o, states_out[:, 0, 1024 + r * DV + e * P:1024 + r * DV + (e + 1) * P],
                                                   decays[:, 1, r * P:(r + 1) * P], start=False, stop=True,
                                                   skip_group_check=True)
                        mm.then_inc(s_o, 1)
                        for r in range(RH):
                            mm = pe.matmul(psum[:, r // 2, (r % 2) * DV:(r % 2 + 1) * DV],
                                           k_tok[:, t, r * DK:(r + 1) * DK], v_tok[:, t, r * DV:(r + 1) * DV],
                                           start=True, stop=True)
                        mm.then_inc(s_kv, 1)
                        pe.wait_ge(s_kvout, L * 2 + t + 1)
                    else:
                        for r in range(RH):
                            for e in range(2):
                                c = 2 * r + e
                                pe.matmul(psum[:, 7, c * NS:(c + 1) * NS],
                                          v_tok[0:n, t, r * DV + e * P:r * DV + (e + 1) * P],
                                          decays[0:n, 0, r * n:(r + 1) * n], start=(c == 0), stop=False,
                                          skip_group_check=True)
                for b in range(DB):
                    w = quad(pe, L, Q_STATE + b // 2)
                    ws = w[:, (b % 2) * 2048:(b % 2 + 1) * 2048]
                    for hd in range(H):
                        c = hd // 2
                        pe.matmul(psum[(hd % 2) * HD:(hd % 2) * HD + HD, 6, c * NS + b * DS:c * NS + (b + 1) * DS],
                                  ws[:, hd * HD:(hd + 1) * HD], c_dec_s[:, hd, b * DS:(b + 1) * DS],
                                  start=False, stop=(b == DB - 1), skip_group_check=True)
                    for r in range(RH):
                        for e in range(2):
                            c = 2 * r + e
                            mm = pe.matmul(psum[:, 7, c * NS + b * DS:c * NS + (b + 1) * DS],
                                           ws[:, 1024 + r * DV + e * P:1024 + r * DV + (e + 1) * P],
                                           q_dec_s[:, r, b * DS:(b + 1) * DS],
                                           start=False, stop=(b == DB - 1), skip_group_check=True)
                    pe.wait_ge(s_own, L * DB + b + 1)
                    if b > 0:
                        pe.wait_ge(s_newst, L * DB + b)
                    for g in range(G):
                        pe.matmul(psum[:, g, 0:BANK], b_own[0:NS, g * N:(g + 1) * N],
                                  x_tok[0:NS, 2, g * BANK:(g + 1) * BANK], start=True, stop=True)
                    for r in range(RH):
                        mm = pe.matmul(psum[:, 2 + r // 2, (r % 2) * DV:(r % 2 + 1) * DV],
                                       k_own[0:NS, r * DK:(r + 1) * DK], v_tok[0:NS, 2, r * DV:(r + 1) * DV],
                                       start=True, stop=True)
                    mm.then_inc(s_batch, 1)

                pe.wait_ge(s_sq6, L * 2 + 1)
                for j in range(KD):
                    mm = pe.matmul(psum[:, j // 4, 0:T], ones, h[:, j, :], start=(j % 4 == 0), stop=(j % 4 == 3))
                mm.then_inc(s_sum6, 1)
                pe.wait_ge(s_sq6, L * 2 + 2)
                for j in range(KD):
                    mm = pe.matmul(psum[:, 2 + j // 2, 0:T], ones, h[:, j, :], start=(j % 2 == 0), stop=(j % 2 == 1))
                mm.then_inc(s_sum6, 1)
                pe.wait_ge(s_mix, L + 1)
                for j in range(KD):
                    w = quad(pe, L, Q_OUT + j // 2)
                    if j >= 4:
                        pe.wait_ge(s_xadd, L * 16 + j - 3)
                    for i in range(2 * KD):
                        a = (j % 2) * 2 * SLAB + i * P
                        src = xbc[:, i, :] if i < KD else kq[:, i - KD, :]
                        mm = pe.matmul(psum[:, j % 4, 0:T], w[:, a:a + P], src, start=(i == 0), stop=(i == 15))
                    mm.then_inc(s_wout, 1)
                    if j % 2 == 1:
                        pe.drain().then_inc(freed[(Q_OUT + j // 2) % RING], 1)

            def attention(L):
                pe.wait_ge(s_mem, 16 * (L + 1))
                for c in range(16):
                    w = quad(pe, L, Q_MK + c // 4)
                    if c >= 2:
                        pe.wait_ge(s_mkvout, L * 16 + c - 1)
                    for j in range(KD):
                        a = (c % 4) * SLAB + j * P
                        mm = pe.matmul(psum[:, 4 + c % 2, 0:M], w[:, a:a + P], mem[:, j, :],
                                       start=(j == 0), stop=(j == KD - 1))
                    mm.then_inc(s_mkv, 1)
                    if c % 4 == 3:
                        pe.drain().then_inc(freed[(Q_MK + c // 4) % RING], 1)
                pe.wait_ge(s_mkvout, (L + 1) * 16)
                for mc in range(2):
                    for half in range(2):
                        transposes([(psum[:, 4 + half, i * P:(i + 1) * P], vt_mem[:, 4 * half + i, mc * P:(mc + 1) * P])
                                    for i in range(4)]).then_inc(s_vt, 1)
                    pe.wait_ge(s_vtout, L * 4 + 2 * mc + 2)
                sums(L, 1)
                pe.wait_ge(s_h, L * NNORM + 2)
                for c in range(KD):
                    w = quad(pe, L, Q_MQ + c // 4)
                    if c >= 4:
                        pe.wait_ge(s_qout, L * KD + c - 3)
                    for j in range(KD):
                        a = (c % 4) * SLAB + j * P
                        mm = pe.matmul(psum[:, c % 4, 0:T], w[:, a:a + P], h[:, j, :],
                                       start=(j == 0), stop=(j == KD - 1))
                    mm.then_inc(s_q, 1)
                    if c % 4 == 3:
                        pe.drain().then_inc(freed[(Q_MQ + c // 4) % RING], 1)
                pe.wait_ge(s_qout, (L + 1) * KD)
                for t in range(2):
                    for r in range(XH):
                        for c in range(2):
                            mm = pe.matmul(psum[:, 2 * t + r // 2, (r % 2) * M:(r % 2 + 1) * M],
                                           q_p[:, 2 * r + c, tok(t)], k_mem[:, 2 * r + c, :],
                                           start=(c == 0), stop=(c == 1))
                    mm.then_inc(s_xs, 1)
                for b in range(DB):
                    w = quad(pe, L, Q_KC + b // 2)
                    for r in range(XH):
                        for c in range(2):
                            a = (b % 2) * 2048 + (2 * r + c) * M
                            mm = pe.matmul(psum[0:NS, 4 + r // 2, (r % 2) * M:(r % 2 + 1) * M],
                                           q_own[:, 2 * r + c, b, :], w[:, a:a + M],
                                           start=(b == 0 and c == 0 and r % 2 == 0), stop=(b == DB - 1),
                                           skip_group_check=True)
                    if b == DB - 1:
                        mm.then_inc(s_xs, 1)
                    if b % 2 == 1:
                        pe.drain().then_inc(freed[(Q_KC + b // 2) % RING], 1)
                np_ = 0
                for t in range(3):
                    pe.wait_ge(s_prob, L * 3 + t + 1)
                    for half in range(2):
                        if np_ >= 2:
                            pe.wait_ge(s_ptout, L * 6 + np_ - 1)
                        n = TOKN[t]
                        for i in range(4):
                            r, c = 2 * half + i // 2, i % 2
                            mm = pe.transpose(psum[:, 6 + np_ % 2, i * P:i * P + n],
                                              prob[0:n, t, r, c * P:(c + 1) * P], ident[0:n, 0:n])
                        mm.then_inc(s_pt, 1)
                        np_ += 1
                pe.wait_ge(s_ptout, (L + 1) * 6)
                for j in range(KD):
                    if j >= 4:
                        pe.wait_ge(s_xoout, L * 9 + j - 3)
                    for c in range(2):
                        mm = pe.matmul(psum[:, j % 4, 0:SEQ], v_mem[:, c, j * P:(j + 1) * P],
                                       prob_t[:, j // 2, c, 0:SEQ], start=(c == 0), stop=(c == 1))
                    mm.then_inc(s_xo, 1)
                for b in range(DB):
                    w = quad(pe, L, Q_VC + b // 2)
                    for j in range(KD):
                        for c in range(2):
                            a = (b % 2) * 2048 + c * D + j * P
                            mm = pe.matmul(psum[:, 4, j * NS + b * DS:j * NS + (b + 1) * DS], w[:, a:a + P],
                                           prob_t[:, j // 2, c, SEQ + b * DS:SEQ + (b + 1) * DS],
                                           start=(c == 0), stop=(c == 1), skip_group_check=True)
                    if b == DB - 1:
                        mm.then_inc(s_xo, 1)
                    if b % 2 == 1:
                        pe.drain().then_inc(freed[(Q_VC + b // 2) % RING], 1)
                pe.wait_ge(s_xoout, (L + 1) * 9)
                for c in range(KD):
                    w = quad(pe, L, Q_MO + c // 4)
                    if c >= 4:
                        pe.wait_ge(s_xadd, L * 16 + KD + c - 3)
                    for j in range(KD):
                        a = (c % 4) * SLAB + j * P
                        mm = pe.matmul(psum[:, c % 4, 0:T], w[:, a:a + P], h[:, j, :],
                                       start=(j == 0), stop=(j == KD - 1))
                    mm.then_inc(s_wout, 1)
                    if c % 4 == 3:
                        pe.drain().then_inc(freed[(Q_MO + c // 4) % RING], 1)

            def moe(L):
                sums(L, 2)
                pe.wait_ge(s_h, L * NNORM + 3)
                for t in range(3):
                    for j in range(KD):
                        a = PAT["route_w"] + j * (EG + E)
                        mm = pe.matmul(psum[0:TOKN[t], 6, t * 32:t * 32 + EG + E], h[:, j, tok(t)],
                                       par[:, L, a:a + EG + E], start=(j == 0), stop=(j == KD - 1))
                mm.then_inc(s_route, 1)
                pe.wait_ge(s_rv, 2 * (L + 1))
                for t in range(3):
                    mm = pe.transpose(psum[0:E, 5, TOK0[t]:TOK0[t] + TOKN[t]],
                                      gates_tok[0:TOKN[t], t, :, :], ident[0:TOKN[t], 0:TOKN[t]])
                mm.then_inc(s_gt, 1)
                for e in range(E):
                    pe.wait_ge(s_orow, L * E + e + 1)
                    if e >= 2:
                        pe.wait_ge(s_gbout, L * E + e - 1)
                    pe.matmul(psum[:, 6 + e % 2, 0:T], ones[0:E, :], one_row[0:E, e % 2, :],
                              start=True, stop=True).then_inc(s_gb, 1)
                pe.wait_ge(s_gbout, (L + 1) * E)
                with pe.Fori(0, E // 4) as i4:
                    for u in range(4):
                        seen = L * E * 4 + i4 * 16 + u * 4
                        rev = L * REVS + Q_MOE // RING + i4 * 3
                        for q in range(2):
                            s, dr = (3 * u + q) % RING, (3 * u + q) // RING
                            pe.wait_ge(loaded[s], 16 * (rev + dr + 1))
                            w = ring[:, s, :]
                            for f in range(2 * q, 2 * q + 2):
                                if f >= 2:
                                    pe.wait_ge(s_sg, seen + f - 1)
                                for j in range(KD):
                                    a = (2 * (f % 2)) * SLAB + j * P
                                    mm = pe.matmul(psum[:, f % 2, 0:T], w[:, a:a + P], h[:, j, :],
                                                   start=(j == 0), stop=(j == KD - 1))
                                mm.then_inc(s_gate, 1)
                                if f >= 2:
                                    pe.wait_ge(s_hid, seen + f - 1)
                                for j in range(KD):
                                    a = (2 * (f % 2) + 1) * SLAB + j * P
                                    mm = pe.matmul(psum[:, 2 + f % 2, 0:T], w[:, a:a + P], h[:, j, :],
                                                   start=(j == 0), stop=(j == KD - 1))
                                mm.then_inc(s_up, 1)
                            pe.drain().then_inc(freed[s], 1)
                        s, dr = (3 * u + 2) % RING, (3 * u + 2) // RING
                        pe.wait_ge(loaded[s], 16 * (rev + dr + 1))
                        w = ring[:, s, :]
                        for f in range(FC):
                            pe.wait_ge(s_hid, seen + f + 1)
                            for j in range(4):
                                a = (j * FC + f) * P
                                mm = pe.matmul(psum[:, 4 + j, 0:T], w[:, a:a + P], hidden[:, f, :],
                                               start=(f == 0), stop=(f == FC - 1), skip_group_check=True)
                                if f == FC - 1:
                                    mm.then_inc(s_down, 1)
                        for j in range(4, KD):
                            pe.wait_ge(s_added, (seen * 2) + j - 3)
                            for f in range(FC):
                                a = (j * FC + f) * P
                                mm = pe.matmul(psum[:, j, 0:T], w[:, a:a + P], hidden[:, f, :],
                                               start=(f == 0), stop=(f == FC - 1))
                            mm.then_inc(s_down, 1)
                        pe.drain().then_inc(freed[s], 1)

            pe.wait_ge(s_const, 48)
            for L in range(DEPTH):
                mixer(L)
                attention(L)
                moe(L)
            sums(DEPTH, 0)

        @block.scalar
        def _(act):
            def square(L, k):
                if L or k:
                    if k == 0:
                        act.wait_ge(s_added, L * E * KD)
                    else:
                        act.wait_ge(s_xadd, L * 16 + 8 * k)
                act.activation(h[:], x[:], ACT.Square).then_inc(s_sq, 1)
                act.wait_ge(s_sum, L * NNORM + k + 1)
                act.activation(rstd[:], psum[:, 7, 0:T], ACT.Ln, scale=1.0 / D, bias=k_("eps", 1))
                act.drain()
                act.activation(rstd[:], rstd[:], ACT.Exp, scale=-0.5).then_inc(s_rstd, 1)

            def mixer(L):
                square(L, 0)
                n_evac = 0
                nt = 0

                def evac(dst, func=ACT.Copy, rows_=P):
                    nonlocal n_evac
                    act.wait_ge(s_proj, L * 45 + n_evac + 1)
                    act.activation(dst, psum[0:rows_, n_evac % 4, 0:T], func).then_inc(s_evac, 1)
                    n_evac += 1

                def turned(dst, n, width):
                    nonlocal nt
                    act.wait_ge(s_t, L * 19 + nt + 1)
                    act.activation(dst, psum[0:n, 6 + nt % 2, 0:width], ACT.Copy).then_inc(s_tout, 1)
                    nt += 1

                for c in range(8):
                    evac(zv[:, c, :])
                for c in range(8):
                    evac(kq[:, c, :])
                for c in range(CC):
                    act.wait_ge(s_proj, L * 45 + n_evac + 1)
                    b = n_evac % 4
                    act.activation(raw[:, c, CW - 1:XS0], psum[:, b, 0:SEQ], ACT.Copy)
                    act.activation(raw[:, c, XS0:XW].rearrange("p (b j) -> p b j", b=DB)[:, :, CW - 1:],
                                   psum[:, b, SEQ:T].rearrange("p (b j) -> p b j", b=DB), ACT.Copy)\
                        .then_inc(s_evac, 1)
                    n_evac += 1
                evac(dt_tmp[0:H, 0, :], rows_=H)
                act.wait_ge(s_dtv, L * 4 + 1)
                act.activation(dt_tmp[0:H, 2, :], dt_tmp[0:H, 1, :], ACT.Exp, scale=-1.0).then_inc(s_dta, 1)
                act.wait_ge(s_dtv, L * 4 + 2)
                act.activation(dt_tmp[0:H, 4, :], dt_tmp[0:H, 3, :], ACT.Ln)
                act.activation(keep[0:H, 0:1], par[0:H, L, PAT["a_log"]:PAT["a_log"] + 1], ACT.Exp)
                act.drain().then_inc(s_dta, 1)
                for t in range(3):
                    for half in range(2):
                        turned(v_tok[0:TOKN[t], t, half * BANK:(half + 1) * BANK], TOKN[t], BANK)
                for c in range(8):
                    evac(zv[:, c, :], ACT.Silu)
                    for cc in range(c * 3 // 2, (c + 1) * 3 // 2):
                        act.wait_ge(s_conv, L * CC + cc + 1)
                        a = conv_acc[:, cc % 2, :]
                        act.activation(xbc[:, cc, 0:SEQ], a[:, 0:SEQ], ACT.Silu)
                        act.activation(xbc[:, cc, SEQ:T - DS].rearrange("p (b j) -> p b j", b=DB - 1),
                                       a[:, XS0:XS0 + 77].rearrange("p (b j) -> p b j", b=DB - 1)[:, :, 0:DS],
                                       ACT.Silu)
                        act.activation(xbc[:, cc, T - DS:T], a[:, XS0 + 77:XOUT], ACT.Silu).then_inc(s_silu, 1)
                for t in range(3):
                    for half in range(2):
                        if t == 0 and half == 0:
                            act.wait_ge(s_silu, (L + 1) * CC)
                        turned(x_tok[0:TOKN[t], t, half * BANK:(half + 1) * BANK], TOKN[t], BANK)
                for t in range(3):
                    turned(b_tok[0:TOKN[t], t, :], TOKN[t], G * N)
                for t in range(3):
                    turned(k_tok[0:TOKN[t], t, :], TOKN[t], BANK)
                act.wait_ge(s_t, L * 19 + nt + 1)
                b = 6 + nt % 2
                for i, dst in enumerate((dt_tok, acum_tok)):
                    act.activation(dst[:, 0:2, :], psum[:, b, 3 * i * H:(3 * i + 2) * H]
                                   .rearrange("p (t h) -> p t h", t=2), ACT.Copy)
                    act.activation(dst[0:NS, 2, :], psum[0:NS, b, (3 * i + 2) * H:(3 * i + 3) * H], ACT.Copy)
                act.drain().then_inc(s_tout, 1)
                nt += 1
                act.wait_ge(s_raw_free, L + 1)
                for c in range(8):
                    evac(gate[:, c, :], ACT.Silu)

                nb = 0
                for t in range(3):
                    n = TOKN[t]
                    hb, banks = heads_of(t)
                    for i in range(banks):
                        act.wait_ge(s_diff, L * 10 + nb + 1)
                        if t == 1:
                            act.activation(decays[:, 1, :], psum[:, 5, :], ACT.Exp)
                        if t == 2:
                            act.activation(c_dec_s[:, i * hb:(i + 1) * hb, :],
                                           psum[:, 5, :].rearrange("p (h l) -> p h l", h=hb), ACT.Exp)
                        act.activation(decays[0:n, 0, :], decays[0:n, 0, :], ACT.Exp)
                        act.drain().then_inc(s_exp, 1)
                        nb += 1
                    act.wait_ge(s_dec, L * 3 + t + 1)
                    act.activation(decay_end[0:n, :], decay_end[0:n, :], ACT.Exp)
                    if t == 2:
                        act.activation(last_s[:], last_s[:], ACT.Exp)
                    else:
                        act.activation(keep[:], last[:], ACT.Exp)
                    act.drain().then_inc(s_dece, 1)
                    if t == 0:
                        act.wait_ge(s_cs, L * 2 + 1)
                        act.activation(states_out[:, 0, 0:1024].rearrange("p (a b) -> p a b", a=2),
                                       psum[:, 0:2, :], ACT.Copy).then_inc(s_csout, 1)
                for t in range(3):
                    if t < 2:
                        act.wait_ge(s_o, L * 2 + t + 1)
                        act.activation(kq[:, :, tok(t)].rearrange("p (a b) t -> p a b t", a=2),
                                       psum[:, 2:4, :].rearrange("p a (b t) -> p a b t", b=4), ACT.Copy)\
                            .then_inc(s_oout, 1)
                    if t == 0:
                        act.wait_ge(s_kv, L * 2 + 1)
                        act.activation(states_out[:, 0, 1024:2048].rearrange("p (a b) -> p a b", a=2),
                                       psum[:, 0:2, :], ACT.Copy).then_inc(s_kvout, 1)
                act.wait_ge(s_batch, (L + 1) * DB)
                act.activation(kq[:, :, tok(2)], psum[:, 7, :].rearrange("p (c t) -> p c t", c=KD), ACT.Copy)
                act.wait_ge(s_gated, L + 1)
                act.activation(h[:], xbc[:, 0:KD, :], ACT.Square).then_inc(s_sq6, 1)
                act.wait_ge(s_sum6, L * 2 + 1)
                act.drain()
                act.activation(h[:], kq[:], ACT.Square).then_inc(s_sq6, 1)
                act.activation(rstd6[:, 0:2, :], psum[:, 0:2, 0:T], ACT.Ln, scale=2.0 / D, bias=k_("eps", 1))
                act.wait_ge(s_sum6, L * 2 + 2)
                act.activation(rstd6[:, 2:6, :], psum[:, 2:6, 0:T], ACT.Ln, scale=1.0 / DV, bias=k_("eps", 1))
                act.drain()
                act.activation(rstd6[:], rstd6[:], ACT.Exp, scale=-0.5).then_inc(s_rstd6, 1)

            def attention(L):
                for c in range(16):
                    act.wait_ge(s_mkv, L * 16 + c + 1)
                    dst = k_mem[:, c, :] if c < KD else vt_mem[:, c - KD, :]
                    act.activation(dst, psum[:, 4 + c % 2, 0:M], ACT.Copy).then_inc(s_mkvout, 1)
                for mc in range(2):
                    for half in range(2):
                        act.wait_ge(s_vt, L * 4 + 2 * mc + half + 1)
                        act.activation(v_mem[:, mc, half * BANK:(half + 1) * BANK], psum[:, 4 + half, :], ACT.Copy)\
                            .then_inc(s_vtout, 1)
                square(L, 1)
                act.wait_ge(s_qzero, L + 1)
                for c in range(KD):
                    act.wait_ge(s_q, L * KD + c + 1)
                    act.activation(q_p[:, c, :], psum[:, c % 4, 0:SEQ], ACT.Copy)
                    own = q_own[:, c, :, :].rearrange("p b t -> p (b t)")
                    for b in range(DB):
                        ins = act.activation(own[:, b * (NS + DS):b * (NS + DS) + DS],
                                             psum[:, c % 4, SEQ + b * DS:SEQ + (b + 1) * DS], ACT.Copy)
                    ins.then_inc(s_qout, 1)
                for t in range(3):
                    n = TOKN[t]
                    act.wait_ge(s_xmax, L * 3 + t + 1)
                    for r in range(XH):
                        b = 2 * t + r // 2
                        act.activation(prob[0:n, t, r, :], psum[0:n, b, (r % 2) * M:(r % 2 + 1) * M], ACT.Exp,
                                       bias=xmax[0:n, t, r:r + 1], scale=1.0 / 16, accum_out=xsum[0:n, t, r:r + 1])
                    act.drain().then_inc(s_xexp, 1)
                np_ = 0
                for t in range(3):
                    n = TOKN[t]
                    for half in range(2):
                        act.wait_ge(s_pt, L * 6 + np_ + 1)
                        act.activation(prob_t[:, 2 * half:2 * half + 2, :, tok(t)],
                                       psum[:, 6 + np_ % 2, :].rearrange("p (r c t) -> p r c t", r=2, c=2)[:, :, :, 0:n],
                                       ACT.Copy).then_inc(s_ptout, 1)
                        np_ += 1
                for j in range(KD):
                    act.wait_ge(s_xo, L * 9 + j + 1)
                    act.activation(h[:, j, 0:SEQ], psum[:, j % 4, 0:SEQ], ACT.Copy).then_inc(s_xoout, 1)
                act.wait_ge(s_xo, (L + 1) * 9)
                act.activation(h[:, :, SEQ:T], psum[:, 4, :].rearrange("p (c t) -> p c t", c=KD), ACT.Copy)\
                    .then_inc(s_xoout, 1)

            def moe(L):
                square(L, 2)
                act.wait_ge(s_rv, 2 * L + 1)
                act.activation(gtmp, gtmp, ACT.Exp)
                act.activation(mt, mt, ACT.Exp)
                act.drain().then_inc(s_ra, 1)
                act.wait_ge(s_gt, L + 1)
                act.activation(gate_row[0:E, :], psum[0:E, 5, 0:T], ACT.Copy).then_inc(s_grow, 1)
                for e in range(E):
                    act.wait_ge(s_gb, L * E + e + 1)
                    act.activation(gates_all[:, e, :], psum[:, 6 + e % 2, 0:T], ACT.Copy).then_inc(s_gbout, 1)
                with act.Fori(0, E // 4) as i4:
                    for u in range(4):
                        seen = L * E * 4 + i4 * 16 + u * 4
                        for f in range(FC):
                            act.wait_ge(s_gate, seen + f + 1)
                            if f >= 2:
                                act.wait_ge(s_hid, seen + f - 1)
                            act.activation(silu_gate[:, f % 2, :], psum[:, f % 2, 0:T], ACT.Silu).then_inc(s_sg, 1)

            act.wait_ge(s_const, 48)
            for L in range(DEPTH):
                mixer(L)
                attention(L)
                moe(L)
            square(DEPTH, 0)

        @block.vector
        def _(dve):
            def normed(L, k, gain, dst=h):
                dve.wait_ge(s_rstd, L * NNORM + k + 1)
                for j in range(KD):
                    a = PAT[gain] + j
                    ins = dve.scalar_tensor_tensor(out=dst[:, j, :], in0=x[:, j, :], scalar=par[:, min(L, 1), a:a + 1],
                                                   in1=rstd[:], op0=ALU.mult, op1=ALU.mult)
                ins.then_inc(s_h, 1)

            def mixer(L):
                normed(L, 0, "norm_mix")
                w = quad(dve, L, Q_DT)
                dve.memset(raw[:, :, 0:CW - 1], 0.0)
                for c in range(CC):
                    a = KD * H + c * DB * (CW - 1)
                    dve.tensor_copy(raw[:, c, XS0:XW].rearrange("p (b j) -> p b j", b=DB)[:, :, 0:CW - 1],
                                    w[:, a:a + DB * (CW - 1)].rearrange("p (b j) -> p b j", b=DB))
                dve.wait_ge(s_proj, L * 45 + 29)
                dve.drain().then_inc(freed[Q_DT % RING], 1)
                for j in range(2 * RH):
                    dve.wait_ge(s_rot, L * 8 + j + 1)
                    tmp = rot_tmp[:, j % 2, :]
                    dve.tensor_tensor(tmp, psum[:, 4 + j % 2, 0:T], k_("sin", T), ALU.mult)
                    dve.tensor_tensor(kq[:, j, :], kq[:, j, :], k_("cos", T), ALU.mult)
                    dve.drain()
                    dve.tensor_tensor(kq[:, j, :], kq[:, j, :], tmp, ALU.add).then_inc(s_rotated, 1)
                d = [dt_tmp[0:H, i, :] for i in range(6)]
                dve.wait_ge(s_evac, L * 45 + 29)
                dve.tensor_scalar(d[0], d[0], par[0:H, L, PAT["dt_bias"]:PAT["dt_bias"] + 1], None, ALU.add)
                dve.drain()
                dve.scalar_tensor_tensor(out=d[1], in0=d[0], scalar=-1.0, in1=d[0], op0=ALU.mult, op1=ALU.max)
                dve.drain().then_inc(s_dtv, 1)
                dve.wait_ge(s_dta, L * 2 + 1)
                dve.tensor_scalar(d[3], d[2], 1.0, None, ALU.add)
                dve.drain().then_inc(s_dtv, 1)
                dve.wait_ge(s_dta, L * 2 + 2)
                dve.reciprocal(d[5], d[3])
                dve.tensor_scalar(d[3], d[3], -1.0, 1e-30, ALU.add, ALU.max)
                dve.drain()
                dve.reciprocal(d[3], d[3])
                dve.tensor_tensor(d[4], d[4], d[2], ALU.mult)
                dve.tensor_tensor(d[5], d[5], d[2], ALU.mult)
                dve.drain()
                dve.tensor_tensor(d[4], d[4], d[3], ALU.mult)
                dve.drain()
                dve.tensor_tensor(d[4], d[4], d[5], ALU.max)
                dve.drain()
                dve.scalar_tensor_tensor(out=dt_row[0:H, :], in0=d[0], scalar=0.0, in1=d[4], op0=ALU.max, op1=ALU.add)
                dve.drain()
                dve.tensor_scalar(d[1], dt_row[0:H, :], keep[0:H, 0:1], -1.0, ALU.mult, ALU.mult)
                dve.drain().then_inc(s_dtv, 1)
                dve.tensor_tensor_scan(acum_row[0:H, :], k_("restart", T, H), d[1], 0.0, ALU.mult, ALU.add)\
                    .then_inc(s_dtv, 1)
                for c in range(CC):
                    dve.wait_ge(s_evac, L * 45 + 16 + c + 1)
                    if c >= 2:
                        dve.wait_ge(s_silu, L * CC + c - 1)
                    a = conv_acc[:, c % 2, :]
                    wa, ba = PAT["conv_w"] + c * CW, PAT["conv_b"] + c
                    dve.tensor_scalar(a, raw[:, c, 0:XOUT], par[:, L, wa:wa + 1], par[:, L, ba:ba + 1],
                                      ALU.mult, ALU.add)
                    for j in range(1, CW):
                        dve.drain()
                        ins = dve.scalar_tensor_tensor(out=a, in0=raw[:, c, j:j + XOUT],
                                                       scalar=par[:, L, wa + j:wa + j + 1], in1=a,
                                                       op0=ALU.mult, op1=ALU.add)
                    ins.then_inc(s_conv, 1)
                dve.tensor_copy(conv_tail[:, :, 0:CW - 1], raw[:, :, XS0 - (CW - 1):XS0])
                for b in range(DB):
                    e = XS0 + (b + 1) * (CW - 1 + DS)
                    dve.tensor_copy(conv_tail[:, :, (b + 1) * (CW - 1):(b + 2) * (CW - 1)],
                                    raw[:, :, e - (CW - 1):e])
                dve.drain().then_inc(s_raw_free, 1)

                nb = 0
                dve.wait_ge(s_tout, (L + 1) * 19)
                dve.wait_ge(s_evac, (L + 1) * 45)
                for t in range(3):
                    n = TOKN[t]
                    hb, banks = heads_of(t)
                    xt = x_tok[0:n, t, :].rearrange("p (h d) -> p h d", h=H)
                    dve.tensor_tensor(xt, xt, dt_tok[0:n, t, :].unsqueeze(2).broadcast_to([n, H, HD]), ALU.mult)
                    dve.wait_ge(s_cb, L * 3 + t + 1)
                    mask = k_("causal", P) if t < 2 else k_("causal_s", NS, NS)
                    dve.tensor_tensor(cbm[0:n, :, 0:n],
                                      psum[0:n, 4, 0:G * P].rearrange("p (g l) -> p g l", g=G)[:, :, 0:n],
                                      mask.unsqueeze(1).broadcast_to([n, G, n]), ALU.mult)
                    for i in range(banks):
                        h0 = i * hb
                        if nb > 0:
                            dve.wait_ge(s_bc, L * 10 + nb)
                        dve.tensor_tensor(rows[0:H, :].rearrange("p (h l) -> p h l", h=hb),
                                          acum_row[0:H, tok(t)].unsqueeze(1).broadcast_to([H, hb, n]),
                                          ident[0:H, h0:h0 + hb].unsqueeze(2).broadcast_to([H, hb, n]), ALU.mult)\
                            .then_inc(s_rows, 1)
                        dve.wait_ge(s_bc, L * 10 + nb + 1)
                        bc = psum[:, 5, :].rearrange("p (h l) -> p h l", h=hb)
                        if nb > 0:
                            dve.wait_ge(s_y, L * 10 + nb)
                        e = decays[0:n, 0, :].rearrange("p (h l) -> p h l", h=hb)
                        for hh in range(hb):
                            dve.tensor_scalar(e[:, hh, :], bc[0:n, hh, :], acum_tok[0:n, t, h0 + hh:h0 + hh + 1],
                                              0.0, ALU.subtract, ALU.min)
                        if t < 2:
                            dve.tensor_copy(last[:, h0:h0 + hb], bc[:, :, n - 1])
                        else:
                            dve.tensor_copy(last_s[:, h0:h0 + hb, :],
                                            bc.rearrange("p h (b j) -> p h b j", b=DB)[:, :, :, DS - 1])
                        dve.drain().then_inc(s_diff, 1)
                        dve.wait_ge(s_exp, L * 10 + nb + 1)
                        g0 = h0 * G // H
                        dve.tensor_tensor(e, e, cbm[0:n, g0, 0:n].unsqueeze(1).broadcast_to([n, hb, n]), ALU.mult)
                        if t > 0:
                            cd = decays[:, 1, :].rearrange("p (h l) -> p h l", h=hb) if t == 1 \
                                else c_dec_s[:, h0:h0 + hb, :]
                            dve.tensor_tensor(cd, cd, xbc[:, 10 + g0, tok(t)].unsqueeze(1)
                                              .broadcast_to([P, hb, n]), ALU.mult)
                        dve.drain().then_inc(s_lm, 1)
                        if t < 2:
                            dve.wait_ge(s_y, L * 10 + nb + 1)
                            for c in range(2):
                                ch = 2 * i + c
                                a = PAT["d_skip"] + ch
                                ins = dve.scalar_tensor_tensor(out=xbc[:, ch, tok(t)], in0=xbc[:, ch, tok(t)],
                                                               scalar=par[:, L, a:a + 1],
                                                               in1=psum[:, 6, c * P:(c + 1) * P],
                                                               op0=ALU.mult, op1=ALU.add)
                            ins.then_inc(s_yout, 1)
                        nb += 1
                    if t < 2:
                        dve.tensor_tensor(decay_end[0:n, :], last[0:n, :], acum_tok[0:n, t, :], ALU.subtract)
                    else:
                        dve.tensor_tensor(last_own[0:n], last_s[0:n],
                                          k_("own", DB, NS).unsqueeze(1).broadcast_to([n, H, DB]), ALU.mult)
                        dve.drain()
                        dve.tensor_reduce(decay_end[0:n, :], last_own[0:n], AX.X, ALU.add)
                        dve.drain()
                        dve.tensor_tensor(decay_end[0:n, :], decay_end[0:n, :], acum_tok[0:n, t, :], ALU.subtract)
                    dve.drain().then_inc(s_dec, 1)
                    dve.wait_ge(s_dece, L * 3 + t + 1)
                    if t == 2:
                        dve.wait_ge(s_y, L * 10 + nb)
                    dve.tensor_tensor(xt, xt, decay_end[0:n, :].unsqueeze(2).broadcast_to([n, H, HD]), ALU.mult)\
                        .then_inc(s_xdec, 1)
                    if t == 1:
                        dve.wait_ge(s_cs, L * 2 + 2)
                        st = states_out[:, 0, 0:1024].rearrange("p (h d) -> p h d", h=H)
                        dve.tensor_tensor(st, st, keep[:].unsqueeze(2).broadcast_to([P, H, HD]), ALU.mult)
                        dve.drain()
                        st = states_out[:, 0, 0:1024].rearrange("p (a b) -> p a b", a=2)
                        dve.tensor_tensor(st, st, psum[:, 0:2, :], ALU.add).then_inc(s_csout, 1)

                for t in range(3):
                    n = TOKN[t]
                    dve.wait_ge(s_score, L * 3 + t + 1)
                    sfx = "" if t < 2 else "_s"
                    e = decays[0:n, 0, 0:RH * n]
                    dve.tensor_tensor(e, psum[0:n, 4, 0:RH * n], k_("decay" + sfx, RH * n, n), ALU.mult)
                    if t > 0:
                        qd = decays[:, 1, :].rearrange("p (h l) -> p h l", h=RH) if t == 1 else q_dec_s
                        dve.tensor_tensor(qd, kq[:, RH:2 * RH, tok(t)],
                                          k_("qdecay" + sfx, RH * n).rearrange("p (h l) -> p h l", h=RH), ALU.mult)
                    kt = k_tok[0:n, t, :].rearrange("p (h d) -> p h d", h=RH)
                    dve.tensor_tensor(kt, kt, k_("kend" + sfx, RH, n).unsqueeze(2).broadcast_to([n, RH, DK]), ALU.mult)
                    dve.drain().then_inc(s_decayed, 1)
                    if t == 1:
                        dve.wait_ge(s_kv, L * 2 + 2)
                        for r in range(RH):
                            st = states_out[:, 0, 1024 + r * DV:1024 + (r + 1) * DV]
                            dve.scalar_tensor_tensor(out=st, in0=st, scalar=float(gam[r] ** P),
                                                     in1=psum[:, r // 2, (r % 2) * DV:(r % 2 + 1) * DV],
                                                     op0=ALU.mult, op1=ALU.add)
                        dve.drain().then_inc(s_kvout, 1)

                for b in range(DB):
                    if b > 0:
                        dve.wait_ge(s_batch, L * DB + b)
                    own = k_("own", 1, NS, b)
                    dve.tensor_scalar(b_own[0:NS, :], b_tok[0:NS, 2, :], own, None, ALU.mult)
                    dve.tensor_scalar(k_own[0:NS, :], k_tok[0:NS, 2, :], own, None, ALU.mult)
                    dve.drain().then_inc(s_own, 1)
                    w = quad(dve, L, Q_STATE + b // 2)
                    ws = w[:, (b % 2) * 2048:(b % 2 + 1) * 2048]
                    slot = (b + 1) % 2
                    if b >= 1:
                        dve.wait_ge(s_store[slot], 16 * (L * (5 - slot) + (b + 1) // 2))
                    so = states_out[:, slot, :]
                    dve.tensor_tensor(so[:, 0:1024].rearrange("p (h d) -> p h d", h=H),
                                      ws[:, 0:1024].rearrange("p (h d) -> p h d", h=H),
                                      last_s[:, :, b].unsqueeze(2).broadcast_to([P, H, HD]), ALU.mult)
                    dve.wait_ge(s_batch, L * DB + b + 1)
                    for r in range(RH):
                        dve.scalar_tensor_tensor(out=so[:, 1024 + r * DV:1024 + (r + 1) * DV],
                                                 in0=ws[:, 1024 + r * DV:1024 + (r + 1) * DV],
                                                 scalar=float(gam[r] ** DS),
                                                 in1=psum[:, 2 + r // 2, (r % 2) * DV:(r % 2 + 1) * DV],
                                                 op0=ALU.mult, op1=ALU.add)
                    dve.drain()
                    so2 = so[:, 0:1024].rearrange("p (a b) -> p a b", a=2)
                    dve.tensor_tensor(so2, so2, psum[:, 0:2, :], ALU.add)
                    dve.drain().then_inc(s_newst, 1)
                    if b % 2 == 1:
                        dve.drain().then_inc(freed[(Q_STATE + b // 2) % RING], 1)
                ys = psum[:, 6, :].rearrange("p (c t) -> p c t", c=KD)
                for c in range(KD):
                    a = PAT["d_skip"] + c
                    dve.scalar_tensor_tensor(out=xbc[:, c, tok(2)], in0=xbc[:, c, tok(2)], scalar=par[:, L, a:a + 1],
                                             in1=ys[:, c, :], op0=ALU.mult, op1=ALU.add)
                dve.drain()
                dve.tensor_tensor(xbc[:, 0:KD, :], xbc[:, 0:KD, :], zv[:], ALU.mult).then_inc(s_gated, 1)
                dve.wait_ge(s_rstd6, L + 1)
                for c in range(KD):
                    a = PAT["ssd_gain"] + c
                    dve.scalar_tensor_tensor(out=xbc[:, c, :], in0=xbc[:, c, :], scalar=par[:, L, a:a + 1],
                                             in1=rstd6[:, c // 4, :], op0=ALU.mult, op1=ALU.mult)
                for c in range(KD):
                    a = PAT["ret_gain"] + c
                    dve.scalar_tensor_tensor(out=kq[:, c, :], in0=kq[:, c, :], scalar=par[:, L, a:a + 1],
                                             in1=rstd6[:, 2 + c // 2, :], op0=ALU.mult, op1=ALU.mult)
                dve.drain()
                dve.tensor_tensor(kq[:], kq[:], gate[:], ALU.mult).then_inc(s_mix, 1)
                for j in range(KD):
                    dve.wait_ge(s_wout, L * 16 + j + 1)
                    dve.tensor_tensor(x[:, j, :], x[:, j, :], psum[:, j % 4, 0:T], ALU.add).then_inc(s_xadd, 1)

            def attention(L):
                dve.memset(q_own[:], 0.0).then_inc(s_qzero, 1)
                normed(L, 1, "norm_mem")
                for t in range(3):
                    n = TOKN[t]
                    dve.wait_ge(s_xs, L * 3 + t + 1)
                    dve.tensor_reduce(xmax[0:n, t, :],
                                      psum[0:n, 2 * t:2 * t + 2, :].rearrange("p a (b m) -> p a b m", b=2),
                                      AX.X, ALU.max)
                    dve.drain()
                    dve.tensor_scalar(xmax[0:n, t, :], xmax[0:n, t, :], -1.0 / 16, None, ALU.mult).then_inc(s_xmax, 1)
                for t in range(3):
                    n = TOKN[t]
                    dve.wait_ge(s_xexp, L * 3 + t + 1)
                    dve.reciprocal(xsum[0:n, t, :], xsum[0:n, t, :])
                    dve.drain()
                    dve.tensor_tensor(prob[0:n, t], prob[0:n, t],
                                      xsum[0:n, t, :].unsqueeze(2).broadcast_to([n, XH, M]), ALU.mult)\
                        .then_inc(s_prob, 1)
                for j in range(KD):
                    dve.wait_ge(s_wout, L * 16 + KD + j + 1)
                    dve.tensor_tensor(x[:, j, :], x[:, j, :], psum[:, j % 4, 0:T], ALU.add).then_inc(s_xadd, 1)

            def first_of(mask, vals, top, tmp):
                dve.tensor_tensor(mask, vals, top.unsqueeze(2).broadcast_to([P, 3, EPG]), ALU.is_equal)
                dve.drain()
                dve.tensor_tensor(mask, mask, k_("rank", EPG).unsqueeze(1).broadcast_to([P, 3, EPG]), ALU.mult)
                dve.drain()
                dve.tensor_reduce(tmp, mask, AX.X, ALU.max)
                dve.drain()
                dve.tensor_tensor(mask, mask, tmp.unsqueeze(2).broadcast_to([P, 3, EPG]), ALU.is_equal)
                dve.drain()

            def moe(L):
                normed(L, 2, "norm_ffn")
                dve.memset(logits[:], 0.0)
                dve.drain()
                dve.wait_ge(s_route, L + 1)
                a = PAT["route_b"]
                for t in range(3):
                    n = TOKN[t]
                    dve.tensor_tensor(logits[0:n, t, :], psum[0:n, 6, t * 32:t * 32 + EG + E],
                                      par[0:n, L, a:a + EG + E], ALU.add)
                dve.drain()
                gl = logits[:, :, 0:EG]
                dve.tensor_reduce(gmax, gl, AX.X, ALU.max)
                dve.drain()
                first_of(gsel, gl, gmax, mt)
                dve.tensor_tensor(gtmp, gl, gmax.unsqueeze(2).broadcast_to([P, 3, EG]), ALU.subtract)
                for t in range(3):
                    dve.tensor_tensor(epick[:, t], logits[:, t, EG:].rearrange("p (g e) -> p g e", g=EG),
                                      gsel[:, t, :].unsqueeze(2).broadcast_to([P, EG, EPG]), ALU.mult)
                dve.drain()
                dve.tensor_tensor(el, epick[:, :, 0, :], epick[:, :, 1, :], ALU.add)
                dve.drain()
                dve.tensor_tensor(el, el, epick[:, :, 2, :], ALU.add)
                dve.drain()
                dve.tensor_tensor(el, el, epick[:, :, 3, :], ALU.add)
                dve.drain()
                dve.tensor_reduce(m1, el, AX.X, ALU.max)
                dve.drain()
                first_of(e1, el, m1, mt)
                dve.scalar_tensor_tensor(out=el, in0=e1, scalar=-1e30, in1=el, op0=ALU.mult, op1=ALU.add)
                dve.drain()
                dve.tensor_reduce(m2, el, AX.X, ALU.max)
                dve.drain()
                first_of(e2, el, m2, mt)
                dve.tensor_tensor(mt, m2, m1, ALU.subtract)
                dve.drain().then_inc(s_rv, 1)
                dve.wait_ge(s_ra, L + 1)
                dve.tensor_reduce(gden, gtmp, AX.X, ALU.add)
                dve.tensor_scalar(w1, mt, 1.0, None, ALU.add)
                dve.drain()
                dve.tensor_tensor(w1, w1, gden, ALU.mult)
                dve.drain()
                dve.reciprocal(w1, w1)
                dve.drain()
                dve.tensor_tensor(w2, w1, mt, ALU.mult)
                dve.tensor_tensor(e1, e1, w1.unsqueeze(2).broadcast_to([P, 3, EPG]), ALU.mult)
                dve.drain()
                dve.tensor_tensor(e2, e2, w2.unsqueeze(2).broadcast_to([P, 3, EPG]), ALU.mult)
                dve.drain()
                dve.tensor_tensor(e1, e1, e2, ALU.add)
                dve.drain()
                for t in range(3):
                    dve.tensor_tensor(gates_tok[:, t], gsel[:, t, :].unsqueeze(2).broadcast_to([P, EG, EPG]),
                                      e1[:, t, :].unsqueeze(1).broadcast_to([P, EG, EPG]), ALU.mult)
                dve.drain().then_inc(s_rv, 1)
                for i in range(2):
                    dve.wait_ge(s_store[i], 16 * (5 - i) * (L + 1))
                dve.wait_ge(s_tstore, 16 * (L + 1))
                dve.wait_ge(s_mkstore, 16 * (L + 1))
                dve.wait_ge(s_mvstore, 16 * (L + 1))
                dve.wait_ge(s_grow, L + 1)
                for e in range(E):
                    if e >= 2:
                        dve.wait_ge(s_gb, L * E + e - 1)
                    dve.tensor_scalar(one_row[0:E, e % 2, :], gate_row[0:E, :], ident[0:E, e:e + 1], None, ALU.mult)\
                        .then_inc(s_orow, 1)
                with dve.Fori(0, E // 4) as i4:
                    for u in range(4):
                        seen = L * E * 4 + i4 * 16 + u * 4
                        for f in range(FC):
                            dve.wait_ge(s_up, seen + f + 1)
                            dve.wait_ge(s_sg, seen + f + 1)
                            sg = silu_gate[:, f % 2, :]
                            dve.tensor_tensor(sg, sg, psum[:, 2 + f % 2, 0:T], ALU.mult)
                            dve.drain()
                            dve.tensor_tensor(hidden[:, f, :], sg, gates_all[:, i4 * 4 + u, :], ALU.mult)\
                                .then_inc(s_hid, 1)
                        for j in range(KD):
                            dve.wait_ge(s_down, seen * 2 + j + 1)
                            dve.tensor_tensor(x[:, j, :], x[:, j, :], psum[:, 4 + j % 4, 0:T], ALU.add)\
                                .then_inc(s_added, 1)

            dve.wait_ge(s_const, 48)
            for L in range(DEPTH):
                mixer(L)
                attention(L)
                moe(L)
            normed(DEPTH, 0, "norm_final")

        @block.gpsimd
        def _(pool):
            for L in range(DEPTH):
                pool.wait_ge(s_raw_free, L + 1)
                pool.dma_start(conv_out[L], conv_tail[:]).then_inc(s_tstore, 16)
                pool.wait_ge(s_csout, L * 2 + 2)
                pool.wait_ge(s_kvout, L * 2 + 2)
                pool.dma_start(st_out[L, 0], states_out[:, 0, :]).then_inc(s_store[0], 16)
                for b in range(DB):
                    pool.wait_ge(s_newst, L * DB + b + 1)
                    pool.dma_start(st_out[L, 1 + b], states_out[:, (b + 1) % 2, :]).then_inc(s_store[(b + 1) % 2], 16)
                pool.wait_ge(s_mix, L + 1)
                pool.dma_start(mem[:], mem_in).then_inc(s_mem, 16)
                pool.wait_ge(s_mkvout, L * 16 + 8)
                pool.dma_start(mk_out[L], k_mem[:]).then_inc(s_mkstore, 16)
                pool.wait_ge(s_mkvout, L * 16 + 16)
                pool.dma_start(mv_out[L], vt_mem[:]).then_inc(s_mvstore, 16)
            pool.wait_ge(s_h, DEPTH * NNORM + 1)
            pool.dma_start(y_out, h[:]).then_inc(s_ystore, 16)
            pool.wait_ge(s_ystore, 16)
            for i in range(2):
                pool.wait_ge(s_store[i], 16 * (5 - i) * DEPTH)
            pool.wait_ge(s_mkstore, 16 * DEPTH)
            pool.wait_ge(s_mvstore, 16 * DEPTH)
            pool.wait_ge(s_tstore, 16 * DEPTH)


def kernel(x_prompt, x_sample, mem_prompt, state_ssm, state_conv, state_ret, cache_mem_k, cache_mem_v,
           norm_mix, w_in, conv_w, conv_b, dt_bias, a_log, d_skip, ssd_gain, ret_gain, w_out,
           norm_mem, w_mq, w_mk, w_mv, w_mo, norm_ffn, w_rg, b_rg, w_re, b_re, w_gate, w_up, w_down,
           norm_final):
    import concourse.bacc as bacc
    from concourse.bass_utils import run_bass_kernel_spmd

    f = lambda a: np.asarray(a)

    def features(a):
        a = f(a)
        return np.moveaxis(a.reshape(*a.shape[:-2], a.shape[-2] // P, P, a.shape[-1]), -3, -2)

    def slabs(w):
        k, c = w.shape
        return w.reshape(k // P, P, c // P, P).transpose(2, 1, 0, 3)

    def quads(w):
        w = w.reshape(w.shape[0], P, -1)
        per = QUAD // w.shape[2]
        return w.reshape(-1, per, P, w.shape[2]).transpose(0, 2, 1, 3).reshape(-1, P, QUAD)

    w_in, w_out = f(w_in), f(w_out)
    w_gate, w_up, w_down = f(w_gate), f(w_up), f(w_down)
    offs = np.cumsum([0, D, CC * P, H, RH * DK, RH * DK, D, D])
    state_conv, state_ssm, state_ret = f(state_conv), f(state_ssm), f(state_ret)
    cache_mem_k, cache_mem_v = f(cache_mem_k), f(cache_mem_v)
    stream = np.zeros((DEPTH, QUADS, P, QUAD), np.float32)
    for l in range(DEPTH):
        z, xbc, dt, q, k, v, g = [w_in[l][:, offs[i]:offs[i + 1]] for i in range(7)]
        st = stream[l]
        for at, w in ((Q_V, v), (Q_K, k), (Q_Q, q), (Q_XBC, xbc), (Q_Z, z), (Q_G, g), (Q_OUT, w_out[l]),
                      (Q_MK, f(w_mk)[l]), (Q_MV, f(w_mv)[l]), (Q_MQ, f(w_mq)[l]), (Q_MO, f(w_mo)[l])):
            r = quads(slabs(w))
            st[at:at + len(r)] = r
        st[Q_DT, :, 0:KD * H] = dt.reshape(KD, P, H).transpose(1, 0, 2).reshape(P, -1)
        c = state_conv[l].reshape(DB, CW - 1, CC, P).transpose(3, 2, 0, 1)
        st[Q_DT, :, KD * H:KD * H + CC * DB * (CW - 1)] = c.reshape(P, -1)
        both = np.concatenate([state_ssm[l].transpose(0, 3, 1, 2).reshape(DB, P, 1024),
                               state_ret[l].transpose(0, 2, 1, 3).reshape(DB, P, 1024)], 2)
        st[Q_STATE:Q_STATE + 4] = both.reshape(4, 2, P, 2048).transpose(0, 2, 1, 3).reshape(4, P, QUAD)
        kc = cache_mem_k[l].reshape(DB, M, KD, P).transpose(0, 3, 2, 1).reshape(DB, P, 2048)
        vc = cache_mem_v[l].reshape(DB, 2, P, D).transpose(0, 2, 1, 3).reshape(DB, P, 2048)
        st[Q_KC:Q_KC + 4] = kc.reshape(4, 2, P, 2048).transpose(0, 2, 1, 3).reshape(4, P, QUAD)
        st[Q_VC:Q_VC + 4] = vc.reshape(4, 2, P, 2048).transpose(0, 2, 1, 3).reshape(4, P, QUAD)
        for e in range(E):
            gs, us = slabs(w_gate[l, e]), slabs(w_up[l, e])
            gu = np.stack([gs, us], 1).reshape(2 * FC, P, SLAB)
            st[Q_MOE + 3 * e:Q_MOE + 3 * e + 2] = quads(gu)
            st[Q_MOE + 3 * e + 2] = slabs(w_down[l, e]).transpose(1, 0, 2, 3).reshape(P, QUAD)

    params = np.zeros((DEPTH, P, PN), np.float32)

    def put(name, l, a):
        params[l, :a.shape[0], PAT[name]:PAT[name] + a.shape[1]] = a

    for l in range(DEPTH):
        for name, a in (("norm_mix", norm_mix), ("norm_mem", norm_mem), ("norm_ffn", norm_ffn),
                        ("ssd_gain", ssd_gain), ("ret_gain", ret_gain)):
            put(name, l, f(a)[l].reshape(KD, P).T)
        put("norm_final", l, f(norm_final).reshape(KD, P).T)
        put("d_skip", l, np.repeat(f(d_skip)[l], HD).reshape(KD, P).T)
        put("conv_b", l, f(conv_b)[l].reshape(CC, P).T)
        put("conv_w", l, f(conv_w)[l].reshape(CW, CC, P).transpose(2, 1, 0).reshape(P, -1))
        put("dt_bias", l, f(dt_bias)[l][:, None])
        put("a_log", l, f(a_log)[l][:, None])
        put("route_b", l, np.tile(np.concatenate([f(b_rg)[l], f(b_re)[l]])[None], (P, 1)))
        w = np.concatenate([f(w_rg)[l], f(w_re)[l]], 1)
        put("route_w", l, w.reshape(KD, P, EG + E).transpose(1, 0, 2).reshape(P, -1))

    tokens = np.concatenate([f(x_prompt).reshape(SEQ, D), f(x_sample).reshape(NS, D)], 0)
    ins = {
        "stream": stream.reshape(DEPTH * QUADS, P, QUAD),
        "params": params,
        "consts": constants(),
        "x_in": np.ascontiguousarray(features(tokens.T)),
        "mem_in": np.ascontiguousarray(features(f(mem_prompt)[0].T)),
    }
    outs = {"y_out": (P, KD, T), "st_out": (DEPTH, 1 + DB, P, 2048), "conv_out": (DEPTH, P, CC, (CW - 1) * (1 + DB)),
            "mk_out": (DEPTH, P, KD, M), "mv_out": (DEPTH, P, KD, M)}
    nc = bacc.Bacc("TRN2", target_bir_lowering=False, num_devices=1)
    aps = [nc.dram_tensor(n, a.shape, F32, kind="ExternalInput").ap() for n, a in ins.items()]
    aps += [nc.dram_tensor(n, s, F32, kind="ExternalOutput").ap() for n, s in outs.items()]
    build(nc, *aps)
    r = run_bass_kernel_spmd(nc, [ins], core_ids=[0]).results[0]

    y = np.asarray(r["y_out"]).transpose(2, 1, 0).reshape(T, D)
    st = np.asarray(r["st_out"])
    ssm = st[..., 0:1024].reshape(DEPTH, 1 + DB, N, H, HD).transpose(0, 1, 3, 4, 2)
    ret = st[..., 1024:].reshape(DEPTH, 1 + DB, DK, RH, DV).transpose(0, 1, 3, 2, 4)
    conv = np.asarray(r["conv_out"]).reshape(DEPTH, P, CC, 1 + DB, CW - 1).transpose(0, 3, 4, 2, 1)
    conv = conv.reshape(DEPTH, 1 + DB, CW - 1, CC * P)

    def memory(a):
        return np.asarray(a).transpose(0, 3, 2, 1).reshape(DEPTH, 1, M, XH, DV)

    c = np.ascontiguousarray
    return (c(y[:SEQ].reshape(1, SEQ, D)), c(y[SEQ:].reshape(DB, DS, D)), c(ssm[:, :1]), c(conv[:, :1]), c(ret[:, :1]),
            c(memory(r["mk_out"])), c(memory(r["mv_out"])), c(ssm[:, 1:]), c(conv[:, 1:]), c(ret[:, 1:]))
```

```python
from contextlib import ExitStack

import numpy as np

import concourse.bass as bass
from concourse import mybir

F32 = mybir.dt.float32
ACT = mybir.ActivationFunctionType
ALU = mybir.AluOpType
AX = mybir.AxisListType

P = 128
DEPTH = 2
D = 1024
KD = D // P
SEQ = 256
DB, DS = 8, 8
NS = DB * DS
T = SEQ + NS
PAST = 2048
H, HD, G, N = 16, 64, 2, 128
CW = 4
CC = 12
RH, DK, DV = 4, 128, 256
M = 256
XH = 4
EG, EPG = 4, 4
E = 16
FC = 4
EPS = 1e-6
CAP = P
ROPE_BASE = 10000.0
BANK = 512

TOK0 = [0, 128, 256]
TOKN = [128, 128, 64]

SLAB = KD * P
QUAD = 4 * SLAB
RING = 4
Q_V, Q_K, Q_Q, Q_XBC, Q_DT, Q_Z, Q_G = 0, 2, 3, 4, 7, 8, 10
Q_STATE = 12
Q_OUT = 16
Q_MK, Q_MV, Q_MQ = 20, 22, 24
Q_KC, Q_VC = 26, 30
Q_MO = 34
Q_MOE = 36
QUADS = Q_MOE + 3 * E
REVS = QUADS // RING
assert QUADS % RING == 0 and Q_MOE % RING == 0

XW = CW - 1 + SEQ + DB * (CW - 1 + DS)
XS0 = CW - 1 + SEQ
XOUT = XW - (CW - 1)


def layout_of(sizes):
    at, n = {}, 0
    for name, size in sizes:
        at[name] = n
        n += size
    return at, n


CONSTS = [("ident", P), ("ones", P), ("rot", P), ("cos", T), ("sin", T), ("causal", P), ("causal_s", NS),
          ("decay", RH * P), ("decay_s", RH * NS), ("qdecay", RH * P), ("qdecay_s", RH * NS),
          ("kend", RH), ("kend_s", RH), ("own", DB), ("restart", T), ("rank", EPG), ("eps", 1), ("slots", P)]
CAT, CN = layout_of(CONSTS)
PARAMS = [("norm_mix", KD), ("norm_mem", KD), ("norm_ffn", KD), ("norm_final", KD), ("ssd_gain", KD),
          ("ret_gain", KD), ("d_skip", KD), ("conv_b", CC), ("conv_w", CC * CW), ("dt_bias", 1), ("a_log", 1),
          ("route_b", EG + E), ("route_w", KD * (EG + E))]
PAT, PN = layout_of(PARAMS)


def gammas():
    return 1.0 - 2.0 ** (-5.0 - np.arange(RH))


def constants():
    c = np.zeros((P, CN), np.float64)

    def put(name, a):
        c[:a.shape[0], CAT[name]:CAT[name] + a.shape[1]] = a

    put("ident", np.eye(P))
    put("ones", np.ones((P, P)))
    half = DK // 2
    rot = np.zeros((P, P))
    for m in range(half):
        rot[m + half, m] = -1.0
        rot[m, m + half] = 1.0
    put("rot", rot)
    pos = np.concatenate([np.arange(SEQ), np.tile(PAST + np.arange(DS), DB)]).astype(np.float32)
    inv = (np.float32(ROPE_BASE) ** (-np.arange(half, dtype=np.float32) / np.float32(half))).astype(np.float32)
    ang = (pos[None, :] * inv[:, None]).astype(np.float32).astype(np.float64)
    put("cos", np.tile(np.cos(ang), (2, 1)))
    put("sin", np.tile(np.sin(ang), (2, 1)))
    s, l = np.arange(P)[:, None], np.arange(P)[None, :]
    put("causal", (l >= s) * 1.0)
    ss, ls = np.arange(NS)[:, None], np.arange(NS)[None, :]
    same = (ss // DS == ls // DS) & (ls >= ss)
    put("causal_s", same * 1.0)
    scale = DK ** -0.5
    lg = np.log(gammas())
    put("decay", np.concatenate([np.where(l >= s, np.exp((l - s) * g), 0.0) * scale for g in lg], 1))
    put("decay_s", np.concatenate([np.where(same, np.exp((ls - ss) * g), 0.0) * scale for g in lg], 1))
    put("qdecay", np.tile(np.concatenate([np.exp((np.arange(P) + 1) * g) for g in lg])[None], (P, 1)))
    put("qdecay_s", np.tile(np.concatenate([np.exp((np.arange(NS) % DS + 1) * g) for g in lg])[None], (P, 1)))
    put("kend", np.stack([np.exp((P - 1 - np.arange(P)) * g) for g in lg], 1) * scale)
    put("kend_s", np.stack([np.exp((DS - 1 - np.arange(NS) % DS) * g) for g in lg], 1) * scale)
    put("own", (np.arange(NS)[:, None] // DS == np.arange(DB)[None]) * 1.0)
    start = np.ones(T)
    start[[0, P] + [SEQ + b * DS for b in range(DB)]] = 0.0
    put("restart", np.tile(start[None], (H, 1)))
    put("rank", np.tile(np.arange(EPG, 0, -1.0)[None], (P, 1)))
    put("eps", np.full((P, 1), EPS))
    put("slots", np.tile(np.arange(1, CAP + 1.0)[None], (P, 1)))
    return c.astype(np.float32)


def build(nc, stream, params, consts, x_in, mem_in, y_out, st_out, conv_out, mk_out, mv_out):
    with ExitStack() as ctx:
        def sb(name, *shape):
            return ctx.enter_context(nc.sbuf_tensor(name, [P, *shape], F32))

        def sem(name):
            return ctx.enter_context(nc.semaphore(name))

        ring = sb("ring", RING, QUAD)
        cst = sb("cst", CN)
        par = sb("par", DEPTH, PN)
        x = sb("x", KD, T)
        h = sb("h", KD, T)
        work_n = 21572
        work = sb("work", work_n)
        states_out = sb("states_out", 2, 2048)
        rstd = sb("rstd", T)
        dt_row = sb("dt_row", T)
        acum_row = sb("acum_row", T)
        dt_tok = sb("dt_tok", 3, H)
        acum_tok = sb("acum_tok", 3, H)
        cbm = sb("cbm", G, P)
        last = sb("last", H)
        last_s = sb("last_s", H, DB)
        last_own = sb("last_own", H, DB)
        decay_end = sb("decay_end", H)
        keep = sb("keep", H)
        conv_tail = sb("conv_tail", CC, (CW - 1) * (1 + DB))
        spilt = ctx.enter_context(nc.sbuf_tensor("spilt", [P, DEPTH], mybir.dt.int32))
        psum = ctx.enter_context(nc.psum_tensor("psum", [P, 8, BANK], F32))

        def view(tensor, at, *shape):
            n = int(np.prod(shape))
            v = tensor[:, at:at + n]
            if len(shape) == 1:
                return v
            names = "abcd"[:len(shape)]
            return v.rearrange(f"p ({' '.join(names)}) -> p {' '.join(names)}",
                               **{k: s for k, s in zip(names, shape)})

        zv = view(work, 0, KD, T)
        raw = view(work, 2560, CC, XW)
        gate = view(work, 2560, KD, T)
        decays = view(work, 5120, 3, BANK)
        xbc = view(work, 6724, CC, T)
        kq = view(work, 10564, 2 * RH, T)
        v_tok = view(work, 13124, 3, D)
        x_tok = view(work, 16196, 3, D)
        conv_acc = view(work, 16196, 2, XOUT)
        dt_tmp = view(work, 16196 + 2 * XOUT, 6, T)
        b_tok = view(work, 19268, 3, G * N)
        k_tok = view(work, 20036, 3, RH * DK)
        rot_tmp = view(work, 20036, 2, T)
        rstd6 = view(work, 13124, 6, T)
        hflat = h[:].rearrange("p a b -> p (a b)")
        c_dec_s = hflat[:, 0:1024].rearrange("p (h t) -> p h t", h=H)
        q_dec_s = hflat[:, 1024:1280].rearrange("p (h t) -> p h t", h=RH)
        k_own = hflat[:, 1280:1792]
        b_own = hflat[:, 1792:2048]
        rows = hflat[:, 2048:2560]
        mem = view(work, 0, KD, M)
        k_mem = view(work, 2048, KD, M)
        vt_mem = view(work, 4096, KD, M)
        v_mem = view(work, 6144, 2, D)
        q_p = view(work, 8192, KD, SEQ)
        q_own = view(work, 10240, KD, DB, NS)
        prob = view(work, 14336, 3, XH, M)
        prob_t = view(work, 17408, XH, 2, T)
        xmax = view(work, 19968, 3, XH)
        xsum = view(work, 19980, 3, XH)
        chosen = view(work, 0, 3, EG, CAP)
        chosen_t = view(work, 1536, EG, T)
        h_tok = view(work, 2816, 3, D)
        h_packed = view(work, 5888, KD, EG, CAP)
        gates = view(work, 9984, EPG, EG, CAP)
        h_group = view(work, 12032, KD, CAP)
        y_group = view(work, 13056, D)
        chosen_group = view(work, 14080, T)
        silu_gate = view(work, 14400, 2, 2 * CAP)
        hidden = view(work, 14912, FC, CAP)
        gate_cols = view(work, 15424, 3, EPG, P)
        all_gates = view(work, 0, E, T)
        all_silu = view(work, 5120, 2, T)
        all_hidden = view(work, 5760, FC, T)
        gate_row = view(work, 7040, T)
        one_row = view(work, 7360, 2, T)
        all_w = view(work, 8192, 3, QUAD)
        R0 = 20500
        logits = view(work, R0 + 300, 3, EG + E)
        gmax = view(work, R0, 3)
        gsel = view(work, R0 + 10, 3, EG)
        gtmp = view(work, R0 + 30, 3, EG)
        gden = view(work, R0 + 50, 3)
        epick = view(work, R0 + 60, 3, EG, EPG)
        el = view(work, R0 + 120, 3, EPG)
        e1 = view(work, R0 + 140, 3, EPG)
        e2 = view(work, R0 + 160, 3, EPG)
        m1 = view(work, R0 + 180, 3)
        m2 = view(work, R0 + 190, 3)
        mt = view(work, R0 + 200, 3)
        w1 = view(work, R0 + 210, 3)
        w2 = view(work, R0 + 220, 3)
        slot = view(work, R0 + 230, 3)
        over = view(work, R0 + 240, 3)
        most = view(work, R0 + 250, 1)
        ranked = view(work, R0 + 260, 3, EG)
        spilt_gates = view(work, R0 + 400, 3, EG, EPG)

        def k_(name, n, rows_=P, at=0):
            return cst[0:rows_, CAT[name] + at:CAT[name] + at + n]

        ident, ones = k_("ident", P), k_("ones", P)

        s_const = sem("s_const")
        loaded = [sem(f"s_loaded{s}") for s in range(RING)]
        freed = [sem(f"s_freed{s}") for s in range(RING)]
        s_sq = sem("s_sq")
        s_sum = sem("s_sum")
        s_rstd = sem("s_rstd")
        s_h = sem("s_h")
        s_proj = sem("s_proj")
        s_evac = sem("s_evac")
        s_rot = sem("s_rot")
        s_rotated = sem("s_rotated")
        s_dtv = sem("s_dtv")
        s_dta = sem("s_dta")
        s_conv = sem("s_conv")
        s_raw_free = sem("s_raw_free")
        s_silu = sem("s_silu")
        s_t = sem("s_t")
        s_tout = sem("s_tout")
        s_cb = sem("s_cb")
        s_rows = sem("s_rows")
        s_bc = sem("s_bc")
        s_diff = sem("s_diff")
        s_exp = sem("s_exp")
        s_lm = sem("s_lm")
        s_y = sem("s_y")
        s_yout = sem("s_yout")
        s_dec = sem("s_dec")
        s_dece = sem("s_dece")
        s_xdec = sem("s_xdec")
        s_cs = sem("s_cs")
        s_csout = sem("s_csout")
        s_score = sem("s_score")
        s_decayed = sem("s_decayed")
        s_o = sem("s_o")
        s_oout = sem("s_oout")
        s_kv = sem("s_kv")
        s_kvout = sem("s_kvout")
        s_own = sem("s_own")
        s_batch = sem("s_batch")
        s_newst = sem("s_newst")
        s_store = [sem(f"s_store{i}") for i in range(2)]
        s_gated = sem("s_gated")
        s_sq6 = sem("s_sq6")
        s_sum6 = sem("s_sum6")
        s_rstd6 = sem("s_rstd6")
        s_mix = sem("s_mix")
        s_wout = sem("s_wout")
        s_xadd = sem("s_xadd")
        s_mem = sem("s_mem")
        s_mkv = sem("s_mkv")
        s_mkvout = sem("s_mkvout")
        s_vt = sem("s_vt")
        s_vtout = sem("s_vtout")
        s_mkstore = sem("s_mkstore")
        s_mvstore = sem("s_mvstore")
        s_qzero = sem("s_qzero")
        s_q = sem("s_q")
        s_qout = sem("s_qout")
        s_xs = sem("s_xs")
        s_xmax = sem("s_xmax")
        s_xexp = sem("s_xexp")
        s_prob = sem("s_prob")
        s_pt = sem("s_pt")
        s_ptout = sem("s_ptout")
        s_xo = sem("s_xo")
        s_xoout = sem("s_xoout")
        s_route = sem("s_route")
        s_rv = sem("s_rv")
        s_ra = sem("s_ra")
        s_ht = sem("s_ht")
        s_htout = sem("s_htout")
        s_cnt = sem("s_cnt")
        s_chosen = sem("s_chosen")
        s_pack = sem("s_pack")
        s_packout = sem("s_packout")
        s_gs = sem("s_gs")
        s_gsout = sem("s_gsout")
        s_ct = sem("s_ct")
        s_ctout = sem("s_ctout")
        s_group = sem("s_group")
        s_gate = sem("s_gate")
        s_up = sem("s_up")
        s_sg = sem("s_sg")
        s_hid = sem("s_hid")
        s_down = sem("s_down")
        s_yg = sem("s_yg")
        s_spread = sem("s_spread")
        s_added = sem("s_added")
        s_spilt = sem("s_spilt")
        d_start = sem("d_start")
        d_loaded = sem("d_loaded")
        d_gt = sem("d_gt")
        d_grow = sem("d_grow")
        d_orow = sem("d_orow")
        d_gb = sem("d_gb")
        d_gbout = sem("d_gbout")
        d_gate = sem("d_gate")
        d_up = sem("d_up")
        d_sg = sem("d_sg")
        d_hid = sem("d_hid")
        d_down = sem("d_down")
        d_added = sem("d_added")
        d_end = sem("d_end")
        s_tstore = sem("s_tstore")
        s_ystore = sem("s_ystore")

        block = ctx.enter_context(nc.Block())
        NNORM = 3
        gam = gammas()

        def quad(eng, L, q):
            eng.wait_ge(loaded[q % RING], 16 * (L * REVS + q // RING + 1))
            return ring[:, q % RING, :]

        def tok(t):
            return slice(TOK0[t], TOK0[t] + TOKN[t])

        def heads_of(t):
            hb = BANK // TOKN[t]
            return hb, H // hb

        @block.sync
        def _(sp):
            sp.dma_start(x[:], x_in).then_inc(s_const, 16)
            sp.dma_start(cst[:], consts).then_inc(s_const, 16)
            sp.dma_start(par[:], params.rearrange("l p n -> p l n")).then_inc(s_const, 16)
            for L in range(DEPTH):
                for r in range(REVS):
                    n = L * REVS + r
                    for s in range(RING):
                        if n >= 1:
                            sp.wait_ge(freed[s], n)
                        sp.dma_start(ring[:, s, :], stream[n * RING + s]).then_inc(loaded[s], 16)
                sp.wait_ge(s_spilt, L + 1)
                with sp.If(sp.value_load(spilt[0:1, L:L + 1], min_val=0, max_val=1) > 0):
                    for e in range(E):
                        sp.wait_ge(d_start, L * (E + 1) + e + 1)
                        q = L * QUADS + Q_MOE + 3 * e
                        sp.dma_start(all_w[:], stream[q:q + 3].rearrange("q p n -> p q n")).then_inc(d_loaded, 16)
                with sp.Else():
                    sp.sem_inc(d_loaded, 16 * E)

        @block.tensor
        def _(pe):
            def sums(L, k):
                pe.wait_ge(s_sq, L * NNORM + k + 1)
                for j in range(KD):
                    mm = pe.matmul(psum[:, 7, 0:T], ones, h[:, j, :], start=(j == 0), stop=(j == KD - 1))
                mm.then_inc(s_sum, 1)

            def transposes(outs_ins):
                for o, i in outs_ins:
                    mm = pe.transpose(o, i, ident[0:i.shape[0], 0:i.shape[0]])
                return mm

            def mixer(L):
                sums(L, 0)
                pe.wait_ge(s_h, L * NNORM + 1)
                n_proj = 0

                def project(q0, chunks):
                    nonlocal n_proj
                    for c in range(chunks):
                        w = quad(pe, L, q0 + c // 4)
                        if n_proj >= 4:
                            pe.wait_ge(s_evac, L * 45 + n_proj - 3)
                        for j in range(KD):
                            a = (c % 4) * SLAB + j * P
                            mm = pe.matmul(psum[:, n_proj % 4, 0:T], w[:, a:a + P], h[:, j, :],
                                           start=(j == 0), stop=(j == KD - 1))
                        mm.then_inc(s_proj, 1)
                        n_proj += 1
                        if c % 4 == 3:
                            pe.drain().then_inc(freed[(q0 + c // 4) % RING], 1)

                project(Q_V, 8)
                project(Q_K, 4)
                project(Q_Q, 4)
                project(Q_XBC, 12)
                w = quad(pe, L, Q_DT)
                pe.wait_ge(s_evac, L * 45 + n_proj - 3)
                for j in range(KD):
                    mm = pe.matmul(psum[0:H, n_proj % 4, 0:T], w[:, j * H:(j + 1) * H], h[:, j, :],
                                   start=(j == 0), stop=(j == KD - 1))
                mm.then_inc(s_proj, 1)
                n_proj += 1
                for j in range(2 * RH):
                    pe.wait_ge(s_evac, L * 45 + 8 + j + 1)
                    if j >= 2:
                        pe.wait_ge(s_rotated, L * 8 + j - 1)
                    pe.matmul(psum[:, 4 + j % 2, 0:T], k_("rot", P), kq[:, j, :], start=True, stop=True)\
                        .then_inc(s_rot, 1)
                nt = 0

                def turn(group, n):
                    nonlocal nt
                    if nt >= 2:
                        pe.wait_ge(s_tout, L * 19 + nt - 1)
                    b = 6 + nt % 2
                    transposes([(psum[0:n, b, i * P:(i + 1) * P], src) for i, src in enumerate(group)])\
                        .then_inc(s_t, 1)
                    nt += 1

                for t in range(3):
                    for half in range(2):
                        turn([zv[:, 4 * half + i, tok(t)] for i in range(4)], TOKN[t])
                project(Q_Z, 8)
                pe.wait_ge(s_silu, (L + 1) * CC)
                for t in range(3):
                    for half in range(2):
                        turn([xbc[:, 4 * half + i, tok(t)] for i in range(4)], TOKN[t])
                for t in range(3):
                    turn([xbc[:, 8 + i, tok(t)] for i in range(2)], TOKN[t])
                pe.wait_ge(s_rotated, (L + 1) * 8)
                for t in range(3):
                    turn([kq[:, i, tok(t)] for i in range(4)], TOKN[t])
                pe.wait_ge(s_dtv, (L + 1) * 4)
                pe.wait_ge(s_tout, L * 19 + nt - 1)
                b = 6 + nt % 2
                for t in range(3):
                    for i, src in enumerate((dt_row, acum_row)):
                        mm = pe.transpose(psum[0:TOKN[t], b, (3 * i + t) * H:(3 * i + t + 1) * H],
                                          src[0:H, tok(t)], ident[0:H, 0:H])
                mm.then_inc(s_t, 1)
                nt += 1
                project(Q_G, 8)
                pe.wait_ge(s_evac, (L + 1) * 45)
                pe.wait_ge(s_tout, (L + 1) * 19)

                nb = 0
                for t in range(3):
                    n = TOKN[t]
                    hb, banks = heads_of(t)
                    for g in range(G):
                        mm = pe.matmul(psum[0:n, 4, g * P:g * P + n], xbc[:, 8 + g, tok(t)], xbc[:, 10 + g, tok(t)],
                                       start=True, stop=True)
                    mm.then_inc(s_cb, 1)
                    for i in range(banks):
                        pe.wait_ge(s_rows, L * 10 + nb + 1)
                        pe.matmul(psum[:, 5, 0:BANK], ones[0:H, :], rows[0:H, :], start=True, stop=True)\
                            .then_inc(s_bc, 1)
                        pe.wait_ge(s_lm, L * 10 + nb + 1)
                        nb += 1
                        for hh in range(hb):
                            hd = i * hb + hh
                            c = hd // 2 if t == 2 else (hd // 2) % 2
                            o = psum[(hd % 2) * HD:(hd % 2) * HD + HD, 6, c * n:c * n + n]
                            first = hd < 2 if t == 2 else True
                            mm = pe.matmul(o, x_tok[0:n, t, hd * HD:(hd + 1) * HD],
                                           decays[0:n, 0, hh * n:(hh + 1) * n],
                                           start=first, stop=(t == 0), skip_group_check=True)
                            if t == 1:
                                mm = pe.matmul(o, states_out[:, 0, hd * HD:(hd + 1) * HD],
                                               decays[:, 1, hh * n:(hh + 1) * n],
                                               start=False, stop=True, skip_group_check=True)
                        mm.then_inc(s_y, 1)
                        if t < 2:
                            pe.wait_ge(s_yout, L * 8 + t * 4 + i + 1)
                    pe.wait_ge(s_xdec, L * 3 + t + 1)
                    if t < 2:
                        for g in range(G):
                            mm = pe.matmul(psum[:, g, 0:BANK], b_tok[0:n, t, g * N:(g + 1) * N],
                                           x_tok[0:n, t, g * BANK:(g + 1) * BANK], start=True, stop=True)
                        mm.then_inc(s_cs, 1)
                        pe.wait_ge(s_csout, L * 2 + t + 1)

                for t in range(3):
                    n = TOKN[t]
                    if t > 0:
                        pe.wait_ge(s_oout, L * 2 + t)
                    for r in range(RH):
                        mm = pe.matmul(psum[0:n, 4, r * n:(r + 1) * n], kq[:, r, tok(t)], kq[:, RH + r, tok(t)],
                                       start=True, stop=True)
                    mm.then_inc(s_score, 1)
                    pe.wait_ge(s_decayed, L * 3 + t + 1)
                    if t < 2:
                        for r in range(RH):
                            for e in range(2):
                                o = psum[:, 2 + r // 2, (r % 2) * 2 * P + e * P:(r % 2) * 2 * P + (e + 1) * P]
                                mm = pe.matmul(o, v_tok[:, t, r * DV + e * P:r * DV + (e + 1) * P],
                                               decays[:, 0, r * P:(r + 1) * P], start=True, stop=(t == 0),
                                               skip_group_check=True)
                                if t == 1:
                                    mm = pe.matmul(o, states_out[:, 0, 1024 + r * DV + e * P:1024 + r * DV + (e + 1) * P],
                                                   decays[:, 1, r * P:(r + 1) * P], start=False, stop=True,
                                                   skip_group_check=True)
                        mm.then_inc(s_o, 1)
                        for r in range(RH):
                            mm = pe.matmul(psum[:, r // 2, (r % 2) * DV:(r % 2 + 1) * DV],
                                           k_tok[:, t, r * DK:(r + 1) * DK], v_tok[:, t, r * DV:(r + 1) * DV],
                                           start=True, stop=True)
                        mm.then_inc(s_kv, 1)
                        pe.wait_ge(s_kvout, L * 2 + t + 1)
                    else:
                        for r in range(RH):
                            for e in range(2):
                                c = 2 * r + e
                                pe.matmul(psum[:, 7, c * NS:(c + 1) * NS],
                                          v_tok[0:n, t, r * DV + e * P:r * DV + (e + 1) * P],
                                          decays[0:n, 0, r * n:(r + 1) * n], start=(c == 0), stop=False,
                                          skip_group_check=True)
                for b in range(DB):
                    w = quad(pe, L, Q_STATE + b // 2)
                    ws = w[:, (b % 2) * 2048:(b % 2 + 1) * 2048]
                    for hd in range(H):
                        c = hd // 2
                        pe.matmul(psum[(hd % 2) * HD:(hd % 2) * HD + HD, 6, c * NS + b * DS:c * NS + (b + 1) * DS],
                                  ws[:, hd * HD:(hd + 1) * HD], c_dec_s[:, hd, b * DS:(b + 1) * DS],
                                  start=False, stop=(b == DB - 1), skip_group_check=True)
                    for r in range(RH):
                        for e in range(2):
                            c = 2 * r + e
                            mm = pe.matmul(psum[:, 7, c * NS + b * DS:c * NS + (b + 1) * DS],
                                           ws[:, 1024 + r * DV + e * P:1024 + r * DV + (e + 1) * P],
                                           q_dec_s[:, r, b * DS:(b + 1) * DS],
                                           start=False, stop=(b == DB - 1), skip_group_check=True)
                    pe.wait_ge(s_own, L * DB + b + 1)
                    if b > 0:
                        pe.wait_ge(s_newst, L * DB + b)
                    for g in range(G):
                        pe.matmul(psum[:, g, 0:BANK], b_own[0:NS, g * N:(g + 1) * N],
                                  x_tok[0:NS, 2, g * BANK:(g + 1) * BANK], start=True, stop=True)
                    for r in range(RH):
                        mm = pe.matmul(psum[:, 2 + r // 2, (r % 2) * DV:(r % 2 + 1) * DV],
                                       k_own[0:NS, r * DK:(r + 1) * DK], v_tok[0:NS, 2, r * DV:(r + 1) * DV],
                                       start=True, stop=True)
                    mm.then_inc(s_batch, 1)

                pe.wait_ge(s_sq6, L * 2 + 1)
                for j in range(KD):
                    mm = pe.matmul(psum[:, j // 4, 0:T], ones, h[:, j, :], start=(j % 4 == 0), stop=(j % 4 == 3))
                mm.then_inc(s_sum6, 1)
                pe.wait_ge(s_sq6, L * 2 + 2)
                for j in range(KD):
                    mm = pe.matmul(psum[:, 2 + j // 2, 0:T], ones, h[:, j, :], start=(j % 2 == 0), stop=(j % 2 == 1))
                mm.then_inc(s_sum6, 1)
                pe.wait_ge(s_mix, L + 1)
                for j in range(KD):
                    w = quad(pe, L, Q_OUT + j // 2)
                    if j >= 4:
                        pe.wait_ge(s_xadd, L * 16 + j - 3)
                    for i in range(2 * KD):
                        a = (j % 2) * 2 * SLAB + i * P
                        src = xbc[:, i, :] if i < KD else kq[:, i - KD, :]
                        mm = pe.matmul(psum[:, j % 4, 0:T], w[:, a:a + P], src, start=(i == 0), stop=(i == 15))
                    mm.then_inc(s_wout, 1)
                    if j % 2 == 1:
                        pe.drain().then_inc(freed[(Q_OUT + j // 2) % RING], 1)

            def attention(L):
                pe.wait_ge(s_mem, 16 * (L + 1))
                for c in range(16):
                    w = quad(pe, L, Q_MK + c // 4)
                    if c >= 2:
                        pe.wait_ge(s_mkvout, L * 16 + c - 1)
                    for j in range(KD):
                        a = (c % 4) * SLAB + j * P
                        mm = pe.matmul(psum[:, 4 + c % 2, 0:M], w[:, a:a + P], mem[:, j, :],
                                       start=(j == 0), stop=(j == KD - 1))
                    mm.then_inc(s_mkv, 1)
                    if c % 4 == 3:
                        pe.drain().then_inc(freed[(Q_MK + c // 4) % RING], 1)
                pe.wait_ge(s_mkvout, (L + 1) * 16)
                for mc in range(2):
                    for half in range(2):
                        transposes([(psum[:, 4 + half, i * P:(i + 1) * P], vt_mem[:, 4 * half + i, mc * P:(mc + 1) * P])
                                    for i in range(4)]).then_inc(s_vt, 1)
                    pe.wait_ge(s_vtout, L * 4 + 2 * mc + 2)
                sums(L, 1)
                pe.wait_ge(s_h, L * NNORM + 2)
                for c in range(KD):
                    w = quad(pe, L, Q_MQ + c // 4)
                    if c >= 4:
                        pe.wait_ge(s_qout, L * KD + c - 3)
                    for j in range(KD):
                        a = (c % 4) * SLAB + j * P
                        mm = pe.matmul(psum[:, c % 4, 0:T], w[:, a:a + P], h[:, j, :],
                                       start=(j == 0), stop=(j == KD - 1))
                    mm.then_inc(s_q, 1)
                    if c % 4 == 3:
                        pe.drain().then_inc(freed[(Q_MQ + c // 4) % RING], 1)
                pe.wait_ge(s_qout, (L + 1) * KD)
                for t in range(2):
                    for r in range(XH):
                        for c in range(2):
                            mm = pe.matmul(psum[:, 2 * t + r // 2, (r % 2) * M:(r % 2 + 1) * M],
                                           q_p[:, 2 * r + c, tok(t)], k_mem[:, 2 * r + c, :],
                                           start=(c == 0), stop=(c == 1))
                    mm.then_inc(s_xs, 1)
                for b in range(DB):
                    w = quad(pe, L, Q_KC + b // 2)
                    for r in range(XH):
                        for c in range(2):
                            a = (b % 2) * 2048 + (2 * r + c) * M
                            mm = pe.matmul(psum[0:NS, 4 + r // 2, (r % 2) * M:(r % 2 + 1) * M],
                                           q_own[:, 2 * r + c, b, :], w[:, a:a + M],
                                           start=(b == 0 and c == 0 and r % 2 == 0), stop=(b == DB - 1),
                                           skip_group_check=True)
                    if b == DB - 1:
                        mm.then_inc(s_xs, 1)
                    if b % 2 == 1:
                        pe.drain().then_inc(freed[(Q_KC + b // 2) % RING], 1)
                np_ = 0
                for t in range(3):
                    pe.wait_ge(s_prob, L * 3 + t + 1)
                    for half in range(2):
                        if np_ >= 2:
                            pe.wait_ge(s_ptout, L * 6 + np_ - 1)
                        n = TOKN[t]
                        for i in range(4):
                            r, c = 2 * half + i // 2, i % 2
                            mm = pe.transpose(psum[:, 6 + np_ % 2, i * P:i * P + n],
                                              prob[0:n, t, r, c * P:(c + 1) * P], ident[0:n, 0:n])
                        mm.then_inc(s_pt, 1)
                        np_ += 1
                pe.wait_ge(s_ptout, (L + 1) * 6)
                for j in range(KD):
                    if j >= 4:
                        pe.wait_ge(s_xoout, L * 9 + j - 3)
                    for c in range(2):
                        mm = pe.matmul(psum[:, j % 4, 0:SEQ], v_mem[:, c, j * P:(j + 1) * P],
                                       prob_t[:, j // 2, c, 0:SEQ], start=(c == 0), stop=(c == 1))
                    mm.then_inc(s_xo, 1)
                for b in range(DB):
                    w = quad(pe, L, Q_VC + b // 2)
                    for j in range(KD):
                        for c in range(2):
                            a = (b % 2) * 2048 + c * D + j * P
                            mm = pe.matmul(psum[:, 4, j * NS + b * DS:j * NS + (b + 1) * DS], w[:, a:a + P],
                                           prob_t[:, j // 2, c, SEQ + b * DS:SEQ + (b + 1) * DS],
                                           start=(c == 0), stop=(c == 1), skip_group_check=True)
                    if b == DB - 1:
                        mm.then_inc(s_xo, 1)
                    if b % 2 == 1:
                        pe.drain().then_inc(freed[(Q_VC + b // 2) % RING], 1)
                pe.wait_ge(s_xoout, (L + 1) * 9)
                for c in range(KD):
                    w = quad(pe, L, Q_MO + c // 4)
                    if c >= 4:
                        pe.wait_ge(s_xadd, L * 16 + KD + c - 3)
                    for j in range(KD):
                        a = (c % 4) * SLAB + j * P
                        mm = pe.matmul(psum[:, c % 4, 0:T], w[:, a:a + P], h[:, j, :],
                                       start=(j == 0), stop=(j == KD - 1))
                    mm.then_inc(s_wout, 1)
                    if c % 4 == 3:
                        pe.drain().then_inc(freed[(Q_MO + c // 4) % RING], 1)

            def moe(L):
                sums(L, 2)
                pe.wait_ge(s_h, L * NNORM + 3)
                for t in range(3):
                    for j in range(KD):
                        a = PAT["route_w"] + j * (EG + E)
                        mm = pe.matmul(psum[0:TOKN[t], 6, t * 32:t * 32 + EG + E], h[:, j, tok(t)],
                                       par[:, L, a:a + EG + E], start=(j == 0), stop=(j == KD - 1))
                mm.then_inc(s_route, 1)
                for i in range(6):
                    t, half = i // 2, i % 2
                    if i >= 2:
                        pe.wait_ge(s_htout, L * 6 + i - 1)
                    transposes([(psum[0:TOKN[t], i % 2, c * P:(c + 1) * P], h[:, 4 * half + c, tok(t)])
                                for c in range(4)]).then_inc(s_ht, 1)
                pe.wait_ge(s_rv, 2 * L + 1)
                for t in range(3):
                    n = TOKN[t]
                    o = psum[0:n, 5, t * 32:t * 32 + EG]
                    for tt in range(t):
                        pe.matmul(o, ones[:, 0:n], gsel[:, tt, :], start=(tt == 0), stop=False)
                    pe.matmul(o, k_("causal", n, n), gsel[0:n, t, :], start=(t == 0), stop=True)
                for t in range(3):
                    n = TOKN[t]
                    mm = pe.matmul(psum[:, 5, 96:96 + EG], ones[0:n, :], gsel[0:n, t, :], start=(t == 0), stop=(t == 2))
                mm.then_inc(s_cnt, 1)
                pe.wait_ge(s_htout, (L + 1) * 6)
                pe.wait_ge(s_chosen, L * 2 + 1)
                for j in range(KD):
                    if j >= 4:
                        pe.wait_ge(s_packout, L * KD + j - 3)
                    for t in range(3):
                        n = TOKN[t]
                        mm = pe.matmul(psum[:, j % 4, :], h_tok[0:n, t, j * P:(j + 1) * P], chosen[0:n, t, :, :],
                                       start=(t == 0), stop=(t == 2))
                    mm.then_inc(s_pack, 1)
                for g in range(EG):
                    if g >= 2:
                        pe.wait_ge(s_ctout, L * EG + g - 1)
                    for t in range(3):
                        n = TOKN[t]
                        mm = pe.transpose(psum[:, 6 + g % 2, TOK0[t]:TOK0[t] + n], chosen[0:n, t, g, :],
                                          ident[0:n, 0:n])
                    mm.then_inc(s_ct, 1)
                pe.wait_ge(s_chosen, L * 2 + 2)
                for e in range(EPG):
                    if e >= 2:
                        pe.wait_ge(s_gsout, L * EPG + e - 1)
                    for t in range(3):
                        n = TOKN[t]
                        mm = pe.matmul(psum[:, 4 + e % 2, :], gate_cols[0:n, t, e, :], chosen[0:n, t, :, :],
                                       start=(t == 0), stop=(t == 2))
                    mm.then_inc(s_gs, 1)
                pe.wait_ge(s_packout, (L + 1) * KD)
                pe.wait_ge(s_gsout, (L + 1) * EPG)
                pe.wait_ge(s_ctout, (L + 1) * EG)
                with pe.Fori(0, EG) as g:
                    pe.wait_ge(s_group, L * EG + g + 1)
                    for u in range(EPG):
                        seen = (L * E + g * EPG + u) * 2
                        rev = L * REVS + Q_MOE // RING + g * 3
                        for q in range(2):
                            s, dr = (3 * u + q) % RING, (3 * u + q) // RING
                            pe.wait_ge(loaded[s], 16 * (rev + dr + 1))
                            w = ring[:, s, :]
                            for up in range(2):
                                for i in range(2):
                                    for j in range(KD):
                                        a = (2 * i + up) * SLAB + j * P
                                        mm = pe.matmul(psum[:, 2 * up + q, i * CAP:(i + 1) * CAP], w[:, a:a + P],
                                                       h_group[:, j, :], start=(j == 0), stop=(j == KD - 1))
                                mm.then_inc(s_up if up else s_gate, 1)
                            pe.drain().then_inc(freed[s], 1)
                        s, dr = (3 * u + 2) % RING, (3 * u + 2) // RING
                        pe.wait_ge(loaded[s], 16 * (rev + dr + 1))
                        w = ring[:, s, :]
                        for f in range(FC):
                            if f % 2 == 0:
                                pe.wait_ge(s_hid, seen + f // 2 + 1)
                            for half in range(2):
                                a = f * D + half * BANK
                                mm = pe.matmul(psum[:, 4 + half, :], hidden[:, f, :], w[:, a:a + BANK],
                                               start=(u == 0 and f == 0), stop=(u == EPG - 1 and f == FC - 1))
                        if u == EPG - 1:
                            mm.then_inc(s_down, 1)
                        pe.drain().then_inc(freed[s], 1)
                    pe.wait_ge(s_yg, L * EG + g + 1)
                    for j in range(KD):
                        if j >= 2:
                            pe.wait_ge(s_added, (L * EG + g) * KD + j - 1)
                        pe.matmul(psum[:, 6 + j % 2, 0:T], y_group[:, j * P:(j + 1) * P], chosen_group,
                                  start=True, stop=True).then_inc(s_spread, 1)
                pe.wait_ge(s_spilt, L + 1)
                with pe.If(pe.value_load(spilt[0:1, L:L + 1], min_val=0, max_val=1) > 0):
                    dense(L)
                with pe.Else():
                    for sm, n in ((d_gt, 1), (d_gb, E), (d_gate, E * FC), (d_up, E * FC), (d_down, E * KD)):
                        pe.sem_inc(sm, n)

            def dense(L):
                pe.wait_ge(d_start, L * (E + 1) + 1)
                for t in range(3):
                    mm = pe.transpose(psum[0:E, 5, TOK0[t]:TOK0[t] + TOKN[t]],
                                      spilt_gates[0:TOKN[t], t, :, :], ident[0:TOKN[t], 0:TOKN[t]])
                mm.then_inc(d_gt, 1)
                for e in range(E):
                    pe.wait_ge(d_orow, L * E + e + 1)
                    if e >= 2:
                        pe.wait_ge(d_gbout, L * E + e - 1)
                    pe.matmul(psum[:, 6 + e % 2, 0:T], ones[0:E, :], one_row[0:E, e % 2, :],
                              start=True, stop=True).then_inc(d_gb, 1)
                pe.wait_ge(d_gbout, (L + 1) * E)
                with pe.Fori(0, E) as e:
                    seen = (L * E + e) * FC
                    pe.wait_ge(d_loaded, (L * E + e + 1) * 16)
                    for f in range(FC):
                        if f >= 2:
                            pe.wait_ge(d_sg, seen + f - 1)
                        for j in range(KD):
                            a = (2 * (f % 2)) * SLAB + j * P
                            mm = pe.matmul(psum[:, f % 2, 0:T], all_w[:, f // 2, a:a + P], h[:, j, :],
                                           start=(j == 0), stop=(j == KD - 1))
                        mm.then_inc(d_gate, 1)
                        if f >= 2:
                            pe.wait_ge(d_hid, seen + f - 1)
                        for j in range(KD):
                            a = (2 * (f % 2) + 1) * SLAB + j * P
                            mm = pe.matmul(psum[:, 2 + f % 2, 0:T], all_w[:, f // 2, a:a + P], h[:, j, :],
                                           start=(j == 0), stop=(j == KD - 1))
                        mm.then_inc(d_up, 1)
                    pe.wait_ge(d_hid, seen + FC)
                    for j in range(KD):
                        if j >= 4:
                            pe.wait_ge(d_added, seen * 2 + j - 3)
                        for f in range(FC):
                            mm = pe.matmul(psum[:, 4 + j % 4, 0:T], all_w[:, 2, f * D + j * P:f * D + (j + 1) * P],
                                           all_hidden[:, f, :], start=(f == 0), stop=(f == FC - 1))
                        mm.then_inc(d_down, 1)

            pe.wait_ge(s_const, 48)
            for L in range(DEPTH):
                mixer(L)
                attention(L)
                moe(L)
            sums(DEPTH, 0)

        @block.scalar
        def _(act):
            def square(L, k):
                if L or k:
                    if k == 0:
                        act.wait_ge(d_end, L)
                    else:
                        act.wait_ge(s_xadd, L * 16 + 8 * k)
                act.activation(h[:], x[:], ACT.Square).then_inc(s_sq, 1)
                act.wait_ge(s_sum, L * NNORM + k + 1)
                act.activation(rstd[:], psum[:, 7, 0:T], ACT.Ln, scale=1.0 / D, bias=k_("eps", 1))
                act.drain()
                act.activation(rstd[:], rstd[:], ACT.Exp, scale=-0.5).then_inc(s_rstd, 1)

            def mixer(L):
                square(L, 0)
                n_evac = 0
                nt = 0

                def evac(dst, func=ACT.Copy, rows_=P):
                    nonlocal n_evac
                    act.wait_ge(s_proj, L * 45 + n_evac + 1)
                    act.activation(dst, psum[0:rows_, n_evac % 4, 0:T], func).then_inc(s_evac, 1)
                    n_evac += 1

                def turned(dst, n, width):
                    nonlocal nt
                    act.wait_ge(s_t, L * 19 + nt + 1)
                    act.activation(dst, psum[0:n, 6 + nt % 2, 0:width], ACT.Copy).then_inc(s_tout, 1)
                    nt += 1

                for c in range(8):
                    evac(zv[:, c, :])
                for c in range(8):
                    evac(kq[:, c, :])
                for c in range(CC):
                    act.wait_ge(s_proj, L * 45 + n_evac + 1)
                    b = n_evac % 4
                    act.activation(raw[:, c, CW - 1:XS0], psum[:, b, 0:SEQ], ACT.Copy)
                    act.activation(raw[:, c, XS0:XW].rearrange("p (b j) -> p b j", b=DB)[:, :, CW - 1:],
                                   psum[:, b, SEQ:T].rearrange("p (b j) -> p b j", b=DB), ACT.Copy)\
                        .then_inc(s_evac, 1)
                    n_evac += 1
                evac(dt_tmp[0:H, 0, :], rows_=H)
                act.wait_ge(s_dtv, L * 4 + 1)
                act.activation(dt_tmp[0:H, 2, :], dt_tmp[0:H, 1, :], ACT.Exp, scale=-1.0).then_inc(s_dta, 1)
                act.wait_ge(s_dtv, L * 4 + 2)
                act.activation(dt_tmp[0:H, 4, :], dt_tmp[0:H, 3, :], ACT.Ln)
                act.activation(keep[0:H, 0:1], par[0:H, L, PAT["a_log"]:PAT["a_log"] + 1], ACT.Exp)
                act.drain().then_inc(s_dta, 1)
                for t in range(3):
                    for half in range(2):
                        turned(v_tok[0:TOKN[t], t, half * BANK:(half + 1) * BANK], TOKN[t], BANK)
                for c in range(8):
                    evac(zv[:, c, :], ACT.Silu)
                    for cc in range(c * 3 // 2, (c + 1) * 3 // 2):
                        act.wait_ge(s_conv, L * CC + cc + 1)
                        a = conv_acc[:, cc % 2, :]
                        act.activation(xbc[:, cc, 0:SEQ], a[:, 0:SEQ], ACT.Silu)
                        act.activation(xbc[:, cc, SEQ:T - DS].rearrange("p (b j) -> p b j", b=DB - 1),
                                       a[:, XS0:XS0 + 77].rearrange("p (b j) -> p b j", b=DB - 1)[:, :, 0:DS],
                                       ACT.Silu)
                        act.activation(xbc[:, cc, T - DS:T], a[:, XS0 + 77:XOUT], ACT.Silu).then_inc(s_silu, 1)
                for t in range(3):
                    for half in range(2):
                        if t == 0 and half == 0:
                            act.wait_ge(s_silu, (L + 1) * CC)
                        turned(x_tok[0:TOKN[t], t, half * BANK:(half + 1) * BANK], TOKN[t], BANK)
                for t in range(3):
                    turned(b_tok[0:TOKN[t], t, :], TOKN[t], G * N)
                for t in range(3):
                    turned(k_tok[0:TOKN[t], t, :], TOKN[t], BANK)
                act.wait_ge(s_t, L * 19 + nt + 1)
                b = 6 + nt % 2
                for i, dst in enumerate((dt_tok, acum_tok)):
                    act.activation(dst[:, 0:2, :], psum[:, b, 3 * i * H:(3 * i + 2) * H]
                                   .rearrange("p (t h) -> p t h", t=2), ACT.Copy)
                    act.activation(dst[0:NS, 2, :], psum[0:NS, b, (3 * i + 2) * H:(3 * i + 3) * H], ACT.Copy)
                act.drain().then_inc(s_tout, 1)
                nt += 1
                act.wait_ge(s_raw_free, L + 1)
                for c in range(8):
                    evac(gate[:, c, :], ACT.Silu)

                nb = 0
                for t in range(3):
                    n = TOKN[t]
                    hb, banks = heads_of(t)
                    for i in range(banks):
                        act.wait_ge(s_diff, L * 10 + nb + 1)
                        if t == 1:
                            act.activation(decays[:, 1, :], psum[:, 5, :], ACT.Exp)
                        if t == 2:
                            act.activation(c_dec_s[:, i * hb:(i + 1) * hb, :],
                                           psum[:, 5, :].rearrange("p (h l) -> p h l", h=hb), ACT.Exp)
                        act.activation(decays[0:n, 0, :], decays[0:n, 0, :], ACT.Exp)
                        act.drain().then_inc(s_exp, 1)
                        nb += 1
                    act.wait_ge(s_dec, L * 3 + t + 1)
                    act.activation(decay_end[0:n, :], decay_end[0:n, :], ACT.Exp)
                    if t == 2:
                        act.activation(last_s[:], last_s[:], ACT.Exp)
                    else:
                        act.activation(keep[:], last[:], ACT.Exp)
                    act.drain().then_inc(s_dece, 1)
                    if t == 0:
                        act.wait_ge(s_cs, L * 2 + 1)
                        act.activation(states_out[:, 0, 0:1024].rearrange("p (a b) -> p a b", a=2),
                                       psum[:, 0:2, :], ACT.Copy).then_inc(s_csout, 1)
                for t in range(3):
                    if t < 2:
                        act.wait_ge(s_o, L * 2 + t + 1)
                        act.activation(kq[:, :, tok(t)].rearrange("p (a b) t -> p a b t", a=2),
                                       psum[:, 2:4, :].rearrange("p a (b t) -> p a b t", b=4), ACT.Copy)\
                            .then_inc(s_oout, 1)
                    if t == 0:
                        act.wait_ge(s_kv, L * 2 + 1)
                        act.activation(states_out[:, 0, 1024:2048].rearrange("p (a b) -> p a b", a=2),
                                       psum[:, 0:2, :], ACT.Copy).then_inc(s_kvout, 1)
                act.wait_ge(s_batch, (L + 1) * DB)
                act.activation(kq[:, :, tok(2)], psum[:, 7, :].rearrange("p (c t) -> p c t", c=KD), ACT.Copy)
                act.wait_ge(s_gated, L + 1)
                act.activation(h[:], xbc[:, 0:KD, :], ACT.Square).then_inc(s_sq6, 1)
                act.wait_ge(s_sum6, L * 2 + 1)
                act.drain()
                act.activation(h[:], kq[:], ACT.Square).then_inc(s_sq6, 1)
                act.activation(rstd6[:, 0:2, :], psum[:, 0:2, 0:T], ACT.Ln, scale=2.0 / D, bias=k_("eps", 1))
                act.wait_ge(s_sum6, L * 2 + 2)
                act.activation(rstd6[:, 2:6, :], psum[:, 2:6, 0:T], ACT.Ln, scale=1.0 / DV, bias=k_("eps", 1))
                act.drain()
                act.activation(rstd6[:], rstd6[:], ACT.Exp, scale=-0.5).then_inc(s_rstd6, 1)

            def attention(L):
                for c in range(16):
                    act.wait_ge(s_mkv, L * 16 + c + 1)
                    dst = k_mem[:, c, :] if c < KD else vt_mem[:, c - KD, :]
                    act.activation(dst, psum[:, 4 + c % 2, 0:M], ACT.Copy).then_inc(s_mkvout, 1)
                for mc in range(2):
                    for half in range(2):
                        act.wait_ge(s_vt, L * 4 + 2 * mc + half + 1)
                        act.activation(v_mem[:, mc, half * BANK:(half + 1) * BANK], psum[:, 4 + half, :], ACT.Copy)\
                            .then_inc(s_vtout, 1)
                square(L, 1)
                act.wait_ge(s_qzero, L + 1)
                for c in range(KD):
                    act.wait_ge(s_q, L * KD + c + 1)
                    act.activation(q_p[:, c, :], psum[:, c % 4, 0:SEQ], ACT.Copy)
                    own = q_own[:, c, :, :].rearrange("p b t -> p (b t)")
                    for b in range(DB):
                        ins = act.activation(own[:, b * (NS + DS):b * (NS + DS) + DS],
                                             psum[:, c % 4, SEQ + b * DS:SEQ + (b + 1) * DS], ACT.Copy)
                    ins.then_inc(s_qout, 1)
                for t in range(3):
                    n = TOKN[t]
                    act.wait_ge(s_xmax, L * 3 + t + 1)
                    for r in range(XH):
                        b = 2 * t + r // 2
                        act.activation(prob[0:n, t, r, :], psum[0:n, b, (r % 2) * M:(r % 2 + 1) * M], ACT.Exp,
                                       bias=xmax[0:n, t, r:r + 1], scale=1.0 / 16, accum_out=xsum[0:n, t, r:r + 1])
                    act.drain().then_inc(s_xexp, 1)
                np_ = 0
                for t in range(3):
                    n = TOKN[t]
                    for half in range(2):
                        act.wait_ge(s_pt, L * 6 + np_ + 1)
                        act.activation(prob_t[:, 2 * half:2 * half + 2, :, tok(t)],
                                       psum[:, 6 + np_ % 2, :].rearrange("p (r c t) -> p r c t", r=2, c=2)[:, :, :, 0:n],
                                       ACT.Copy).then_inc(s_ptout, 1)
                        np_ += 1
                for j in range(KD):
                    act.wait_ge(s_xo, L * 9 + j + 1)
                    act.activation(h[:, j, 0:SEQ], psum[:, j % 4, 0:SEQ], ACT.Copy).then_inc(s_xoout, 1)
                act.wait_ge(s_xo, (L + 1) * 9)
                act.activation(h[:, :, SEQ:T], psum[:, 4, :].rearrange("p (c t) -> p c t", c=KD), ACT.Copy)\
                    .then_inc(s_xoout, 1)

            def moe(L):
                square(L, 2)
                for i in range(6):
                    t, half = i // 2, i % 2
                    act.wait_ge(s_ht, L * 6 + i + 1)
                    act.activation(h_tok[0:TOKN[t], t, half * BANK:(half + 1) * BANK],
                                   psum[0:TOKN[t], i % 2, :], ACT.Copy).then_inc(s_htout, 1)
                act.wait_ge(s_rv, 2 * L + 2)
                act.activation(gtmp, gtmp, ACT.Exp)
                act.activation(mt, mt, ACT.Exp)
                act.drain().then_inc(s_ra, 1)
                for j in range(KD):
                    act.wait_ge(s_pack, L * KD + j + 1)
                    act.activation(h_packed[:, j, :, :], psum[:, j % 4, :].rearrange("p (g c) -> p g c", g=EG),
                                   ACT.Copy).then_inc(s_packout, 1)
                for e in range(EPG):
                    act.wait_ge(s_gs, L * EPG + e + 1)
                    act.activation(gates[:, e, :, :], psum[:, 4 + e % 2, :].rearrange("p (g c) -> p g c", g=EG),
                                   ACT.Copy).then_inc(s_gsout, 1)
                with act.Fori(0, EG) as g:
                    for u in range(EPG):
                        seen = (L * E + g * EPG + u) * 2
                        for q in range(2):
                            act.wait_ge(s_gate, seen + q + 1)
                            act.activation(silu_gate[:, q, :], psum[:, q, 0:2 * CAP], ACT.Silu).then_inc(s_sg, 1)
                    act.wait_ge(s_down, L * EG + g + 1)
                    act.activation(y_group.rearrange("p (a b) -> p a b", a=2), psum[:, 4:6, :], ACT.Copy)\
                        .then_inc(s_yg, 1)
                act.wait_ge(s_spilt, L + 1)
                with act.If(act.value_load(spilt[0:1, L:L + 1], min_val=0, max_val=1) > 0):
                    act.wait_ge(d_gt, L + 1)
                    act.activation(gate_row[0:E, :], psum[0:E, 5, 0:T], ACT.Copy).then_inc(d_grow, 1)
                    for e in range(E):
                        act.wait_ge(d_gb, L * E + e + 1)
                        act.activation(all_gates[:, e, :], psum[:, 6 + e % 2, 0:T], ACT.Copy).then_inc(d_gbout, 1)
                    with act.Fori(0, E) as e:
                        for f in range(FC):
                            act.wait_ge(d_gate, (L * E + e) * FC + f + 1)
                            if f >= 2:
                                act.wait_ge(d_hid, (L * E + e) * FC + f - 1)
                            act.activation(all_silu[:, f % 2, :], psum[:, f % 2, 0:T], ACT.Silu).then_inc(d_sg, 1)
                with act.Else():
                    for sm, n in ((d_grow, 1), (d_gbout, E), (d_sg, E * FC)):
                        act.sem_inc(sm, n)

            act.wait_ge(s_const, 48)
            for L in range(DEPTH):
                mixer(L)
                attention(L)
                moe(L)
            square(DEPTH, 0)

        @block.vector
        def _(dve):
            def normed(L, k, gain, dst=h):
                dve.wait_ge(s_rstd, L * NNORM + k + 1)
                for j in range(KD):
                    a = PAT[gain] + j
                    ins = dve.scalar_tensor_tensor(out=dst[:, j, :], in0=x[:, j, :], scalar=par[:, min(L, 1), a:a + 1],
                                                   in1=rstd[:], op0=ALU.mult, op1=ALU.mult)
                ins.then_inc(s_h, 1)

            def mixer(L):
                normed(L, 0, "norm_mix")
                w = quad(dve, L, Q_DT)
                dve.memset(raw[:, :, 0:CW - 1], 0.0)
                for c in range(CC):
                    a = KD * H + c * DB * (CW - 1)
                    dve.tensor_copy(raw[:, c, XS0:XW].rearrange("p (b j) -> p b j", b=DB)[:, :, 0:CW - 1],
                                    w[:, a:a + DB * (CW - 1)].rearrange("p (b j) -> p b j", b=DB))
                dve.wait_ge(s_proj, L * 45 + 29)
                dve.drain().then_inc(freed[Q_DT % RING], 1)
                for j in range(2 * RH):
                    dve.wait_ge(s_rot, L * 8 + j + 1)
                    tmp = rot_tmp[:, j % 2, :]
                    dve.tensor_tensor(tmp, psum[:, 4 + j % 2, 0:T], k_("sin", T), ALU.mult)
                    dve.tensor_tensor(kq[:, j, :], kq[:, j, :], k_("cos", T), ALU.mult)
                    dve.drain()
                    dve.tensor_tensor(kq[:, j, :], kq[:, j, :], tmp, ALU.add).then_inc(s_rotated, 1)
                d = [dt_tmp[0:H, i, :] for i in range(6)]
                dve.wait_ge(s_evac, L * 45 + 29)
                dve.tensor_scalar(d[0], d[0], par[0:H, L, PAT["dt_bias"]:PAT["dt_bias"] + 1], None, ALU.add)
                dve.drain()
                dve.scalar_tensor_tensor(out=d[1], in0=d[0], scalar=-1.0, in1=d[0], op0=ALU.mult, op1=ALU.max)
                dve.drain().then_inc(s_dtv, 1)
                dve.wait_ge(s_dta, L * 2 + 1)
                dve.tensor_scalar(d[3], d[2], 1.0, None, ALU.add)
                dve.drain().then_inc(s_dtv, 1)
                dve.wait_ge(s_dta, L * 2 + 2)
                dve.reciprocal(d[5], d[3])
                dve.tensor_scalar(d[3], d[3], -1.0, 1e-30, ALU.add, ALU.max)
                dve.drain()
                dve.reciprocal(d[3], d[3])
                dve.tensor_tensor(d[4], d[4], d[2], ALU.mult)
                dve.tensor_tensor(d[5], d[5], d[2], ALU.mult)
                dve.drain()
                dve.tensor_tensor(d[4], d[4], d[3], ALU.mult)
                dve.drain()
                dve.tensor_tensor(d[4], d[4], d[5], ALU.max)
                dve.drain()
                dve.scalar_tensor_tensor(out=dt_row[0:H, :], in0=d[0], scalar=0.0, in1=d[4], op0=ALU.max, op1=ALU.add)
                dve.drain()
                dve.tensor_scalar(d[1], dt_row[0:H, :], keep[0:H, 0:1], -1.0, ALU.mult, ALU.mult)
                dve.drain().then_inc(s_dtv, 1)
                dve.tensor_tensor_scan(acum_row[0:H, :], k_("restart", T, H), d[1], 0.0, ALU.mult, ALU.add)\
                    .then_inc(s_dtv, 1)
                for c in range(CC):
                    dve.wait_ge(s_evac, L * 45 + 16 + c + 1)
                    if c >= 2:
                        dve.wait_ge(s_silu, L * CC + c - 1)
                    a = conv_acc[:, c % 2, :]
                    wa, ba = PAT["conv_w"] + c * CW, PAT["conv_b"] + c
                    dve.tensor_scalar(a, raw[:, c, 0:XOUT], par[:, L, wa:wa + 1], par[:, L, ba:ba + 1],
                                      ALU.mult, ALU.add)
                    for j in range(1, CW):
                        dve.drain()
                        ins = dve.scalar_tensor_tensor(out=a, in0=raw[:, c, j:j + XOUT],
                                                       scalar=par[:, L, wa + j:wa + j + 1], in1=a,
                                                       op0=ALU.mult, op1=ALU.add)
                    ins.then_inc(s_conv, 1)
                dve.tensor_copy(conv_tail[:, :, 0:CW - 1], raw[:, :, XS0 - (CW - 1):XS0])
                for b in range(DB):
                    e = XS0 + (b + 1) * (CW - 1 + DS)
                    dve.tensor_copy(conv_tail[:, :, (b + 1) * (CW - 1):(b + 2) * (CW - 1)],
                                    raw[:, :, e - (CW - 1):e])
                dve.drain().then_inc(s_raw_free, 1)

                nb = 0
                dve.wait_ge(s_tout, (L + 1) * 19)
                dve.wait_ge(s_evac, (L + 1) * 45)
                for t in range(3):
                    n = TOKN[t]
                    hb, banks = heads_of(t)
                    xt = x_tok[0:n, t, :].rearrange("p (h d) -> p h d", h=H)
                    dve.tensor_tensor(xt, xt, dt_tok[0:n, t, :].unsqueeze(2).broadcast_to([n, H, HD]), ALU.mult)
                    dve.wait_ge(s_cb, L * 3 + t + 1)
                    mask = k_("causal", P) if t < 2 else k_("causal_s", NS, NS)
                    dve.tensor_tensor(cbm[0:n, :, 0:n],
                                      psum[0:n, 4, 0:G * P].rearrange("p (g l) -> p g l", g=G)[:, :, 0:n],
                                      mask.unsqueeze(1).broadcast_to([n, G, n]), ALU.mult)
                    for i in range(banks):
                        h0 = i * hb
                        if nb > 0:
                            dve.wait_ge(s_bc, L * 10 + nb)
                        dve.tensor_tensor(rows[0:H, :].rearrange("p (h l) -> p h l", h=hb),
                                          acum_row[0:H, tok(t)].unsqueeze(1).broadcast_to([H, hb, n]),
                                          ident[0:H, h0:h0 + hb].unsqueeze(2).broadcast_to([H, hb, n]), ALU.mult)\
                            .then_inc(s_rows, 1)
                        dve.wait_ge(s_bc, L * 10 + nb + 1)
                        bc = psum[:, 5, :].rearrange("p (h l) -> p h l", h=hb)
                        if nb > 0:
                            dve.wait_ge(s_y, L * 10 + nb)
                        e = decays[0:n, 0, :].rearrange("p (h l) -> p h l", h=hb)
                        for hh in range(hb):
                            dve.tensor_scalar(e[:, hh, :], bc[0:n, hh, :], acum_tok[0:n, t, h0 + hh:h0 + hh + 1],
                                              0.0, ALU.subtract, ALU.min)
                        if t < 2:
                            dve.tensor_copy(last[:, h0:h0 + hb], bc[:, :, n - 1])
                        else:
                            dve.tensor_copy(last_s[:, h0:h0 + hb, :],
                                            bc.rearrange("p h (b j) -> p h b j", b=DB)[:, :, :, DS - 1])
                        dve.drain().then_inc(s_diff, 1)
                        dve.wait_ge(s_exp, L * 10 + nb + 1)
                        g0 = h0 * G // H
                        dve.tensor_tensor(e, e, cbm[0:n, g0, 0:n].unsqueeze(1).broadcast_to([n, hb, n]), ALU.mult)
                        if t > 0:
                            cd = decays[:, 1, :].rearrange("p (h l) -> p h l", h=hb) if t == 1 \
                                else c_dec_s[:, h0:h0 + hb, :]
                            dve.tensor_tensor(cd, cd, xbc[:, 10 + g0, tok(t)].unsqueeze(1)
                                              .broadcast_to([P, hb, n]), ALU.mult)
                        dve.drain().then_inc(s_lm, 1)
                        if t < 2:
                            dve.wait_ge(s_y, L * 10 + nb + 1)
                            for c in range(2):
                                ch = 2 * i + c
                                a = PAT["d_skip"] + ch
                                ins = dve.scalar_tensor_tensor(out=xbc[:, ch, tok(t)], in0=xbc[:, ch, tok(t)],
                                                               scalar=par[:, L, a:a + 1],
                                                               in1=psum[:, 6, c * P:(c + 1) * P],
                                                               op0=ALU.mult, op1=ALU.add)
                            ins.then_inc(s_yout, 1)
                        nb += 1
                    if t < 2:
                        dve.tensor_tensor(decay_end[0:n, :], last[0:n, :], acum_tok[0:n, t, :], ALU.subtract)
                    else:
                        dve.tensor_tensor(last_own[0:n], last_s[0:n],
                                          k_("own", DB, NS).unsqueeze(1).broadcast_to([n, H, DB]), ALU.mult)
                        dve.drain()
                        dve.tensor_reduce(decay_end[0:n, :], last_own[0:n], AX.X, ALU.add)
                        dve.drain()
                        dve.tensor_tensor(decay_end[0:n, :], decay_end[0:n, :], acum_tok[0:n, t, :], ALU.subtract)
                    dve.drain().then_inc(s_dec, 1)
                    dve.wait_ge(s_dece, L * 3 + t + 1)
                    if t == 2:
                        dve.wait_ge(s_y, L * 10 + nb)
                    dve.tensor_tensor(xt, xt, decay_end[0:n, :].unsqueeze(2).broadcast_to([n, H, HD]), ALU.mult)\
                        .then_inc(s_xdec, 1)
                    if t == 1:
                        dve.wait_ge(s_cs, L * 2 + 2)
                        st = states_out[:, 0, 0:1024].rearrange("p (h d) -> p h d", h=H)
                        dve.tensor_tensor(st, st, keep[:].unsqueeze(2).broadcast_to([P, H, HD]), ALU.mult)
                        dve.drain()
                        st = states_out[:, 0, 0:1024].rearrange("p (a b) -> p a b", a=2)
                        dve.tensor_tensor(st, st, psum[:, 0:2, :], ALU.add).then_inc(s_csout, 1)

                for t in range(3):
                    n = TOKN[t]
                    dve.wait_ge(s_score, L * 3 + t + 1)
                    sfx = "" if t < 2 else "_s"
                    e = decays[0:n, 0, 0:RH * n]
                    dve.tensor_tensor(e, psum[0:n, 4, 0:RH * n], k_("decay" + sfx, RH * n, n), ALU.mult)
                    if t > 0:
                        qd = decays[:, 1, :].rearrange("p (h l) -> p h l", h=RH) if t == 1 else q_dec_s
                        dve.tensor_tensor(qd, kq[:, RH:2 * RH, tok(t)],
                                          k_("qdecay" + sfx, RH * n).rearrange("p (h l) -> p h l", h=RH), ALU.mult)
                    kt = k_tok[0:n, t, :].rearrange("p (h d) -> p h d", h=RH)
                    dve.tensor_tensor(kt, kt, k_("kend" + sfx, RH, n).unsqueeze(2).broadcast_to([n, RH, DK]), ALU.mult)
                    dve.drain().then_inc(s_decayed, 1)
                    if t == 1:
                        dve.wait_ge(s_kv, L * 2 + 2)
                        for r in range(RH):
                            st = states_out[:, 0, 1024 + r * DV:1024 + (r + 1) * DV]
                            dve.scalar_tensor_tensor(out=st, in0=st, scalar=float(gam[r] ** P),
                                                     in1=psum[:, r // 2, (r % 2) * DV:(r % 2 + 1) * DV],
                                                     op0=ALU.mult, op1=ALU.add)
                        dve.drain().then_inc(s_kvout, 1)

                for b in range(DB):
                    if b > 0:
                        dve.wait_ge(s_batch, L * DB + b)
                    own = k_("own", 1, NS, b)
                    dve.tensor_scalar(b_own[0:NS, :], b_tok[0:NS, 2, :], own, None, ALU.mult)
                    dve.tensor_scalar(k_own[0:NS, :], k_tok[0:NS, 2, :], own, None, ALU.mult)
                    dve.drain().then_inc(s_own, 1)
                    w = quad(dve, L, Q_STATE + b // 2)
                    ws = w[:, (b % 2) * 2048:(b % 2 + 1) * 2048]
                    slot = (b + 1) % 2
                    if b >= 1:
                        dve.wait_ge(s_store[slot], 16 * (L * (5 - slot) + (b + 1) // 2))
                    so = states_out[:, slot, :]
                    dve.tensor_tensor(so[:, 0:1024].rearrange("p (h d) -> p h d", h=H),
                                      ws[:, 0:1024].rearrange("p (h d) -> p h d", h=H),
                                      last_s[:, :, b].unsqueeze(2).broadcast_to([P, H, HD]), ALU.mult)
                    dve.wait_ge(s_batch, L * DB + b + 1)
                    for r in range(RH):
                        dve.scalar_tensor_tensor(out=so[:, 1024 + r * DV:1024 + (r + 1) * DV],
                                                 in0=ws[:, 1024 + r * DV:1024 + (r + 1) * DV],
                                                 scalar=float(gam[r] ** DS),
                                                 in1=psum[:, 2 + r // 2, (r % 2) * DV:(r % 2 + 1) * DV],
                                                 op0=ALU.mult, op1=ALU.add)
                    dve.drain()
                    so2 = so[:, 0:1024].rearrange("p (a b) -> p a b", a=2)
                    dve.tensor_tensor(so2, so2, psum[:, 0:2, :], ALU.add)
                    dve.drain().then_inc(s_newst, 1)
                    if b % 2 == 1:
                        dve.drain().then_inc(freed[(Q_STATE + b // 2) % RING], 1)
                ys = psum[:, 6, :].rearrange("p (c t) -> p c t", c=KD)
                for c in range(KD):
                    a = PAT["d_skip"] + c
                    dve.scalar_tensor_tensor(out=xbc[:, c, tok(2)], in0=xbc[:, c, tok(2)], scalar=par[:, L, a:a + 1],
                                             in1=ys[:, c, :], op0=ALU.mult, op1=ALU.add)
                dve.drain()
                dve.tensor_tensor(xbc[:, 0:KD, :], xbc[:, 0:KD, :], zv[:], ALU.mult).then_inc(s_gated, 1)
                dve.wait_ge(s_rstd6, L + 1)
                for c in range(KD):
                    a = PAT["ssd_gain"] + c
                    dve.scalar_tensor_tensor(out=xbc[:, c, :], in0=xbc[:, c, :], scalar=par[:, L, a:a + 1],
                                             in1=rstd6[:, c // 4, :], op0=ALU.mult, op1=ALU.mult)
                for c in range(KD):
                    a = PAT["ret_gain"] + c
                    dve.scalar_tensor_tensor(out=kq[:, c, :], in0=kq[:, c, :], scalar=par[:, L, a:a + 1],
                                             in1=rstd6[:, 2 + c // 2, :], op0=ALU.mult, op1=ALU.mult)
                dve.drain()
                dve.tensor_tensor(kq[:], kq[:], gate[:], ALU.mult).then_inc(s_mix, 1)
                for j in range(KD):
                    dve.wait_ge(s_wout, L * 16 + j + 1)
                    dve.tensor_tensor(x[:, j, :], x[:, j, :], psum[:, j % 4, 0:T], ALU.add).then_inc(s_xadd, 1)

            def attention(L):
                dve.memset(q_own[:], 0.0).then_inc(s_qzero, 1)
                normed(L, 1, "norm_mem")
                for t in range(3):
                    n = TOKN[t]
                    dve.wait_ge(s_xs, L * 3 + t + 1)
                    dve.tensor_reduce(xmax[0:n, t, :],
                                      psum[0:n, 2 * t:2 * t + 2, :].rearrange("p a (b m) -> p a b m", b=2),
                                      AX.X, ALU.max)
                    dve.drain()
                    dve.tensor_scalar(xmax[0:n, t, :], xmax[0:n, t, :], -1.0 / 16, None, ALU.mult).then_inc(s_xmax, 1)
                for t in range(3):
                    n = TOKN[t]
                    dve.wait_ge(s_xexp, L * 3 + t + 1)
                    dve.reciprocal(xsum[0:n, t, :], xsum[0:n, t, :])
                    dve.drain()
                    dve.tensor_tensor(prob[0:n, t], prob[0:n, t],
                                      xsum[0:n, t, :].unsqueeze(2).broadcast_to([n, XH, M]), ALU.mult)\
                        .then_inc(s_prob, 1)
                for j in range(KD):
                    dve.wait_ge(s_wout, L * 16 + KD + j + 1)
                    dve.tensor_tensor(x[:, j, :], x[:, j, :], psum[:, j % 4, 0:T], ALU.add).then_inc(s_xadd, 1)

            def first_of(mask, vals, top, tmp):
                dve.tensor_tensor(mask, vals, top.unsqueeze(2).broadcast_to([P, 3, EPG]), ALU.is_equal)
                dve.drain()
                dve.tensor_tensor(mask, mask, k_("rank", EPG).unsqueeze(1).broadcast_to([P, 3, EPG]), ALU.mult)
                dve.drain()
                dve.tensor_reduce(tmp, mask, AX.X, ALU.max)
                dve.drain()
                dve.tensor_tensor(mask, mask, tmp.unsqueeze(2).broadcast_to([P, 3, EPG]), ALU.is_equal)
                dve.drain()

            def moe(L):
                for i in range(2):
                    dve.wait_ge(s_store[i], 16 * (5 - i) * (L + 1))
                dve.wait_ge(s_tstore, 16 * (L + 1))
                dve.wait_ge(s_mkstore, 16 * (L + 1))
                dve.wait_ge(s_mvstore, 16 * (L + 1))
                normed(L, 2, "norm_ffn")
                dve.memset(logits[:], 0.0)
                dve.drain()
                dve.wait_ge(s_route, L + 1)
                a = PAT["route_b"]
                for t in range(3):
                    n = TOKN[t]
                    dve.tensor_tensor(logits[0:n, t, :], psum[0:n, 6, t * 32:t * 32 + EG + E],
                                      par[0:n, L, a:a + EG + E], ALU.add)
                dve.drain()
                gl = logits[:, :, 0:EG]
                dve.tensor_reduce(gmax, gl, AX.X, ALU.max)
                dve.drain()
                first_of(gsel, gl, gmax, mt)
                dve.drain().then_inc(s_rv, 1)
                dve.tensor_tensor(gtmp, gl, gmax.unsqueeze(2).broadcast_to([P, 3, EG]), ALU.subtract)
                for t in range(3):
                    dve.tensor_tensor(epick[:, t], logits[:, t, EG:].rearrange("p (g e) -> p g e", g=EG),
                                      gsel[:, t, :].unsqueeze(2).broadcast_to([P, EG, EPG]), ALU.mult)
                dve.drain()
                dve.tensor_tensor(el, epick[:, :, 0, :], epick[:, :, 1, :], ALU.add)
                dve.drain()
                dve.tensor_tensor(el, el, epick[:, :, 2, :], ALU.add)
                dve.drain()
                dve.tensor_tensor(el, el, epick[:, :, 3, :], ALU.add)
                dve.wait_ge(s_cnt, L + 1)
                dve.memset(ranked, 0.0)
                dve.drain()
                for t in range(3):
                    n = TOKN[t]
                    dve.tensor_tensor(ranked[0:n, t, :], gsel[0:n, t, :], psum[0:n, 5, t * 32:t * 32 + EG], ALU.mult)
                dve.tensor_reduce(most, psum[:, 5, 96:96 + EG], AX.X, ALU.max)
                dve.drain()
                dve.tensor_reduce(slot, ranked, AX.X, ALU.max)
                dve.tensor_scalar(spilt[:, L:L + 1], most, float(CAP), None, ALU.is_gt)
                dve.drain().then_inc(s_spilt, 1)
                for t in range(3):
                    n = TOKN[t]
                    for g in range(EG):
                        dve.tensor_scalar(chosen[0:n, t, g, :], k_("slots", CAP, n), slot[0:n, t:t + 1],
                                          gsel[0:n, t, g:g + 1], ALU.is_equal, ALU.mult)
                dve.drain().then_inc(s_chosen, 1)
                dve.tensor_reduce(m1, el, AX.X, ALU.max)
                dve.drain()
                first_of(e1, el, m1, mt)
                dve.scalar_tensor_tensor(out=el, in0=e1, scalar=-1e30, in1=el, op0=ALU.mult, op1=ALU.add)
                dve.drain()
                dve.tensor_reduce(m2, el, AX.X, ALU.max)
                dve.drain()
                first_of(e2, el, m2, mt)
                dve.tensor_tensor(mt, m2, m1, ALU.subtract)
                dve.drain().then_inc(s_rv, 1)
                dve.wait_ge(s_ra, L + 1)
                dve.tensor_reduce(gden, gtmp, AX.X, ALU.add)
                dve.tensor_scalar(w1, mt, 1.0, None, ALU.add)
                dve.drain()
                dve.tensor_tensor(w1, w1, gden, ALU.mult)
                dve.drain()
                dve.reciprocal(w1, w1)
                dve.drain()
                dve.tensor_tensor(w2, w1, mt, ALU.mult)
                dve.tensor_tensor(e1, e1, w1.unsqueeze(2).broadcast_to([P, 3, EPG]), ALU.mult)
                dve.drain()
                dve.tensor_tensor(e2, e2, w2.unsqueeze(2).broadcast_to([P, 3, EPG]), ALU.mult)
                dve.drain()
                dve.tensor_tensor(e1, e1, e2, ALU.add)
                dve.drain()
                for t in range(3):
                    for e in range(EPG):
                        dve.tensor_scalar(gate_cols[:, t, e, :], ones, e1[:, t, e:e + 1], None, ALU.mult)
                dve.drain().then_inc(s_chosen, 1)
                dve.tensor_scalar(over, slot, float(CAP), None, ALU.is_gt)
                dve.drain()
                dve.tensor_tensor(e2, e1, over.unsqueeze(2).broadcast_to([P, 3, EPG]), ALU.mult)
                dve.drain()
                for t in range(3):
                    dve.tensor_tensor(spilt_gates[:, t], gsel[:, t, :].unsqueeze(2).broadcast_to([P, EG, EPG]),
                                      e2[:, t, :].unsqueeze(1).broadcast_to([P, EG, EPG]), ALU.mult)
                for g in range(EG):
                    dve.wait_ge(s_ct, L * EG + g + 1)
                    dve.tensor_copy(chosen_t[:, g, :], psum[:, 6 + g % 2, 0:T]).then_inc(s_ctout, 1)
                dve.wait_ge(s_packout, (L + 1) * KD)
                dve.wait_ge(s_gsout, (L + 1) * EPG)
                dve.drain()
                with dve.Fori(0, EG) as g:
                    dve.tensor_copy(h_group, h_packed[:, :, g, :])
                    dve.tensor_copy(chosen_group, chosen_t[:, g, :])
                    dve.drain().then_inc(s_group, 1)
                    for u in range(EPG):
                        seen = (L * E + g * EPG + u) * 2
                        for q in range(2):
                            dve.wait_ge(s_up, seen + q + 1)
                            dve.wait_ge(s_sg, seen + q + 1)
                            sg = silu_gate[:, q, :]
                            dve.tensor_tensor(sg, sg, psum[:, 2 + q, 0:2 * CAP], ALU.mult)
                            dve.drain()
                            dve.tensor_tensor(hidden[:, 2 * q:2 * q + 2, :], sg.rearrange("p (f c) -> p f c", f=2),
                                              gates[:, u, g, :].unsqueeze(1).broadcast_to([P, 2, CAP]), ALU.mult)\
                                .then_inc(s_hid, 1)
                    for j in range(KD):
                        dve.wait_ge(s_spread, (L * EG + g) * KD + j + 1)
                        dve.tensor_tensor(x[:, j, :], x[:, j, :], psum[:, 6 + j % 2, 0:T], ALU.add)\
                            .then_inc(s_added, 1)
                with dve.If(dve.value_load(spilt[0:1, L:L + 1], min_val=0, max_val=1) > 0):
                    dve.drain().then_inc(d_start, 1)
                    dve.wait_ge(d_grow, L + 1)
                    for e in range(E):
                        if e >= 2:
                            dve.wait_ge(d_gb, L * E + e - 1)
                        dve.tensor_scalar(one_row[0:E, e % 2, :], gate_row[0:E, :], ident[0:E, e:e + 1], None,
                                          ALU.mult).then_inc(d_orow, 1)
                    with dve.Fori(0, E) as e:
                        seen = (L * E + e) * FC
                        for f in range(FC):
                            dve.wait_ge(d_up, seen + f + 1)
                            dve.wait_ge(d_sg, seen + f + 1)
                            sg = all_silu[:, f % 2, :]
                            dve.tensor_tensor(sg, sg, psum[:, 2 + f % 2, 0:T], ALU.mult)
                            dve.drain()
                            dve.tensor_tensor(all_hidden[:, f, :], sg, all_gates[:, e, :], ALU.mult)\
                                .then_inc(d_hid, 1)
                        for j in range(KD):
                            dve.wait_ge(d_down, seen * 2 + j + 1)
                            dve.tensor_tensor(x[:, j, :], x[:, j, :], psum[:, 4 + j % 4, 0:T], ALU.add)\
                                .then_inc(d_added, 1)
                        dve.drain().then_inc(d_start, 1)
                with dve.Else():
                    for sm, n in ((d_start, E + 1), (d_orow, E), (d_hid, E * FC), (d_added, E * KD)):
                        dve.sem_inc(sm, n)
                dve.drain().then_inc(d_end, 1)

            dve.wait_ge(s_const, 48)
            for L in range(DEPTH):
                mixer(L)
                attention(L)
                moe(L)
            normed(DEPTH, 0, "norm_final")

        @block.gpsimd
        def _(pool):
            for L in range(DEPTH):
                pool.wait_ge(s_raw_free, L + 1)
                pool.dma_start(conv_out[L], conv_tail[:]).then_inc(s_tstore, 16)
                pool.wait_ge(s_csout, L * 2 + 2)
                pool.wait_ge(s_kvout, L * 2 + 2)
                pool.dma_start(st_out[L, 0], states_out[:, 0, :]).then_inc(s_store[0], 16)
                for b in range(DB):
                    pool.wait_ge(s_newst, L * DB + b + 1)
                    pool.dma_start(st_out[L, 1 + b], states_out[:, (b + 1) % 2, :]).then_inc(s_store[(b + 1) % 2], 16)
                pool.wait_ge(s_mix, L + 1)
                pool.dma_start(mem[:], mem_in).then_inc(s_mem, 16)
                pool.wait_ge(s_mkvout, L * 16 + 8)
                pool.dma_start(mk_out[L], k_mem[:]).then_inc(s_mkstore, 16)
                pool.wait_ge(s_mkvout, L * 16 + 16)
                pool.dma_start(mv_out[L], vt_mem[:]).then_inc(s_mvstore, 16)
            pool.wait_ge(s_h, DEPTH * NNORM + 1)
            pool.dma_start(y_out, h[:]).then_inc(s_ystore, 16)
            pool.wait_ge(s_ystore, 16)
            for i in range(2):
                pool.wait_ge(s_store[i], 16 * (5 - i) * DEPTH)
            pool.wait_ge(s_mkstore, 16 * DEPTH)
            pool.wait_ge(s_mvstore, 16 * DEPTH)
            pool.wait_ge(s_tstore, 16 * DEPTH)


def kernel(x_prompt, x_sample, mem_prompt, state_ssm, state_conv, state_ret, cache_mem_k, cache_mem_v,
           norm_mix, w_in, conv_w, conv_b, dt_bias, a_log, d_skip, ssd_gain, ret_gain, w_out,
           norm_mem, w_mq, w_mk, w_mv, w_mo, norm_ffn, w_rg, b_rg, w_re, b_re, w_gate, w_up, w_down,
           norm_final):
    import concourse.bacc as bacc
    from concourse.bass_utils import run_bass_kernel_spmd

    f = lambda a: np.asarray(a)

    def features(a):
        a = f(a)
        return np.moveaxis(a.reshape(*a.shape[:-2], a.shape[-2] // P, P, a.shape[-1]), -3, -2)

    def slabs(w):
        k, c = w.shape
        return w.reshape(k // P, P, c // P, P).transpose(2, 1, 0, 3)

    def quads(w):
        w = w.reshape(w.shape[0], P, -1)
        per = QUAD // w.shape[2]
        return w.reshape(-1, per, P, w.shape[2]).transpose(0, 2, 1, 3).reshape(-1, P, QUAD)

    w_in, w_out = f(w_in), f(w_out)
    w_gate, w_up, w_down = f(w_gate), f(w_up), f(w_down)
    offs = np.cumsum([0, D, CC * P, H, RH * DK, RH * DK, D, D])
    state_conv, state_ssm, state_ret = f(state_conv), f(state_ssm), f(state_ret)
    cache_mem_k, cache_mem_v = f(cache_mem_k), f(cache_mem_v)
    stream = np.zeros((DEPTH, QUADS, P, QUAD), np.float32)
    for l in range(DEPTH):
        z, xbc, dt, q, k, v, g = [w_in[l][:, offs[i]:offs[i + 1]] for i in range(7)]
        st = stream[l]
        for at, w in ((Q_V, v), (Q_K, k), (Q_Q, q), (Q_XBC, xbc), (Q_Z, z), (Q_G, g), (Q_OUT, w_out[l]),
                      (Q_MK, f(w_mk)[l]), (Q_MV, f(w_mv)[l]), (Q_MQ, f(w_mq)[l]), (Q_MO, f(w_mo)[l])):
            r = quads(slabs(w))
            st[at:at + len(r)] = r
        st[Q_DT, :, 0:KD * H] = dt.reshape(KD, P, H).transpose(1, 0, 2).reshape(P, -1)
        c = state_conv[l].reshape(DB, CW - 1, CC, P).transpose(3, 2, 0, 1)
        st[Q_DT, :, KD * H:KD * H + CC * DB * (CW - 1)] = c.reshape(P, -1)
        both = np.concatenate([state_ssm[l].transpose(0, 3, 1, 2).reshape(DB, P, 1024),
                               state_ret[l].transpose(0, 2, 1, 3).reshape(DB, P, 1024)], 2)
        st[Q_STATE:Q_STATE + 4] = both.reshape(4, 2, P, 2048).transpose(0, 2, 1, 3).reshape(4, P, QUAD)
        kc = cache_mem_k[l].reshape(DB, M, KD, P).transpose(0, 3, 2, 1).reshape(DB, P, 2048)
        vc = cache_mem_v[l].reshape(DB, 2, P, D).transpose(0, 2, 1, 3).reshape(DB, P, 2048)
        st[Q_KC:Q_KC + 4] = kc.reshape(4, 2, P, 2048).transpose(0, 2, 1, 3).reshape(4, P, QUAD)
        st[Q_VC:Q_VC + 4] = vc.reshape(4, 2, P, 2048).transpose(0, 2, 1, 3).reshape(4, P, QUAD)
        for e in range(E):
            gs, us = slabs(w_gate[l, e]), slabs(w_up[l, e])
            gu = np.stack([gs, us], 1).reshape(2 * FC, P, SLAB)
            st[Q_MOE + 3 * e:Q_MOE + 3 * e + 2] = quads(gu)
            st[Q_MOE + 3 * e + 2] = w_down[l, e].reshape(FC, P, D).transpose(1, 0, 2).reshape(P, QUAD)

    params = np.zeros((DEPTH, P, PN), np.float32)

    def put(name, l, a):
        params[l, :a.shape[0], PAT[name]:PAT[name] + a.shape[1]] = a

    for l in range(DEPTH):
        for name, a in (("norm_mix", norm_mix), ("norm_mem", norm_mem), ("norm_ffn", norm_ffn),
                        ("ssd_gain", ssd_gain), ("ret_gain", ret_gain)):
            put(name, l, f(a)[l].reshape(KD, P).T)
        put("norm_final", l, f(norm_final).reshape(KD, P).T)
        put("d_skip", l, np.repeat(f(d_skip)[l], HD).reshape(KD, P).T)
        put("conv_b", l, f(conv_b)[l].reshape(CC, P).T)
        put("conv_w", l, f(conv_w)[l].reshape(CW, CC, P).transpose(2, 1, 0).reshape(P, -1))
        put("dt_bias", l, f(dt_bias)[l][:, None])
        put("a_log", l, f(a_log)[l][:, None])
        put("route_b", l, np.tile(np.concatenate([f(b_rg)[l], f(b_re)[l]])[None], (P, 1)))
        w = np.concatenate([f(w_rg)[l], f(w_re)[l]], 1)
        put("route_w", l, w.reshape(KD, P, EG + E).transpose(1, 0, 2).reshape(P, -1))

    tokens = np.concatenate([f(x_prompt).reshape(SEQ, D), f(x_sample).reshape(NS, D)], 0)
    ins = {
        "stream": stream.reshape(DEPTH * QUADS, P, QUAD),
        "params": params,
        "consts": constants(),
        "x_in": np.ascontiguousarray(features(tokens.T)),
        "mem_in": np.ascontiguousarray(features(f(mem_prompt)[0].T)),
    }
    outs = {"y_out": (P, KD, T), "st_out": (DEPTH, 1 + DB, P, 2048), "conv_out": (DEPTH, P, CC, (CW - 1) * (1 + DB)),
            "mk_out": (DEPTH, P, KD, M), "mv_out": (DEPTH, P, KD, M)}
    nc = bacc.Bacc("TRN2", target_bir_lowering=False, num_devices=1)
    aps = [nc.dram_tensor(n, a.shape, F32, kind="ExternalInput").ap() for n, a in ins.items()]
    aps += [nc.dram_tensor(n, s, F32, kind="ExternalOutput").ap() for n, s in outs.items()]
    build(nc, *aps)
    r = run_bass_kernel_spmd(nc, [ins], core_ids=[0]).results[0]

    y = np.asarray(r["y_out"]).transpose(2, 1, 0).reshape(T, D)
    st = np.asarray(r["st_out"])
    ssm = st[..., 0:1024].reshape(DEPTH, 1 + DB, N, H, HD).transpose(0, 1, 3, 4, 2)
    ret = st[..., 1024:].reshape(DEPTH, 1 + DB, DK, RH, DV).transpose(0, 1, 3, 2, 4)
    conv = np.asarray(r["conv_out"]).reshape(DEPTH, P, CC, 1 + DB, CW - 1).transpose(0, 3, 4, 2, 1)
    conv = conv.reshape(DEPTH, 1 + DB, CW - 1, CC * P)

    def memory(a):
        return np.asarray(a).transpose(0, 3, 2, 1).reshape(DEPTH, 1, M, XH, DV)

    c = np.ascontiguousarray
    return (c(y[:SEQ].reshape(1, SEQ, D)), c(y[SEQ:].reshape(DB, DS, D)), c(ssm[:, :1]), c(conv[:, :1]), c(ret[:, :1]),
            c(memory(r["mk_out"])), c(memory(r["mv_out"])), c(ssm[:, 1:]), c(conv[:, 1:]), c(ret[:, 1:]))
```

```python
from contextlib import ExitStack

import numpy as np

import concourse.bass as bass
from concourse import mybir

F32 = mybir.dt.float32
ACT = mybir.ActivationFunctionType
ALU = mybir.AluOpType
AX = mybir.AxisListType

P = 128
DEPTH = 2
D = 1024
KD = D // P
SEQ = 256
DB, DS = 8, 8
NS = DB * DS
T = SEQ + NS
PAST = 2048
H, HD, G, N = 16, 64, 2, 128
CW = 4
CC = 12
RH, DK, DV = 4, 128, 256
M = 256
XH = 4
EG, EPG = 4, 4
E = 16
FC = 4
EPS = 1e-6
CAP = P
ROPE_BASE = 10000.0
BANK = 512

TOK0 = [0, 128, 256]
TOKN = [128, 128, 64]

SLAB = KD * P
QUAD = 4 * SLAB
RING = 3
Q_V, Q_K, Q_Q, Q_XBC, Q_DT, Q_Z, Q_G = 0, 2, 3, 4, 7, 8, 10
Q_MEM = [12, 14, 17, 19]
Q_STATE = [13, 15, 16, 18]
Q_OUT = 20
Q_MQ = 24
Q_KC, Q_VC = 26, 30
Q_MO = 34
Q_MOE = 36
QUADS = Q_MOE + 3 * E
OWN = DB * (NS + DS)
REVS = QUADS // RING
assert QUADS % RING == 0 and Q_MOE % RING == 0

XW = CW - 1 + SEQ + DB * (CW - 1 + DS)
XS0 = CW - 1 + SEQ
XOUT = XW - (CW - 1)


def layout_of(sizes):
    at, n = {}, 0
    for name, size in sizes:
        at[name] = n
        n += size
    return at, n


CONSTS = [("ident", P), ("ones", P), ("half", P), ("eps", 1),
          ("rot", P), ("cos", T), ("sin", T), ("causal", P), ("causal_s", NS),
          ("decay", RH * P), ("decay_s", RH * NS), ("qdecay", RH * P), ("qdecay_s", RH * NS),
          ("kend", RH), ("kend_s", RH), ("own", DB), ("restart", T), ("rank", EPG), ("slots", P)]
CAT, CN = layout_of(CONSTS)
FIRST = CAT["rot"]
PARAMS = [("norm_mix", KD), ("norm_mem", KD), ("norm_ffn", KD), ("norm_final", KD), ("ssd_gain", KD),
          ("ret_gain", KD), ("d_skip", KD), ("conv_b", CC), ("conv_w", CC * CW), ("dt_bias", 1), ("a_log", 1),
          ("route_b", EG + E), ("route_w", KD * (EG + E))]
PAT, PN = layout_of(PARAMS)


def gammas():
    return 1.0 - 2.0 ** (-5.0 - np.arange(RH))


def constants():
    c = np.zeros((P, CN), np.float64)

    def put(name, a):
        c[:a.shape[0], CAT[name]:CAT[name] + a.shape[1]] = a

    put("ident", np.eye(P))
    put("ones", np.ones((P, P)))
    put("half", np.full((P, P), 0.5))
    half = DK // 2
    rot = np.zeros((P, P))
    for m in range(half):
        rot[m + half, m] = -1.0
        rot[m, m + half] = 1.0
    put("rot", rot)
    pos = np.concatenate([np.arange(SEQ), np.tile(PAST + np.arange(DS), DB)]).astype(np.float32)
    inv = (np.float32(ROPE_BASE) ** (-np.arange(half, dtype=np.float32) / np.float32(half))).astype(np.float32)
    ang = (pos[None, :] * inv[:, None]).astype(np.float32).astype(np.float64)
    put("cos", np.tile(np.cos(ang), (2, 1)))
    put("sin", np.tile(np.sin(ang), (2, 1)))
    s, l = np.arange(P)[:, None], np.arange(P)[None, :]
    put("causal", (l >= s) * 1.0)
    ss, ls = np.arange(NS)[:, None], np.arange(NS)[None, :]
    same = (ss // DS == ls // DS) & (ls >= ss)
    put("causal_s", same * 1.0)
    scale = DK ** -0.5
    lg = np.log(gammas())
    put("decay", np.concatenate([np.where(l >= s, np.exp((l - s) * g), 0.0) * scale for g in lg], 1))
    put("decay_s", np.concatenate([np.where(same, np.exp((ls - ss) * g), 0.0) * scale for g in lg], 1))
    put("qdecay", np.tile(np.concatenate([np.exp((np.arange(P) + 1) * g) for g in lg])[None], (P, 1)))
    put("qdecay_s", np.tile(np.concatenate([np.exp((np.arange(NS) % DS + 1) * g) for g in lg])[None], (P, 1)))
    put("kend", np.stack([np.exp((P - 1 - np.arange(P)) * g) for g in lg], 1) * scale)
    put("kend_s", np.stack([np.exp((DS - 1 - np.arange(NS) % DS) * g) for g in lg], 1) * scale)
    put("own", (np.arange(NS)[:, None] // DS == np.arange(DB)[None]) * 1.0)
    start = np.ones(T)
    start[[0, P] + [SEQ + b * DS for b in range(DB)]] = 0.0
    put("restart", np.tile(start[None], (H, 1)))
    put("rank", np.tile(np.arange(EPG, 0, -1.0)[None], (P, 1)))
    put("eps", np.full((P, 1), EPS))
    put("slots", np.tile(np.arange(1, CAP + 1.0)[None], (P, 1)))
    return c.astype(np.float32)


def build(nc, stream, params, consts, x_in, mem_in, y_out, st_out, conv_out, mk_out, mv_out):
    with ExitStack() as ctx:
        def sb(name, *shape):
            return ctx.enter_context(nc.sbuf_tensor(name, [P, *shape], F32))

        def sem(name):
            return ctx.enter_context(nc.semaphore(name))

        ring = sb("ring", RING, QUAD)
        cst = sb("cst", CN)
        par = sb("par", DEPTH, PN)
        x = sb("x", KD, T)
        h = sb("h", KD, T)
        work_n = 21572
        work = sb("work", work_n)
        states_out = sb("states_out", 2, 2048)
        rstd = sb("rstd", T)
        head_rows = sb("head_rows", 2, T)
        dt_row, acum_row = head_rows[:, 0, :], head_rows[:, 1, :]
        squares = head_rows
        mem = sb("mem", KD, M)
        k_mem = sb("k_mem", KD, M)
        dt_tok = sb("dt_tok", 3, H)
        acum_tok = sb("acum_tok", 3, H)
        cbm = sb("cbm", G, P)
        last = sb("last", 2, H)
        last_s = sb("last_s", H, DB)
        last_own = sb("last_own", H, DB)
        grown = sb("grown", H)
        decay_end = sb("decay_end", H)
        keep = sb("keep", H)
        table = sb("table", 1)
        conv_tail = sb("conv_tail", CC, (CW - 1) * (1 + DB))
        spilt = ctx.enter_context(nc.sbuf_tensor("spilt", [P, DEPTH], mybir.dt.int32))
        psum = ctx.enter_context(nc.psum_tensor("psum", [P, 8, BANK], F32))

        def view(tensor, at, *shape):
            n = int(np.prod(shape))
            v = tensor[:, at:at + n]
            if len(shape) == 1:
                return v
            names = "abcd"[:len(shape)]
            return v.rearrange(f"p ({' '.join(names)}) -> p {' '.join(names)}",
                               **{k: s for k, s in zip(names, shape)})

        zv = view(work, 0, KD, T)
        raw = view(work, 2560, CC, XW)
        gate = view(work, 2560, KD, T)
        decays = view(work, 5120, 2, BANK)
        decays_of = [decays, view(k_mem[:].rearrange("p a b -> p (a b)"), 1024, 2, BANK)]
        xbc = view(work, 6724, CC, T)
        kq = view(work, 10564, 2 * RH, T)
        v_tok = view(work, 13124, 3, D)
        x_tok = view(work, 16196, 3, D)
        conv_acc = view(work, 16196, 2, XOUT)
        dt_tmp = view(work, 16196 + 2 * XOUT, 6, T)
        b_tok = view(work, 19268, 3, G * N)
        k_tok = view(work, 20036, 3, RH * DK)
        rot_tmp = view(work, 20036, 2, T)
        rstd6 = view(work, 13124, 6, T)
        hflat = h[:].rearrange("p a b -> p (a b)")
        c_own = hflat[:, 0:G * OWN].rearrange("p (g n) -> p g n", g=G)
        q_dec_s = hflat[:, 1152:1408].rearrange("p (h t) -> p h t", h=RH)
        k_own = hflat[:, 1408:1920]
        b_own = hflat[:, 1920:2176]
        rows = work[:, 6144:6656]
        vt_mem = view(work, 16196, KD, M)
        v_mem = view(work, 0, 2, D)
        q_p = view(work, 2048, KD, SEQ)
        q_own = view(work, 4096, KD, OWN)
        prob = view(work, 8704, 3, XH, M)
        prob_t = view(work, 11776, XH, 2, SEQ)
        prob_own = view(work, 13824, XH, 2, OWN)
        o_tok = view(work, 18432, D)
        xmax = view(work, 19968, 3, XH)
        xsum = view(work, 19980, 3, XH)
        chosen = view(work, 0, 3, EG, CAP)
        chosen_t = view(work, 1536, EG, T)
        h_tok = view(work, 2816, 3, D)
        h_packed = view(work, 5888, KD, EG, CAP)
        slot_gates = view(work, 9984, EG, EPG)
        group_gates = view(work, 10000, EPG)
        y_group = view(work, 13056, D)
        silu_gate = view(work, 14400, 2, 2 * CAP)
        hidden = view(work, 14912, FC, CAP)
        all_gates = view(work, 0, E, T)
        all_silu = view(work, 5120, 2, T)
        all_hidden = view(work, 5760, FC, T)
        gate_row = view(work, 7040, T)
        one_row = view(work, 7360, 2, T)
        all_w = view(work, 8192, 3, QUAD)
        R0 = 20500
        logits = view(work, R0 + 300, 3, EG + E)
        gmax = view(work, R0, 3)
        gsel = view(work, R0 + 10, 3, EG)
        gtmp = view(work, R0 + 30, 3, EG)
        gden = view(work, R0 + 50, 3)
        epick = view(work, R0 + 60, 3, EG, EPG)
        el = view(work, R0 + 120, 3, EPG)
        e1 = view(work, R0 + 140, 3, EPG)
        e2 = view(work, R0 + 160, 3, EPG)
        m1 = view(work, R0 + 180, 3)
        m2 = view(work, R0 + 190, 3)
        mt = view(work, R0 + 200, 3)
        w1 = view(work, R0 + 210, 3)
        w2 = view(work, R0 + 220, 3)
        slot = view(work, R0 + 230, 3)
        over = view(work, R0 + 240, 3)
        most = view(work, R0 + 250, 1)
        ranked = view(work, R0 + 260, 3, EG)
        spilt_gates = view(work, R0 + 400, 3, EG, EPG)

        def k_(name, n, rows_=P, at=0):
            return cst[0:rows_, CAT[name] + at:CAT[name] + at + n]

        ident, ones = k_("ident", P), k_("ones", P)

        s_const = sem("s_const")
        s_tables = sem("s_tables")
        loaded = [sem(f"s_loaded{s}") for s in range(RING)]
        freed = [sem(f"s_freed{s}") for s in range(RING)]
        s_sq = sem("s_sq")
        s_acc = sem("s_acc")
        s_sum = sem("s_sum")
        s_rstd = sem("s_rstd")
        s_h = sem("s_h")
        s_proj = sem("s_proj")
        s_evac = sem("s_evac")
        s_rot = sem("s_rot")
        s_rotated = sem("s_rotated")
        s_dtv = sem("s_dtv")
        s_dta = sem("s_dta")
        s_conv = sem("s_conv")
        s_raw_free = sem("s_raw_free")
        s_silu = sem("s_silu")
        s_t = sem("s_t")
        s_tout = [sem(f"s_tout{i}") for i in range(2)]
        s_cb = sem("s_cb")
        s_rows = sem("s_rows")
        s_bc = sem("s_bc")
        s_diff = sem("s_diff")
        s_exp = sem("s_exp")
        s_lm = sem("s_lm")
        s_y = sem("s_y")
        s_yout = sem("s_yout")
        s_dec = sem("s_dec")
        s_dece = sem("s_dece")
        s_xdec = sem("s_xdec")
        s_cs = sem("s_cs")
        s_csout = sem("s_csout")
        s_score = sem("s_score")
        s_decayed = sem("s_decayed")
        s_o = sem("s_o")
        s_oout = sem("s_oout")
        s_kv = sem("s_kv")
        s_kvout = sem("s_kvout")
        s_own = sem("s_own")
        s_off = sem("s_off")
        s_offtok = sem("s_offtok")
        s_offt = sem("s_offt")
        s_otok = sem("s_otok")
        s_ott = sem("s_ott")
        s_batch = sem("s_batch")
        s_newst = sem("s_newst")
        s_store = [sem(f"s_store{i}") for i in range(2)]
        s_gated = sem("s_gated")
        s_sq6 = sem("s_sq6")
        s_pair6 = sem("s_pair6")
        s_sum6 = sem("s_sum6")
        s_rstd6 = sem("s_rstd6")
        s_mix = sem("s_mix")
        s_wout = sem("s_wout")
        s_xadd = sem("s_xadd")
        s_mem = sem("s_mem")
        s_mkv = sem("s_mkv")
        s_mkvout = sem("s_mkvout")
        s_vt = sem("s_vt")
        s_vtout = sem("s_vtout")
        s_mkstore = sem("s_mkstore")
        s_mvstore = sem("s_mvstore")
        s_qzero = sem("s_qzero")
        s_pzero = sem("s_pzero")
        s_q = sem("s_q")
        s_qout = sem("s_qout")
        s_xs = sem("s_xs")
        s_xmax = sem("s_xmax")
        s_xexp = sem("s_xexp")
        s_prob = sem("s_prob")
        s_pt = sem("s_pt")
        s_ptout = sem("s_ptout")
        s_xo = sem("s_xo")
        s_xoout = sem("s_xoout")
        s_route = sem("s_route")
        s_rv = sem("s_rv")
        s_ra = sem("s_ra")
        s_ht = sem("s_ht")
        s_htout = sem("s_htout")
        s_cnt = sem("s_cnt")
        s_chosen = sem("s_chosen")
        s_pack = sem("s_pack")
        s_packout = sem("s_packout")
        s_gs = sem("s_gs")
        s_gsout = sem("s_gsout")
        s_ct = sem("s_ct")
        s_ctout = sem("s_ctout")
        s_gate = sem("s_gate")
        s_up = sem("s_up")
        s_sg = sem("s_sg")
        s_hid = sem("s_hid")
        s_down = sem("s_down")
        s_yg = sem("s_yg")
        s_spread = sem("s_spread")
        s_added = sem("s_added")
        s_spilt = sem("s_spilt")
        d_start = sem("d_start")
        d_loaded = sem("d_loaded")
        d_gt = sem("d_gt")
        d_grow = sem("d_grow")
        d_orow = sem("d_orow")
        d_gb = sem("d_gb")
        d_gbout = sem("d_gbout")
        d_gate = sem("d_gate")
        d_up = sem("d_up")
        d_sg = sem("d_sg")
        d_hid = sem("d_hid")
        d_down = sem("d_down")
        d_added = sem("d_added")
        d_end = sem("d_end")
        s_tstore = sem("s_tstore")
        s_ystore = sem("s_ystore")

        block = ctx.enter_context(nc.Block())
        NNORM = 3
        SUM_BANK = [0, 7, 7]
        gam = gammas()

        def quad(eng, L, q):
            eng.wait_ge(loaded[q % RING], 16 * (L * REVS + q // RING + 1))
            return ring[:, q % RING, :]

        def tok(t):
            return slice(TOK0[t], TOK0[t] + TOKN[t])

        def turned_by(L, i):
            return L * (10 - i % 2) + i // 2 + 1

        def own_blocks(a):
            return a.rearrange("p (b j) -> p b j", b=DB)[:, :, 0:DS]

        def heads_of(t):
            hb = BANK // TOKN[t]
            return hb, H // hb

        @block.sync
        def _(sp):
            sp.dma_start(cst[:, 0:FIRST], consts[:, 0:FIRST]).then_inc(s_const, 16)
            sp.dma_start(x[:], x_in).then_inc(s_const, 16)
            sp.dma_start(par[:], params.rearrange("l p n -> p l n")).then_inc(s_const, 16)
            for L in range(DEPTH):
                for r in range(REVS):
                    n = L * REVS + r
                    for s in range(RING):
                        if n >= 1:
                            sp.wait_ge(freed[s], n)
                        sp.dma_start(ring[:, s, :], stream[n * RING + s]).then_inc(loaded[s], 16)
                    if n == 0:
                        sp.dma_start(cst[:, FIRST:], consts[:, FIRST:]).then_inc(s_tables, 16)
                        sp.dma_start(mem[:], mem_in).then_inc(s_mem, 16)
                sp.wait_ge(s_spilt, L + 1)
                with sp.If(sp.value_load(spilt[0:1, L:L + 1], min_val=0, max_val=1) > 0):
                    for e in range(E):
                        sp.wait_ge(d_start, L * (E + 1) + e + 1)
                        q = L * QUADS + Q_MOE + 3 * e
                        sp.dma_start(all_w[:], stream[q:q + 3].rearrange("q p n -> p q n")).then_inc(d_loaded, 16)
                with sp.Else():
                    sp.sem_inc(d_loaded, 16 * E)

        @block.tensor
        def _(pe):
            riding = []

            def free(q):
                riding.append(freed[q % RING])

            def first(ins):
                for sm in riding:
                    ins.then_inc(sm, 1)
                riding.clear()
                return ins

            def sums_of_squares(L, k):
                done = (L * NNORM + k) * KD
                if k == 0:
                    for j in range(KD):
                        pe.wait_ge(s_sq, done + j + 1)
                        mm = pe.matmul(psum[:, SUM_BANK[k], 0:T], ones, h[:, j, :], start=(j == 0), stop=(j == KD - 1))
                else:
                    pe.wait_ge(s_acc, (L * 2 + k) * (KD - 2))
                    pe.matmul(psum[:, SUM_BANK[k], 0:T], ones, rstd[:], start=True, stop=False)
                    pe.wait_ge(s_sq, done + KD)
                    mm = pe.matmul(psum[:, SUM_BANK[k], 0:T], ones, squares[:, 1, :], start=False, stop=True)
                mm.then_inc(s_sum, 1)

            def products(out, w, base, step, rhs, norm=None):
                for j in range(KD):
                    if norm is not None:
                        pe.wait_ge(s_h, norm * KD + j + 1)
                    a = base + j * step
                    mm = pe.matmul(out, w[:, a:a + P], rhs[:, j, :], start=(j == 0), stop=(j == KD - 1))
                    if j == 0:
                        first(mm)
                return mm

            def transposes(outs_ins):
                for o, i in outs_ins:
                    mm = pe.transpose(o, i, ident[0:i.shape[0], 0:i.shape[0]])
                return mm

            def mixer(L):
                if L == 0:
                    sums_of_squares(L, 0)
                n_proj = 0

                def project(q0, chunks, banks=4, fresh=False):
                    nonlocal n_proj
                    for c in chunks:
                        w = quad(pe, L, q0 + c // 4)
                        if n_proj >= 4:
                            pe.wait_ge(s_evac, L * 45 + n_proj + 1 - banks)
                        products(psum[:, n_proj % banks, 0:T], w, (c % 4) * SLAB, P, h,
                                 L * NNORM if fresh and c == 0 else None).then_inc(s_proj, 1)
                        n_proj += 1
                        if c % 4 == 3:
                            free(q0 + c // 4)

                project(Q_V, range(8), fresh=True)
                project(Q_K, range(4))
                project(Q_Q, range(4))
                pe.wait_ge(s_tables, 16)
                for j in range(12):
                    project(Q_XBC, [j])
                    if j < 2 * RH:
                        pe.wait_ge(s_evac, L * 45 + 8 + j + 1)
                        if j >= 2:
                            pe.wait_ge(s_rotated, L * 8 + j - 1)
                        pe.matmul(psum[:, 4 + j % 2, 0:T], k_("rot", P), kq[:, j, :], start=True, stop=True)\
                            .then_inc(s_rot, 1)
                w = quad(pe, L, Q_DT)
                pe.wait_ge(s_evac, L * 45 + n_proj - 3)
                for j in range(KD):
                    mm = pe.matmul(psum[0:H, n_proj % 4, 0:T], w[:, j * H:(j + 1) * H], h[:, j, :],
                                   start=(j == 0), stop=(j == KD - 1))
                    if j == 0:
                        first(mm)
                mm.then_inc(s_proj, 1)
                n_proj += 1
                nt = 0
                project(Q_Z, range(2))
                pe.wait_ge(s_rotated, (L + 1) * 8)

                def turn(group, n):
                    nonlocal nt
                    if nt >= 4:
                        pe.wait_ge(s_tout[nt % 2], turned_by(L, nt - 4))
                    b = 4 + nt % 4
                    transposes([(psum[0:n, b, i * P:(i + 1) * P], src) for i, src in enumerate(group)])\
                        .then_inc(s_t, 1)
                    nt += 1

                for t in range(3):
                    for half in range(2):
                        turn([zv[:, 4 * half + i, tok(t)] for i in range(4)], TOKN[t])
                project(Q_Z, range(2, 4))
                for t in range(3):
                    turn([kq[:, i, tok(t)] for i in range(4)], TOKN[t])
                project(Q_Z, range(4, 8))
                pe.wait_ge(s_silu, (L + 1) * CC)
                for t in range(3):
                    for half in range(2):
                        turn([xbc[:, 4 * half + i, tok(t)] for i in range(4)], TOKN[t])
                for t in range(3):
                    turn([xbc[:, 8 + i, tok(t)] for i in range(2)], TOKN[t])
                pe.wait_ge(s_dtv, (L + 1) * 4)
                pe.wait_ge(s_tout[nt % 2], turned_by(L, nt - 4))
                b = 4 + nt % 4
                for t in range(3):
                    for i, src in enumerate((dt_row, acum_row)):
                        mm = pe.transpose(psum[0:TOKN[t], b, (3 * i + t) * H:(3 * i + t + 1) * H],
                                          src[0:H, tok(t)], ident[0:H, 0:H])
                mm.then_inc(s_t, 1)
                nt += 1

                def scores_cb(t):
                    n = TOKN[t]
                    for g in range(G):
                        mm = pe.matmul(psum[0:n, 4, g * P:g * P + n], xbc[:, 8 + g, tok(t)], xbc[:, 10 + g, tok(t)],
                                       start=True, stop=True)
                    mm.then_inc(s_cb, 1)

                def broadcast(step):
                    if step in (0, 4, 8):
                        scores_cb(step // 4)
                    pe.wait_ge(s_rows, L * 10 + step + 1)
                    if step >= 2:
                        pe.wait_ge(s_exp, L * 10 + step - 1)
                    pe.matmul(psum[:, (5, 7)[step % 2], 0:BANK], ones[0:H, :], rows[0:H, :], start=True, stop=True)\
                        .then_inc(s_bc, 1)

                for i in (17, 18):
                    pe.wait_ge(s_tout[i % 2], turned_by(L, i))
                pe.wait_ge(s_evac, L * 45 + n_proj)
                n_mem = 0

                def project_memory(chunks):
                    nonlocal n_mem
                    for _ in range(chunks):
                        c = n_mem
                        w = quad(pe, L, Q_MEM[c // 4])
                        if c >= 2:
                            pe.wait_ge(s_mkvout, L * 16 + c)
                        out = psum[:, c, 0:M] if c < 2 else psum[:, 4, M:2 * M]
                        products(out, w, (c % 4) * SLAB, P, mem).then_inc(s_mkv, 1)
                        n_mem += 1
                        if c % 4 == 3:
                            free(Q_MEM[c // 4])

                def chunk_states(t):
                    pe.wait_ge(s_xdec, L * 3 + t + 1)
                    for g in range(G):
                        mm = pe.matmul(psum[:, 2 + g, 0:BANK], b_tok[:, t, g * N:(g + 1) * N],
                                       x_tok[:, t, g * BANK:(g + 1) * BANK], start=True, stop=True)
                    mm.then_inc(s_cs, 1)

                def retention_scores(t):
                    n = TOKN[t]
                    for r in range(RH):
                        mm = pe.matmul(psum[0:n, 5, r * n:(r + 1) * n], kq[:, r, tok(t)], kq[:, RH + r, tok(t)],
                                       start=True, stop=True)
                    mm.then_inc(s_score, 1)

                broadcast(0)
                broadcast(1)
                for step in range(10):
                    t, i = min(step // 4, 2), step - 4 * min(step // 4, 2)
                    n = TOKN[t]
                    hb = heads_of(t)[0]
                    if step < KD:
                        project(Q_G, [step], banks=2)
                    else:
                        if step == KD:
                            pe.wait_ge(s_mem, 16)
                            pe.wait_ge(s_evac, (L + 1) * 45)
                        project_memory(1)
                        if step == 9:
                            pe.wait_ge(s_exp, L * 10 + 9)
                            retention_scores(0)
                    if i == 0 and t > 0:
                        chunk_states(t - 1)
                    if step + 2 < 10:
                        broadcast(step + 2)
                    if step == 4:
                        pe.wait_ge(s_csout, L * 2 + 1)
                    pe.wait_ge(s_lm, L * 10 + step + 1)
                    if step > 0:
                        pe.wait_ge(s_yout, L * 10 + step)
                    dec = decays_of[step % 2]
                    for hh in range(hb):
                        hd = i * hb + hh
                        c = hh // 2
                        o = psum[(hd % 2) * HD:(hd % 2) * HD + HD, 6, c * n:c * n + n]
                        mm = pe.matmul(o, x_tok[0:n, t, hd * HD:(hd + 1) * HD], dec[0:n, 0, hh * n:(hh + 1) * n],
                                       start=True, stop=(t != 1), skip_group_check=True)
                        if t == 1:
                            mm = pe.matmul(o, states_out[:, 0, hd * HD:(hd + 1) * HD],
                                           dec[:, 1, hh * n:(hh + 1) * n],
                                           start=False, stop=True, skip_group_check=True)
                    mm.then_inc(s_y, 1)

                for t in range(3):
                    n = TOKN[t]
                    project_memory(1)
                    if t == 0:
                        pe.wait_ge(s_csout, L * 2 + 2)
                        pe.wait_ge(s_yout, (L + 1) * 10)
                    else:
                        pe.wait_ge(s_oout, L * 2 + t)
                        pe.wait_ge(s_kvout, L * 2 + t)
                    pe.wait_ge(s_decayed, L * 3 + t + 1)
                    if t < 2:
                        for r in range(RH):
                            for e in range(2):
                                o = psum[:, 2 + r // 2, (r % 2) * 2 * P + e * P:(r % 2) * 2 * P + (e + 1) * P]
                                mm = pe.matmul(o, v_tok[:, t, r * DV + e * P:r * DV + (e + 1) * P],
                                               decays[:, 0, r * P:(r + 1) * P], start=True, stop=(t == 0),
                                               skip_group_check=True)
                                if t == 1:
                                    mm = pe.matmul(o, states_out[:, 0, 1024 + r * DV + e * P:1024 + r * DV + (e + 1) * P],
                                                   decays[:, 1, r * P:(r + 1) * P], start=False, stop=True,
                                                   skip_group_check=True)
                        mm.then_inc(s_o, 1)
                        for r in range(RH):
                            mm = pe.matmul(psum[:, r // 2, (r % 2) * DV:(r % 2 + 1) * DV],
                                           k_tok[:, t, r * DK:(r + 1) * DK], v_tok[:, t, r * DV:(r + 1) * DV],
                                           start=True, stop=True)
                        mm.then_inc(s_kv, 1)
                        retention_scores(t + 1)
                    else:
                        for r in range(RH):
                            for e in range(2):
                                c = 2 * r + e
                                pe.matmul(psum[:, 7, c * NS:(c + 1) * NS],
                                          v_tok[0:n, t, r * DV + e * P:r * DV + (e + 1) * P],
                                          decays[0:n, 0, r * n:(r + 1) * n], start=(c == 0), stop=False,
                                          skip_group_check=True)
                for b in range(DB):
                    w = quad(pe, L, Q_STATE[b // 2])
                    ws = w[:, (b % 2) * 2048:(b % 2 + 1) * 2048]
                    for g in range(G):
                        mm = pe.matmul(psum[0:NS, 5 + g, 0:BANK], c_own[:, g, b * NS:(b + 1) * NS],
                                       ws[:, g * BANK:(g + 1) * BANK], start=(b == 0), stop=(b == DB - 1),
                                       skip_group_check=True)
                        if g == 0:
                            first(mm)
                    if b == DB - 1:
                        mm.then_inc(s_off, 1)
                    for r in range(RH):
                        for e in range(2):
                            c = 2 * r + e
                            mm = pe.matmul(psum[:, 7, c * NS + b * DS:c * NS + (b + 1) * DS],
                                           ws[:, 1024 + r * DV + e * P:1024 + r * DV + (e + 1) * P],
                                           q_dec_s[:, r, b * DS:(b + 1) * DS],
                                           start=False, stop=(b == DB - 1), skip_group_check=True)
                    if b not in (3, 5, 7):
                        project_memory(1)
                    pe.wait_ge(s_own, L * DB + b + 1)
                    if b > 0:
                        pe.wait_ge(s_newst, L * DB + b)
                    for g in range(G):
                        pe.matmul(psum[:, g, 0:BANK], b_own[0:NS, g * N:(g + 1) * N],
                                  x_tok[0:NS, 2, g * BANK:(g + 1) * BANK], start=True, stop=True)
                    for r in range(RH):
                        mm = pe.matmul(psum[:, 2 + r // 2, (r % 2) * DV:(r % 2 + 1) * DV],
                                       k_own[0:NS, r * DK:(r + 1) * DK], v_tok[0:NS, 2, r * DV:(r + 1) * DV],
                                       start=True, stop=True)
                    mm.then_inc(s_batch, 1)
                project_memory(1)
                pe.wait_ge(s_offtok, L + 1)
                transposes([(psum[:, 6, c * NS:(c + 1) * NS], x_tok[0:NS, 2, c * P:(c + 1) * P])
                            for c in range(KD)]).then_inc(s_offt, 1)
                project_memory(2)
                pe.wait_ge(s_pair6, L * 2 + 1)
                for g in range(G):
                    for i in range(2):
                        mm = pe.matmul(psum[:, g, 0:T], k_("half", P), h[:, 4 * g + i, :],
                                       start=(i == 0), stop=(i == 1))
                        if g + i == 0:
                            first(mm)
                mm.then_inc(s_sum6, 1)
                project_memory(1)
                pe.wait_ge(s_pair6, L * 2 + 2)
                for r in range(RH):
                    mm = pe.matmul(psum[:, (2, 3, 5, 6)[r], 0:T], ones, h[:, 2 * r, :], start=True, stop=True)
                    if r == 0:
                        first(mm)
                mm.then_inc(s_sum6, 1)
                project_memory(16 - n_mem)
                pe.wait_ge(s_mkvout, (L + 1) * 16)
                for j in range(KD):
                    w = quad(pe, L, Q_OUT + j // 2)
                    if j >= 4:
                        pe.wait_ge(s_xadd, L * 16 + j - 3)
                    for i in range(2 * KD):
                        if j == 0 and i % KD == 0:
                            pe.wait_ge(s_mix, L * 2 + i // KD + 1)
                        a = (j % 2) * 2 * SLAB + i * P
                        src = xbc[:, i, :] if i < KD else kq[:, i - KD, :]
                        mm = pe.matmul(psum[:, j % 4, 0:T], w[:, a:a + P], src, start=(i == 0), stop=(i == 15))
                        if i == 0:
                            first(mm)
                    mm.then_inc(s_wout, 1)
                    if j % 2 == 1:
                        free(Q_OUT + j // 2)
                sums_of_squares(L, 1)

            def attention(L):
                for i in range(4):
                    mc, half = i // 2, i % 2
                    if i >= 2:
                        pe.wait_ge(s_vtout, L * 4 + i - 1)
                    mm = transposes([(psum[:, 4 + half, c * P:(c + 1) * P], vt_mem[:, 4 * half + c, mc * P:(mc + 1) * P])
                                     for c in range(4)])
                    mm.then_inc(s_vt, 1)
                for c in range(KD):
                    w = quad(pe, L, Q_MQ + c // 4)
                    if c >= 4:
                        pe.wait_ge(s_qout, L * KD + c - 3)
                    products(psum[:, c % 4, 0:T], w, (c % 4) * SLAB, P, h,
                             L * NNORM + 1 if c == 0 else None).then_inc(s_q, 1)
                    if c % 4 == 3:
                        free(Q_MQ + c // 4)
                pe.wait_ge(s_qout, (L + 1) * KD)
                pe.wait_ge(s_vtout, (L + 1) * 4)
                for t in range(2):
                    for r in range(XH):
                        for c in range(2):
                            mm = pe.matmul(psum[:, 2 * t + r // 2, (r % 2) * M:(r % 2 + 1) * M],
                                           q_p[:, 2 * r + c, tok(t)], k_mem[:, 2 * r + c, :],
                                           start=(c == 0), stop=(c == 1))
                            if t + r + c == 0:
                                first(mm)
                    mm.then_inc(s_xs, 1)
                np_ = 0

                def turn_probs(t):
                    nonlocal np_
                    pe.wait_ge(s_prob, L * 3 + t + 1)
                    for half in range(2):
                        if np_ >= 2:
                            pe.wait_ge(s_ptout, L * 6 + np_ - 1)
                        n = TOKN[t]
                        for i in range(4):
                            r, c = 2 * half + i // 2, i % 2
                            mm = pe.transpose(psum[:, 6 + np_ % 2, i * P:i * P + n],
                                              prob[0:n, t, r, c * P:(c + 1) * P], ident[0:n, 0:n])
                        mm.then_inc(s_pt, 1)
                        np_ += 1

                for b in range(DB):
                    w = quad(pe, L, Q_KC + b // 2)
                    for r in range(XH):
                        for c in range(2):
                            a = (b % 2) * 2048 + (2 * r + c) * M
                            mm = pe.matmul(psum[0:NS, 4 + r // 2, (r % 2) * M:(r % 2 + 1) * M],
                                           q_own[:, 2 * r + c, b * NS:(b + 1) * NS], w[:, a:a + M],
                                           start=(b == 0 and c == 0 and r % 2 == 0), stop=(b == DB - 1),
                                           skip_group_check=True)
                            if r + c == 0:
                                first(mm)
                    if b == DB - 1:
                        mm.then_inc(s_xs, 1)
                    if b % 2 == 1:
                        free(Q_KC + b // 2)
                    if b in (3, 6):
                        turn_probs(b // 3 - 1)
                pe.wait_ge(s_ptout, L * 6 + 4)
                for j in range(KD):
                    if j >= 4:
                        pe.wait_ge(s_xoout, L * 9 + j - 3)
                    for c in range(2):
                        mm = pe.matmul(psum[:, j % 4, 0:SEQ], v_mem[:, c, j * P:(j + 1) * P],
                                       prob_t[:, j // 2, c, :], start=(c == 0), stop=(c == 1))
                        if j + c == 0:
                            first(mm)
                    mm.then_inc(s_xo, 1)
                    if j == 3:
                        turn_probs(2)
                pe.wait_ge(s_ptout, (L + 1) * 6)
                for b in range(DB):
                    w = quad(pe, L, Q_VC + b // 2)
                    for r in range(XH):
                        for c in range(2):
                            a = (b % 2) * 2048 + c * D + r * DV
                            mm = pe.matmul(psum[0:NS, 4 + r // 2, (r % 2) * DV:(r % 2 + 1) * DV],
                                           prob_own[:, r, c, b * NS:(b + 1) * NS], w[:, a:a + DV],
                                           start=(b == 0 and c == 0 and r % 2 == 0), stop=(b == DB - 1),
                                           skip_group_check=True)
                            if r + c == 0:
                                first(mm)
                    if b == DB - 1:
                        mm.then_inc(s_xo, 1)
                    if b % 2 == 1:
                        free(Q_VC + b // 2)
                pe.wait_ge(s_otok, L + 1)
                mm = transposes([(psum[:, 6, c * NS:(c + 1) * NS], o_tok[0:NS, c * P:(c + 1) * P])
                                 for c in range(KD)])
                mm.then_inc(s_ott, 1)
                pe.wait_ge(s_xoout, (L + 1) * 9)
                for c in range(KD):
                    w = quad(pe, L, Q_MO + c // 4)
                    if c >= 4:
                        pe.wait_ge(s_xadd, L * 16 + KD + c - 3)
                    products(psum[:, c % 4, 0:T], w, (c % 4) * SLAB, P, h).then_inc(s_wout, 1)
                    if c % 4 == 3:
                        free(Q_MO + c // 4)
                sums_of_squares(L, 2)

            def moe(L):
                def turn_h(i):
                    t, half = i % 3, i // 3
                    if i >= 2:
                        pe.wait_ge(s_htout, L * 6 + i - 1)
                    transposes([(psum[0:TOKN[t], i % 2, c * P:(c + 1) * P], h[:, 4 * half + c, tok(t)])
                                for c in range(4)]).then_inc(s_ht, 1)

                for j in range(KD):
                    pe.wait_ge(s_h, (L * NNORM + 2) * KD + j + 1)
                    a = PAT["route_w"] + j * (EG + E)
                    for t in range(3):
                        mm = pe.matmul(psum[0:TOKN[t], 6, t * 32:t * 32 + EG + E], h[:, j, tok(t)],
                                       par[:, L, a:a + EG + E], start=(t + j == 0), stop=(j == KD - 1),
                                       skip_group_check=True)
                        if t + j == 0:
                            first(mm)
                mm.then_inc(s_route, 1)
                for i in range(3):
                    turn_h(i)
                pe.wait_ge(s_rv, 2 * L + 1)
                for t in range(3):
                    n = TOKN[t]
                    o = psum[0:n, 5, t * 32:t * 32 + EG]
                    for tt in range(t):
                        pe.matmul(o, ones[:, 0:n], gsel[:, tt, :], start=(tt == 0), stop=False)
                    pe.matmul(o, k_("causal", n, n), gsel[0:n, t, :], start=(t == 0), stop=True)
                for t in range(3):
                    n = TOKN[t]
                    mm = pe.matmul(psum[:, 5, 96:96 + EG], ones[0:n, :], gsel[0:n, t, :], start=(t == 0), stop=(t == 2))
                mm.then_inc(s_cnt, 1)
                for i in range(3, 6):
                    turn_h(i)
                pe.wait_ge(s_htout, (L + 1) * 6)
                pe.wait_ge(s_chosen, L * 2 + 1)
                for j in range(KD):
                    if j >= 4:
                        pe.wait_ge(s_packout, L * KD + j - 3)
                    for t in range(3):
                        n = TOKN[t]
                        mm = pe.matmul(psum[:, j % 4, :], h_tok[0:n, t, j * P:(j + 1) * P], chosen[0:n, t, :, :],
                                       start=(t == 0), stop=(t == 2))
                    mm.then_inc(s_pack, 1)
                for g in range(EG):
                    if g >= 2:
                        pe.wait_ge(s_ctout, L * EG + g - 1)
                    for t in range(3):
                        n = TOKN[t]
                        mm = pe.transpose(psum[:, 6 + g % 2, TOK0[t]:TOK0[t] + n], chosen[0:n, t, g, :],
                                          ident[0:n, 0:n])
                    mm.then_inc(s_ct, 1)
                pe.wait_ge(s_chosen, L * 2 + 2)
                for g in range(EG):
                    for t in range(3):
                        n = TOKN[t]
                        mm = pe.matmul(psum[:, 4, g * EPG:(g + 1) * EPG], chosen[0:n, t, g, :], e1[0:n, t, :],
                                       start=(t == 0), stop=(t == 2))
                mm.then_inc(s_gs, 1)
                pe.wait_ge(s_packout, (L + 1) * KD)
                pe.wait_ge(s_gsout, L + 1)
                pe.wait_ge(s_ctout, (L + 1) * EG)
                with pe.Fori(0, EG) as g:
                    for u in range(EPG):
                        seen = (L * E + g * EPG + u) * 2
                        rev = L * REVS + Q_MOE // RING + g * EPG
                        for q in range(2):
                            s, dr = (3 * u + q) % RING, (3 * u + q) // RING
                            pe.wait_ge(loaded[s], 16 * (rev + dr + 1))
                            w = ring[:, s, :]
                            for up in range(2):
                                for i in range(2):
                                    for j in range(KD):
                                        a = (2 * i + up) * SLAB + j * P
                                        mm = pe.matmul(psum[:, 2 * up + q, i * CAP:(i + 1) * CAP], w[:, a:a + P],
                                                       h_packed[:, j, g, :], start=(j == 0), stop=(j == KD - 1))
                                        if up + i + j == 0:
                                            first(mm)
                                mm.then_inc(s_up if up else s_gate, 1)
                            free(s)
                        s, dr = (3 * u + 2) % RING, (3 * u + 2) // RING
                        pe.wait_ge(loaded[s], 16 * (rev + dr + 1))
                        w = ring[:, s, :]
                        for half in range(2):
                            for f in range(FC):
                                if half == 0 and f % 2 == 0:
                                    pe.wait_ge(s_hid, seen + f // 2 + 1)
                                a = f * D + half * BANK
                                mm = pe.matmul(psum[:, 4 + half, :], hidden[:, f, :], w[:, a:a + BANK],
                                               start=(f == 0), stop=(f == FC - 1))
                                if f + half == 0:
                                    first(mm)
                            mm.then_inc(s_down, 1)
                        if u == EPG - 1:
                            pe.drain().then_inc(freed[s], 1)
                        else:
                            free(s)
                    for j in range(KD):
                        if j % 4 == 0:
                            pe.wait_ge(s_yg, (L * EG + g) * 2 + j // 4 + 1)
                        if j >= 2:
                            pe.wait_ge(s_added, (L * EG + g) * KD + j - 1)
                        pe.matmul(psum[:, 6 + j % 2, 0:T], y_group[:, j * P:(j + 1) * P], chosen_t[:, g, :],
                                  start=True, stop=True).then_inc(s_spread, 1)
                pe.wait_ge(s_spilt, L + 1)
                with pe.If(pe.value_load(spilt[0:1, L:L + 1], min_val=0, max_val=1) > 0):
                    dense(L)
                with pe.Else():
                    for sm, n in ((d_gt, 1), (d_gb, E), (d_gate, E * FC), (d_up, E * FC), (d_down, E * KD)):
                        pe.sem_inc(sm, n)
                sums_of_squares(L + 1, 0)

            def dense(L):
                pe.wait_ge(d_start, L * (E + 1) + 1)
                for t in range(3):
                    mm = pe.transpose(psum[0:E, 5, TOK0[t]:TOK0[t] + TOKN[t]],
                                      spilt_gates[0:TOKN[t], t, :, :], ident[0:TOKN[t], 0:TOKN[t]])
                mm.then_inc(d_gt, 1)
                for e in range(E):
                    pe.wait_ge(d_orow, L * E + e + 1)
                    if e >= 2:
                        pe.wait_ge(d_gbout, L * E + e - 1)
                    pe.matmul(psum[:, 6 + e % 2, 0:T], ones[0:E, :], one_row[0:E, e % 2, :],
                              start=True, stop=True).then_inc(d_gb, 1)
                pe.wait_ge(d_gbout, (L + 1) * E)
                with pe.Fori(0, E) as e:
                    seen = (L * E + e) * FC
                    pe.wait_ge(d_loaded, (L * E + e + 1) * 16)
                    for f in range(FC):
                        if f >= 2:
                            pe.wait_ge(d_sg, seen + f - 1)
                        for j in range(KD):
                            a = (2 * (f % 2)) * SLAB + j * P
                            mm = pe.matmul(psum[:, f % 2, 0:T], all_w[:, f // 2, a:a + P], h[:, j, :],
                                           start=(j == 0), stop=(j == KD - 1))
                        mm.then_inc(d_gate, 1)
                        if f >= 2:
                            pe.wait_ge(d_hid, seen + f - 1)
                        for j in range(KD):
                            a = (2 * (f % 2) + 1) * SLAB + j * P
                            mm = pe.matmul(psum[:, 2 + f % 2, 0:T], all_w[:, f // 2, a:a + P], h[:, j, :],
                                           start=(j == 0), stop=(j == KD - 1))
                        mm.then_inc(d_up, 1)
                    pe.wait_ge(d_hid, seen + FC)
                    for j in range(KD):
                        if j >= 4:
                            pe.wait_ge(d_added, seen * 2 + j - 3)
                        for f in range(FC):
                            mm = pe.matmul(psum[:, 4 + j % 4, 0:T], all_w[:, 2, f * D + j * P:f * D + (j + 1) * P],
                                           all_hidden[:, f, :], start=(f == 0), stop=(f == FC - 1))
                        mm.then_inc(d_down, 1)

            pe.wait_ge(s_const, 48)
            for L in range(DEPTH):
                mixer(L)
                attention(L)
                moe(L)

        @block.scalar
        def _(act):
            def square(L, k, j):
                if k == 0:
                    dst = h[:, j, :]
                else:
                    dst = squares[:, j % 2, :]
                    if j >= 2:
                        act.wait_ge(s_acc, (L * 2 + k - 1) * (KD - 2) + max(1, j - 2))
                act.activation(dst, x[:, j, :], ACT.Square, scale=D ** -0.5).then_inc(s_sq, 1)
                if j == KD - 2:
                    warm()

            def warm():
                act.activation(table[0:1, 0:1], k_("eps", 1, 1), ACT.Ln)

            def inverse_rms(L, k):
                act.wait_ge(s_sum, L * NNORM + k + 1)
                act.activation(rstd[:], psum[:, SUM_BANK[k], 0:T], ACT.Ln, bias=k_("eps", 1))
                act.drain()
                act.activation(rstd[:], rstd[:], ACT.Exp, scale=-0.5).then_inc(s_rstd, 1)

            def mixer(L):
                if L == 0:
                    for j in range(KD):
                        square(L, 0, j)
                inverse_rms(L, 0)
                n_evac = 0
                n_mem = 0

                def memory(chunks):
                    nonlocal n_mem
                    for _ in range(chunks):
                        c = n_mem
                        act.wait_ge(s_mkv, L * 16 + c + 1)
                        dst = k_mem[:, c, :] if c < KD else vt_mem[:, c - KD, :]
                        src = psum[:, c, 0:M] if c < 2 else psum[:, 4, M:2 * M]
                        act.activation(dst, src, ACT.Copy).then_inc(s_mkvout, 1)
                        n_mem += 1
                nt = 0

                def evac(dst, func=ACT.Copy, rows_=P, banks=4):
                    nonlocal n_evac
                    act.wait_ge(s_proj, L * 45 + n_evac + 1)
                    act.activation(dst, psum[0:rows_, n_evac % banks, 0:T], func).then_inc(s_evac, 1)
                    n_evac += 1

                def turned(dst, n, width):
                    nonlocal nt
                    if nt < 9 or nt % 2 == 0:
                        act.wait_ge(s_t, L * 19 + nt + 1)
                        act.activation(dst, psum[0:n, 4 + nt % 4, 0:width], ACT.Copy).then_inc(s_tout[nt % 2], 1)
                    nt += 1

                for c in range(8):
                    evac(zv[:, c, :])
                for c in range(8):
                    evac(kq[:, c, :])
                for c in range(CC):
                    act.wait_ge(s_proj, L * 45 + n_evac + 1)
                    b = n_evac % 4
                    act.activation(raw[:, c, CW - 1:XS0], psum[:, b, 0:SEQ], ACT.Copy)
                    act.activation(raw[:, c, XS0:XW].rearrange("p (b j) -> p b j", b=DB)[:, :, CW - 1:],
                                   psum[:, b, SEQ:T].rearrange("p (b j) -> p b j", b=DB), ACT.Copy)\
                        .then_inc(s_evac, 1)
                    n_evac += 1
                evac(dt_tmp[0:H, 0, :], rows_=H)
                act.wait_ge(s_dtv, L * 4 + 1)
                act.activation(dt_tmp[0:H, 2, :], dt_tmp[0:H, 1, :], ACT.Exp, scale=-1.0).then_inc(s_dta, 1)
                act.activation(keep[0:H, 0:1], par[0:H, L, PAT["a_log"]:PAT["a_log"] + 1], ACT.Exp)
                act.wait_ge(s_dtv, L * 4 + 2)
                act.activation(dt_tmp[0:H, 4, :], dt_tmp[0:H, 3, :], ACT.Ln)
                act.drain().then_inc(s_dta, 1)
                for t in range(3):
                    for half in range(2):
                        turned(v_tok[0:TOKN[t], t, half * BANK:(half + 1) * BANK], TOKN[t], BANK)
                for c in range(8):
                    evac(zv[:, c, :], ACT.Silu)
                    if c == 3:
                        for t in range(3):
                            turned(k_tok[0:TOKN[t], t, :], TOKN[t], BANK)
                    for cc in range(c * 3 // 2, (c + 1) * 3 // 2):
                        act.wait_ge(s_conv, L * CC + cc + 1)
                        a = conv_acc[:, cc % 2, :]
                        act.activation(xbc[:, cc, 0:SEQ], a[:, 0:SEQ], ACT.Silu)
                        act.activation(xbc[:, cc, SEQ:T - DS].rearrange("p (b j) -> p b j", b=DB - 1),
                                       a[:, XS0:XS0 + 77].rearrange("p (b j) -> p b j", b=DB - 1)[:, :, 0:DS],
                                       ACT.Silu)
                        act.activation(xbc[:, cc, T - DS:T], a[:, XS0 + 77:XOUT], ACT.Silu).then_inc(s_silu, 1)
                for t in range(3):
                    for half in range(2):
                        if t == 0 and half == 0:
                            act.wait_ge(s_silu, (L + 1) * CC)
                        turned(x_tok[0:TOKN[t], t, half * BANK:(half + 1) * BANK], TOKN[t], BANK)
                for t in range(3):
                    turned(b_tok[0:TOKN[t], t, :], TOKN[t], G * N)
                act.wait_ge(s_t, L * 19 + nt + 1)
                b = 4 + nt % 4
                for i, dst in enumerate((dt_tok, acum_tok)):
                    act.activation(dst[:, 0:2, :], psum[:, b, 3 * i * H:(3 * i + 2) * H]
                                   .rearrange("p (t h) -> p t h", t=2), ACT.Copy)
                    act.activation(dst[0:NS, 2, :], psum[0:NS, b, (3 * i + 2) * H:(3 * i + 3) * H], ACT.Copy)
                act.drain().then_inc(s_tout[nt % 2], 1)
                nt += 1
                act.wait_ge(s_raw_free, L + 1)
                for step in range(10):
                    t = min(step // 4, 2)
                    i = step - 4 * t
                    n = TOKN[t]
                    hb, banks = heads_of(t)
                    act.wait_ge(s_diff, L * 10 + step + 1)
                    dec = decays_of[step % 2]
                    if t == 1:
                        act.activation(dec[:, 1, :], psum[:, (5, 7)[step % 2], :], ACT.Exp)
                    act.activation(dec[0:n, 0, :], dec[0:n, 0, :], ACT.Exp)
                    act.drain().then_inc(s_exp, 1)
                    if step < KD:
                        evac(gate[:, step, :], banks=2)
                    else:
                        memory(1)
                    if step == 4:
                        act.wait_ge(s_cs, L * 2 + 1)
                        act.activation(states_out[:, 0, 0:1024].rearrange("p (a b) -> p a b", a=2),
                                       psum[:, 2:4, :], ACT.Copy).then_inc(s_csout, 1)
                    if i < banks - 1:
                        continue
                    act.wait_ge(s_dec, L * 3 + t + 1)
                    act.activation(decay_end[0:n, :], decay_end[0:n, :], ACT.Exp)
                    if t == 2:
                        act.activation(last_s[:], last_s[:], ACT.Exp)
                        act.activation(grown[0:n, :], acum_tok[0:n, 2, :], ACT.Exp)
                    else:
                        act.activation(keep[:], last[:, t % 2], ACT.Exp)
                    act.drain().then_inc(s_dece, 1)
                for t in range(3):
                    memory(1)
                    if t < 2:
                        act.wait_ge(s_o, L * 2 + t + 1)
                        act.activation(kq[:, :, tok(t)].rearrange("p (a b) t -> p a b t", a=2),
                                       psum[:, 2:4, :].rearrange("p a (b t) -> p a b t", b=4), ACT.Copy)\
                            .then_inc(s_oout, 1)
                    if t == 0:
                        act.wait_ge(s_kv, L * 2 + 1)
                        act.activation(states_out[:, 0, 1024:2048].rearrange("p (a b) -> p a b", a=2),
                                       psum[:, 0:2, :], ACT.Copy).then_inc(s_kvout, 1)
                memory(5)
                act.activation(gate[:], gate[:], ACT.Silu)
                warm()
                act.wait_ge(s_batch, (L + 1) * DB)
                act.activation(kq[:, :, tok(2)], psum[:, 7, :].rearrange("p (c t) -> p c t", c=KD), ACT.Copy)
                memory(1)
                act.wait_ge(s_gated, L * 2 + 1)
                act.activation(h[:, :, 0:SEQ], xbc[:, 0:KD, 0:SEQ], ACT.Square, scale=DV ** -0.5)
                act.wait_ge(s_gated, L * 2 + 2)
                act.activation(h[:, :, tok(2)], xbc[:, 0:KD, tok(2)], ACT.Square, scale=DV ** -0.5).then_inc(s_sq6, 1)
                memory(2)
                act.wait_ge(s_sum6, L * 2 + 1)
                act.drain()
                act.activation(h[:], kq[:], ACT.Square, scale=DV ** -0.5).then_inc(s_sq6, 1)
                act.activation(rstd6[:, 0:2, :], psum[:, 0:2, 0:T], ACT.Ln, bias=k_("eps", 1))
                act.drain()
                act.activation(rstd6[:, 0:2, :], rstd6[:, 0:2, :], ACT.Exp, scale=-0.5).then_inc(s_rstd6, 1)
                memory(1)
                act.wait_ge(s_sum6, L * 2 + 2)
                for at in (2, 5):
                    o = 2 if at == 2 else 4
                    act.activation(rstd6[:, o:o + 2, :], psum[:, at:at + 2, 0:T], ACT.Ln, bias=k_("eps", 1))
                act.drain()
                act.activation(rstd6[:, 2:6, :], rstd6[:, 2:6, :], ACT.Exp, scale=-0.5).then_inc(s_rstd6, 1)
                memory(16 - n_mem)
                for j in range(KD):
                    act.wait_ge(s_xadd, L * 16 + j + 1)
                    square(L, 1, j)
                inverse_rms(L, 1)

            def attention(L):
                for i in range(4):
                    act.wait_ge(s_vt, L * 4 + i + 1)
                    act.activation(v_mem[:, i // 2, (i % 2) * BANK:(i % 2 + 1) * BANK], psum[:, 4 + i % 2, :],
                                   ACT.Copy).then_inc(s_vtout, 1)
                act.wait_ge(s_qzero, L + 1)
                for c in range(KD):
                    act.wait_ge(s_q, L * KD + c + 1)
                    act.activation(q_p[:, c, :], psum[:, c % 4, 0:SEQ], ACT.Copy)
                    act.activation(own_blocks(q_own[:, c, :]),
                                   psum[:, c % 4, SEQ:T].rearrange("p (b j) -> p b j", b=DB), ACT.Copy)\
                        .then_inc(s_qout, 1)

                def exps(t):
                    n = TOKN[t]
                    act.wait_ge(s_xmax, L * 3 + t + 1)
                    for r in range(XH):
                        b = 2 * t + r // 2
                        act.activation(prob[0:n, t, r, :], psum[0:n, b, (r % 2) * M:(r % 2 + 1) * M], ACT.Exp,
                                       bias=xmax[0:n, t, r:r + 1], scale=1.0 / 16, accum_out=xsum[0:n, t, r:r + 1])
                    act.drain().then_inc(s_xexp, 1)

                exps(0)
                exps(1)
                np_ = 0

                def probs(t):
                    nonlocal np_
                    for half in range(2):
                        act.wait_ge(s_pt, L * 6 + np_ + 1)
                        src = psum[:, 6 + np_ % 2, :]
                        if t < 2:
                            act.activation(prob_t[:, 2 * half:2 * half + 2, :, tok(t)],
                                           src.rearrange("p (r c t) -> p r c t", r=2, c=2), ACT.Copy)\
                                .then_inc(s_ptout, 1)
                        else:
                            for i in range(4):
                                ins = act.activation(own_blocks(prob_own[:, 2 * half + i // 2, i % 2, :]),
                                                     src[:, i * P:i * P + NS].rearrange("p (b j) -> p b j", b=DB),
                                                     ACT.Copy)
                            ins.then_inc(s_ptout, 1)
                        np_ += 1

                probs(0)
                probs(1)
                exps(2)
                for j in range(KD):
                    act.wait_ge(s_xo, L * 9 + j + 1)
                    act.activation(h[:, j, 0:SEQ], psum[:, j % 4, 0:SEQ], ACT.Copy).then_inc(s_xoout, 1)
                    if j == 3:
                        act.wait_ge(s_pzero, L + 1)
                        probs(2)
                act.wait_ge(s_xo, (L + 1) * 9)
                act.activation(o_tok[0:NS, :].rearrange("p (a b) -> p a b", a=2), psum[0:NS, 4:6, :], ACT.Copy)\
                    .then_inc(s_otok, 1)
                act.wait_ge(s_ott, L + 1)
                act.activation(h[:, :, SEQ:T], psum[:, 6, :].rearrange("p (c t) -> p c t", c=KD), ACT.Copy)\
                    .then_inc(s_xoout, 1)
                for j in range(KD):
                    act.wait_ge(s_xadd, L * 16 + KD + j + 1)
                    square(L, 2, j)
                inverse_rms(L, 2)

            def moe(L):
                for i in range(6):
                    t, half = i % 3, i // 3
                    act.wait_ge(s_ht, L * 6 + i + 1)
                    act.activation(h_tok[0:TOKN[t], t, half * BANK:(half + 1) * BANK],
                                   psum[0:TOKN[t], i % 2, :], ACT.Copy).then_inc(s_htout, 1)
                act.wait_ge(s_rv, 2 * L + 2)
                act.activation(gtmp, gtmp, ACT.Exp)
                act.activation(mt, mt, ACT.Exp)
                act.drain().then_inc(s_ra, 1)
                for j in range(KD):
                    act.wait_ge(s_pack, L * KD + j + 1)
                    act.activation(h_packed[:, j, :, :], psum[:, j % 4, :].rearrange("p (g c) -> p g c", g=EG),
                                   ACT.Copy).then_inc(s_packout, 1)
                act.wait_ge(s_gs, L + 1)
                act.activation(slot_gates, psum[:, 4, 0:E].rearrange("p (g e) -> p g e", g=EG), ACT.Copy)\
                    .then_inc(s_gsout, 1)
                with act.Fori(0, EG) as g:
                    for u in range(EPG):
                        seen = (L * E + g * EPG + u) * 2
                        for q in range(2):
                            act.wait_ge(s_gate, seen + q + 1)
                            act.activation(silu_gate[:, q, :], psum[:, q, 0:2 * CAP], ACT.Silu).then_inc(s_sg, 1)
                act.wait_ge(s_spilt, L + 1)
                with act.If(act.value_load(spilt[0:1, L:L + 1], min_val=0, max_val=1) > 0):
                    act.wait_ge(d_gt, L + 1)
                    act.activation(gate_row[0:E, :], psum[0:E, 5, 0:T], ACT.Copy).then_inc(d_grow, 1)
                    for e in range(E):
                        act.wait_ge(d_gb, L * E + e + 1)
                        act.activation(all_gates[:, e, :], psum[:, 6 + e % 2, 0:T], ACT.Copy).then_inc(d_gbout, 1)
                    with act.Fori(0, E) as e:
                        for f in range(FC):
                            act.wait_ge(d_gate, (L * E + e) * FC + f + 1)
                            if f >= 2:
                                act.wait_ge(d_hid, (L * E + e) * FC + f - 1)
                            act.activation(all_silu[:, f % 2, :], psum[:, f % 2, 0:T], ACT.Silu).then_inc(d_sg, 1)
                    act.wait_ge(d_end, L + 1)
                with act.Else():
                    for sm, n in ((d_grow, 1), (d_gbout, E), (d_sg, E * FC)):
                        act.sem_inc(sm, n)
                for j in range(KD):
                    act.wait_ge(s_added, (L * EG + EG - 1) * KD + j + 1)
                    square(L + 1, 0, j)

            act.wait_ge(s_const, 48)
            for L in range(DEPTH):
                mixer(L)
                attention(L)
                moe(L)
            inverse_rms(DEPTH, 0)

        @block.vector
        def _(dve):
            def normed(L, k, gain, dst=h):
                dve.wait_ge(s_rstd, L * NNORM + k + 1)
                for j in range(KD):
                    a = PAT[gain] + j
                    ins = dve.scalar_tensor_tensor(out=dst[:, j, :], in0=x[:, j, :], scalar=par[:, min(L, 1), a:a + 1],
                                                   in1=rstd[:], op0=ALU.mult, op1=ALU.mult)
                    ins.then_inc(s_h, 1)

            def add_to_x(L, k):
                for j in range(KD):
                    dve.wait_ge(s_wout, (L * 2 + k - 1) * KD + j + 1)
                    dve.tensor_tensor(x[:, j, :], x[:, j, :], psum[:, j % 4, 0:T], ALU.add).then_inc(s_xadd, 1)
                    if j >= 2:
                        dve.wait_ge(s_sq, (L * NNORM + k) * KD + j)
                        dve.drain()
                        so_far = squares[:, 0, :] if j == 2 else rstd[:]
                        dve.tensor_tensor(rstd[:], so_far, squares[:, (j - 1) % 2, :], ALU.add).then_inc(s_acc, 1)

            def mixer(L):
                normed(L, 0, "norm_mix")
                dve.wait_ge(s_tables, 16)
                for j in range(2 * RH):
                    dve.wait_ge(s_rot, L * 8 + j + 1)
                    tmp = rot_tmp[:, j % 2, :]
                    dve.tensor_tensor(tmp, psum[:, 4 + j % 2, 0:T], k_("sin", T), ALU.mult)
                    dve.tensor_tensor(kq[:, j, :], kq[:, j, :], k_("cos", T), ALU.mult)
                    dve.drain()
                    dve.tensor_tensor(kq[:, j, :], kq[:, j, :], tmp, ALU.add).then_inc(s_rotated, 1)
                w = quad(dve, L, Q_DT)
                dve.memset(raw[:, :, 0:CW - 1], 0.0)
                for c in range(CC):
                    a = KD * H + c * DB * (CW - 1)
                    dve.tensor_copy(raw[:, c, XS0:XW].rearrange("p (b j) -> p b j", b=DB)[:, :, 0:CW - 1],
                                    w[:, a:a + DB * (CW - 1)].rearrange("p (b j) -> p b j", b=DB))
                dve.wait_ge(s_proj, L * 45 + 29)
                dve.drain().then_inc(freed[Q_DT % RING], 1)
                d = [dt_tmp[0:H, i, :] for i in range(6)]
                dve.wait_ge(s_evac, L * 45 + 29)
                dve.tensor_scalar(d[0], d[0], par[0:H, L, PAT["dt_bias"]:PAT["dt_bias"] + 1], None, ALU.add)
                dve.drain()
                dve.scalar_tensor_tensor(out=d[1], in0=d[0], scalar=-1.0, in1=d[0], op0=ALU.mult, op1=ALU.max)
                dve.drain().then_inc(s_dtv, 1)
                dve.wait_ge(s_dta, L * 2 + 1)
                dve.tensor_scalar(d[3], d[2], 1.0, None, ALU.add)
                dve.drain().then_inc(s_dtv, 1)
                dve.wait_ge(s_dta, L * 2 + 2)
                dve.reciprocal(d[5], d[3])
                dve.tensor_scalar(d[3], d[3], -1.0, 1e-30, ALU.add, ALU.max)
                dve.drain()
                dve.reciprocal(d[3], d[3])
                dve.tensor_tensor(d[4], d[4], d[2], ALU.mult)
                dve.tensor_tensor(d[5], d[5], d[2], ALU.mult)
                dve.drain()
                dve.tensor_tensor(d[4], d[4], d[3], ALU.mult)
                dve.drain()
                dve.tensor_tensor(d[4], d[4], d[5], ALU.max)
                dve.drain()
                dve.scalar_tensor_tensor(out=dt_row[0:H, :], in0=d[0], scalar=0.0, in1=d[4], op0=ALU.max, op1=ALU.add)
                dve.drain()
                dve.tensor_scalar(d[1], dt_row[0:H, :], keep[0:H, 0:1], -1.0, ALU.mult, ALU.mult)
                dve.drain().then_inc(s_dtv, 1)
                dve.tensor_tensor_scan(acum_row[0:H, :], k_("restart", T, H), d[1], 0.0, ALU.mult, ALU.add)\
                    .then_inc(s_dtv, 1)
                for c in range(CC):
                    dve.wait_ge(s_evac, L * 45 + 16 + c + 1)
                    if c >= 2:
                        dve.wait_ge(s_silu, L * CC + c - 1)
                    a = conv_acc[:, c % 2, :]
                    wa, ba = PAT["conv_w"] + c * CW, PAT["conv_b"] + c
                    dve.tensor_scalar(a, raw[:, c, 0:XOUT], par[:, L, wa:wa + 1], par[:, L, ba:ba + 1],
                                      ALU.mult, ALU.add)
                    for j in range(1, CW):
                        dve.drain()
                        ins = dve.scalar_tensor_tensor(out=a, in0=raw[:, c, j:j + XOUT],
                                                       scalar=par[:, L, wa + j:wa + j + 1], in1=a,
                                                       op0=ALU.mult, op1=ALU.add)
                    ins.then_inc(s_conv, 1)
                dve.tensor_copy(conv_tail[:, :, 0:CW - 1], raw[:, :, XS0 - (CW - 1):XS0])
                for b in range(DB):
                    e = XS0 + (b + 1) * (CW - 1 + DS)
                    dve.tensor_copy(conv_tail[:, :, (b + 1) * (CW - 1):(b + 2) * (CW - 1)],
                                    raw[:, :, e - (CW - 1):e])
                dve.drain().then_inc(s_raw_free, 1)

                dve.wait_ge(s_silu, (L + 1) * CC)
                outs = [(x_tok, t, half * BANK, BANK) for t in range(3) for half in range(2)]
                outs += [(b_tok, t, 0, G * N) for t in range(3)]
                for i in range(9, 18):
                    if i % 2 == 1:
                        dst, t, at, width = outs[i - 9]
                        dve.wait_ge(s_t, L * 19 + i + 1)
                        dve.tensor_copy(dst[0:TOKN[t], t, at:at + width], psum[0:TOKN[t], 4 + i % 4, 0:width])\
                            .then_inc(s_tout[1], 1)
                dve.wait_ge(s_tout[0], turned_by(L, 18))
                dve.wait_ge(s_evac, L * 45 + 37)

                def head_rows_of(step):
                    t, i = min(step // 4, 2), step - 4 * min(step // 4, 2)
                    hb, n = heads_of(t)[0], TOKN[t]
                    dve.tensor_tensor(rows[0:H, :].rearrange("p (h l) -> p h l", h=hb),
                                      acum_row[0:H, tok(t)].unsqueeze(1).broadcast_to([H, hb, n]),
                                      ident[0:H, i * hb:(i + 1) * hb].unsqueeze(2).broadcast_to([H, hb, n]), ALU.mult)\
                        .then_inc(s_rows, 1)

                def add_skip(step):
                    t, i = min(step // 4, 2), step - 4 * min(step // 4, 2)
                    hb, n = heads_of(t)[0], TOKN[t]
                    dve.wait_ge(s_y, L * 10 + step + 1)
                    for c in range(hb // 2):
                        ch = i * hb // 2 + c
                        a = PAT["d_skip"] + ch
                        ins = dve.scalar_tensor_tensor(out=xbc[:, ch, tok(t)], in0=xbc[:, ch, tok(t)],
                                                       scalar=par[:, L, a:a + 1], in1=psum[:, 6, c * n:(c + 1) * n],
                                                       op0=ALU.mult, op1=ALU.add)
                    ins.then_inc(s_yout, 1)

                def differences(step):
                    t, i = min(step // 4, 2), step - 4 * min(step // 4, 2)
                    hb, n = heads_of(t)[0], TOKN[t]
                    h0 = i * hb
                    if step >= 2:
                        dve.wait_ge(s_y, L * 10 + step - 1)
                    bc = psum[:, (5, 7)[step % 2], :].rearrange("p (h l) -> p h l", h=hb)
                    e = decays_of[step % 2][0:n, 0, :].rearrange("p (h l) -> p h l", h=hb)
                    for hh in range(hb):
                        dve.tensor_scalar(e[:, hh, :], bc[0:n, hh, :], acum_tok[0:n, t, h0 + hh:h0 + hh + 1],
                                          0.0, ALU.subtract, ALU.min)
                    if t < 2:
                        dve.tensor_copy(last[:, t % 2, h0:h0 + hb], bc[:, :, n - 1])
                    else:
                        dve.tensor_copy(last_s[:, h0:h0 + hb, :],
                                        bc.rearrange("p h (b j) -> p h b j", b=DB)[:, :, :, DS - 1])
                    dve.drain().then_inc(s_diff, 1)

                def times_dt(t):
                    n = TOKN[t]
                    xt = x_tok[0:n, t, :].rearrange("p (h d) -> p h d", h=H)
                    dve.tensor_tensor(xt, xt, dt_tok[0:n, t, :].unsqueeze(2).broadcast_to([n, H, HD]), ALU.mult)

                head_rows_of(0)
                times_dt(0)
                dve.wait_ge(s_bc, L * 10 + 1)
                head_rows_of(1)
                differences(0)
                for step in range(10):
                    t, i = min(step // 4, 2), step - 4 * min(step // 4, 2)
                    n = TOKN[t]
                    hb, banks = heads_of(t)
                    if i == 0:
                        dve.wait_ge(s_cb, L * 3 + t + 1)
                        mask = k_("causal", P) if t < 2 else k_("causal_s", NS, NS)
                        dve.tensor_tensor(cbm[0:n, :, 0:n],
                                          psum[0:n, 4, 0:G * P].rearrange("p (g l) -> p g l", g=G)[:, :, 0:n],
                                          mask.unsqueeze(1).broadcast_to([n, G, n]), ALU.mult)
                    if step + 1 < 10:
                        dve.wait_ge(s_bc, L * 10 + step + 2)
                        if step + 2 < 10:
                            head_rows_of(step + 2)
                        differences(step + 1)
                    if step > 0:
                        add_skip(step - 1)
                    dve.wait_ge(s_exp, L * 10 + step + 1)
                    dve.drain()
                    g0 = i * hb * G // H
                    e, cd = [decays_of[step % 2][:, k, :].rearrange("p (h l) -> p h l", h=hb) for k in range(2)]
                    dve.tensor_tensor(e[0:n], e[0:n], cbm[0:n, g0, 0:n].unsqueeze(1).broadcast_to([n, hb, n]), ALU.mult)
                    if t == 1:
                        dve.tensor_tensor(cd, cd, xbc[:, 10 + g0, tok(t)].unsqueeze(1)
                                          .broadcast_to([P, hb, n]), ALU.mult)
                    dve.drain().then_inc(s_lm, 1)
                    if i == 2:
                        times_dt(t + 1)
                    if step == KD:
                        dve.wait_ge(s_cs, L * 2 + 2)
                        st = states_out[:, 0, 0:1024].rearrange("p (a b) -> p a b", a=2)
                        dve.tensor_tensor(st, st, psum[:, 2:4, :], ALU.add).then_inc(s_csout, 1)
                    if i < banks - 1:
                        continue
                    if t < 2:
                        dve.tensor_tensor(decay_end[0:n, :], last[0:n, t % 2, :], acum_tok[0:n, t, :], ALU.subtract)
                    else:
                        dve.tensor_tensor(last_own[0:n], last_s[0:n],
                                          k_("own", DB, NS).unsqueeze(1).broadcast_to([n, H, DB]), ALU.mult)
                        dve.drain()
                        dve.tensor_reduce(decay_end[0:n, :], last_own[0:n], AX.X, ALU.add)
                        dve.drain()
                        dve.tensor_tensor(decay_end[0:n, :], decay_end[0:n, :], acum_tok[0:n, t, :], ALU.subtract)
                    dve.drain().then_inc(s_dec, 1)
                    dve.wait_ge(s_dece, L * 3 + t + 1)
                    dve.wait_ge(s_y, L * 10 + step + 1)
                    xt = x_tok[0:n, t, :].rearrange("p (h d) -> p h d", h=H)
                    dve.tensor_tensor(xt, xt, decay_end[0:n, :].unsqueeze(2).broadcast_to([n, H, HD]), ALU.mult)\
                        .then_inc(s_xdec, 1)
                    if t == 1:
                        st = states_out[:, 0, 0:1024].rearrange("p (h d) -> p h d", h=H)
                        dve.tensor_tensor(st, st, keep[:].unsqueeze(2).broadcast_to([P, H, HD]), ALU.mult)
                add_skip(9)
                dve.wait_ge(s_evac, (L + 1) * 45)
                dve.memset(c_own, 0.0)
                dve.drain()
                for g in range(G):
                    dve.tensor_copy(own_blocks(c_own[:, g, :]),
                                    xbc[:, 10 + g, tok(2)].rearrange("p (b j) -> p b j", b=DB))

                for t in range(3):
                    n = TOKN[t]
                    dve.wait_ge(s_score, L * 3 + t + 1)
                    sfx = "" if t < 2 else "_s"
                    e = decays[0:n, 0, 0:RH * n]
                    dve.tensor_tensor(e, psum[0:n, 5, 0:RH * n], k_("decay" + sfx, RH * n, n), ALU.mult)
                    if t > 0:
                        qd = decays[:, 1, :].rearrange("p (h l) -> p h l", h=RH) if t == 1 else q_dec_s
                        dve.tensor_tensor(qd, kq[:, RH:2 * RH, tok(t)],
                                          k_("qdecay" + sfx, RH * n).rearrange("p (h l) -> p h l", h=RH), ALU.mult)
                    kt = k_tok[0:n, t, :].rearrange("p (h d) -> p h d", h=RH)
                    dve.tensor_tensor(kt, kt, k_("kend" + sfx, RH, n).unsqueeze(2).broadcast_to([n, RH, DK]), ALU.mult)
                    dve.drain().then_inc(s_decayed, 1)
                    if t == 1:
                        dve.wait_ge(s_kv, L * 2 + 2)
                        for r in range(RH):
                            st = states_out[:, 0, 1024 + r * DV:1024 + (r + 1) * DV]
                            dve.scalar_tensor_tensor(out=st, in0=st, scalar=float(gam[r] ** P),
                                                     in1=psum[:, r // 2, (r % 2) * DV:(r % 2 + 1) * DV],
                                                     op0=ALU.mult, op1=ALU.add)
                        dve.drain().then_inc(s_kvout, 1)

                for b in range(DB):
                    if b > 0:
                        dve.wait_ge(s_batch, L * DB + b)
                    own = k_("own", 1, NS, b)
                    dve.tensor_scalar(b_own[0:NS, :], b_tok[0:NS, 2, :], own, None, ALU.mult)
                    dve.tensor_scalar(k_own[0:NS, :], k_tok[0:NS, 2, :], own, None, ALU.mult)
                    dve.drain().then_inc(s_own, 1)
                    w = quad(dve, L, Q_STATE[b // 2])
                    ws = w[:, (b % 2) * 2048:(b % 2 + 1) * 2048]
                    slot = (b + 1) % 2
                    if b >= 1:
                        dve.wait_ge(s_store[slot], 16 * (L * (5 - slot) + (b + 1) // 2))
                    so = states_out[:, slot, :]
                    dve.tensor_tensor(so[:, 0:1024].rearrange("p (h d) -> p h d", h=H),
                                      ws[:, 0:1024].rearrange("p (h d) -> p h d", h=H),
                                      last_s[:, :, b].unsqueeze(2).broadcast_to([P, H, HD]), ALU.mult)
                    dve.wait_ge(s_batch, L * DB + b + 1)
                    for r in range(RH):
                        dve.scalar_tensor_tensor(out=so[:, 1024 + r * DV:1024 + (r + 1) * DV],
                                                 in0=ws[:, 1024 + r * DV:1024 + (r + 1) * DV],
                                                 scalar=float(gam[r] ** DS),
                                                 in1=psum[:, 2 + r // 2, (r % 2) * DV:(r % 2 + 1) * DV],
                                                 op0=ALU.mult, op1=ALU.add)
                    dve.drain()
                    so2 = so[:, 0:1024].rearrange("p (a b) -> p a b", a=2)
                    dve.tensor_tensor(so2, so2, psum[:, 0:2, :], ALU.add)
                    dve.drain().then_inc(s_newst, 1)
                    if b % 2 == 1:
                        dve.drain().then_inc(freed[(Q_STATE[b // 2]) % RING], 1)
                dve.wait_ge(s_off, L + 1)
                dve.tensor_tensor(x_tok[0:NS, 2, :].rearrange("p (g h d) -> p g h d", g=G, h=H // G),
                                  psum[0:NS, 5:7, :].rearrange("p g (h d) -> p g h d", h=H // G),
                                  grown[0:NS, :].rearrange("p (g h) -> p g h", g=G).unsqueeze(3)
                                  .broadcast_to([NS, G, H // G, HD]), ALU.mult).then_inc(s_offtok, 1)
                dve.tensor_tensor(xbc[:, 0:KD, 0:SEQ], xbc[:, 0:KD, 0:SEQ], zv[:, :, 0:SEQ], ALU.mult)\
                    .then_inc(s_gated, 1)
                dve.wait_ge(s_offt, L + 1)
                dve.tensor_tensor(xbc[:, 0:KD, tok(2)], xbc[:, 0:KD, tok(2)],
                                  psum[:, 6, :].rearrange("p (c t) -> p c t", c=KD), ALU.add)
                dve.drain()
                dve.tensor_tensor(xbc[:, 0:KD, tok(2)], xbc[:, 0:KD, tok(2)], zv[:, :, tok(2)], ALU.mult)\
                    .then_inc(s_gated, 1)
                dve.wait_ge(s_sq6, L * 2 + 1)
                hg = h[:].rearrange("p (g i) t -> p g i t", g=G)
                dve.tensor_tensor(hg[:, :, 0:2, :], hg[:, :, 0:2, :], hg[:, :, 2:4, :], ALU.add).then_inc(s_pair6, 1)
                dve.wait_ge(s_sq6, L * 2 + 2)
                hr = h[:].rearrange("p (r i) t -> p r i t", r=RH)
                dve.tensor_tensor(hr[:, :, 0, :], hr[:, :, 0, :], hr[:, :, 1, :], ALU.add).then_inc(s_pair6, 1)
                dve.wait_ge(s_rstd6, L * 2 + 1)
                for c in range(KD):
                    a = PAT["ssd_gain"] + c
                    ins = dve.scalar_tensor_tensor(out=xbc[:, c, :], in0=xbc[:, c, :], scalar=par[:, L, a:a + 1],
                                                   in1=rstd6[:, c // 4, :], op0=ALU.mult, op1=ALU.mult)
                ins.then_inc(s_mix, 1)
                dve.wait_ge(s_rstd6, L * 2 + 2)
                for c in range(KD):
                    a = PAT["ret_gain"] + c
                    dve.scalar_tensor_tensor(out=kq[:, c, :], in0=kq[:, c, :], scalar=par[:, L, a:a + 1],
                                             in1=rstd6[:, 2 + c // 2, :], op0=ALU.mult, op1=ALU.mult)
                dve.drain()
                dve.tensor_tensor(kq[:], kq[:], gate[:], ALU.mult).then_inc(s_mix, 1)
                add_to_x(L, 1)

            def attention(L):
                normed(L, 1, "norm_mem")

                def maxima(t):
                    n = TOKN[t]
                    dve.wait_ge(s_xs, L * 3 + t + 1)
                    dve.tensor_reduce(xmax[0:n, t, :],
                                      psum[0:n, 2 * t:2 * t + 2, :].rearrange("p a (b m) -> p a b m", b=2),
                                      AX.X, ALU.max)
                    dve.drain()
                    dve.tensor_scalar(xmax[0:n, t, :], xmax[0:n, t, :], -1.0 / 16, None, ALU.mult).then_inc(s_xmax, 1)

                def probabilities(t):
                    n = TOKN[t]
                    dve.wait_ge(s_xexp, L * 3 + t + 1)
                    dve.reciprocal(xsum[0:n, t, :], xsum[0:n, t, :])
                    dve.drain()
                    dve.tensor_tensor(prob[0:n, t], prob[0:n, t],
                                      xsum[0:n, t, :].unsqueeze(2).broadcast_to([n, XH, M]), ALU.mult)\
                        .then_inc(s_prob, 1)

                for t in range(2):
                    maxima(t)
                for t in range(2):
                    probabilities(t)
                maxima(2)
                probabilities(2)
                add_to_x(L, 2)

            def first_of(mask, vals, top, tmp):
                dve.tensor_tensor(mask, vals, top.unsqueeze(2).broadcast_to([P, 3, EPG]), ALU.is_equal)
                dve.drain()
                dve.tensor_tensor(mask, mask, k_("rank", EPG).unsqueeze(1).broadcast_to([P, 3, EPG]), ALU.mult)
                dve.drain()
                dve.tensor_reduce(tmp, mask, AX.X, ALU.max)
                dve.drain()
                dve.tensor_tensor(mask, mask, tmp.unsqueeze(2).broadcast_to([P, 3, EPG]), ALU.is_equal)
                dve.drain()

            def moe(L):
                for i in range(2):
                    dve.wait_ge(s_store[i], 16 * (5 - i) * (L + 1))
                dve.wait_ge(s_tstore, 16 * (L + 1))
                dve.wait_ge(s_mkstore, 16 * (L + 1))
                dve.wait_ge(s_mvstore, 16 * (L + 1))
                normed(L, 2, "norm_ffn")
                dve.memset(logits[:], 0.0)
                dve.drain()
                dve.wait_ge(s_route, L + 1)
                a = PAT["route_b"]
                for t in range(3):
                    n = TOKN[t]
                    dve.tensor_tensor(logits[0:n, t, :], psum[0:n, 6, t * 32:t * 32 + EG + E],
                                      par[0:n, L, a:a + EG + E], ALU.add)
                dve.drain()
                gl = logits[:, :, 0:EG]
                dve.tensor_reduce(gmax, gl, AX.X, ALU.max)
                dve.drain()
                first_of(gsel, gl, gmax, mt)
                dve.drain().then_inc(s_rv, 1)
                dve.tensor_tensor(gtmp, gl, gmax.unsqueeze(2).broadcast_to([P, 3, EG]), ALU.subtract)
                for t in range(3):
                    dve.tensor_tensor(epick[:, t], logits[:, t, EG:].rearrange("p (g e) -> p g e", g=EG),
                                      gsel[:, t, :].unsqueeze(2).broadcast_to([P, EG, EPG]), ALU.mult)
                dve.drain()
                dve.tensor_tensor(el, epick[:, :, 0, :], epick[:, :, 1, :], ALU.add)
                dve.drain()
                dve.tensor_tensor(el, el, epick[:, :, 2, :], ALU.add)
                dve.drain()
                dve.tensor_tensor(el, el, epick[:, :, 3, :], ALU.add)
                dve.wait_ge(s_cnt, L + 1)
                dve.memset(ranked, 0.0)
                dve.drain()
                for t in range(3):
                    n = TOKN[t]
                    dve.tensor_tensor(ranked[0:n, t, :], gsel[0:n, t, :], psum[0:n, 5, t * 32:t * 32 + EG], ALU.mult)
                dve.tensor_reduce(most, psum[:, 5, 96:96 + EG], AX.X, ALU.max)
                dve.drain()
                dve.tensor_reduce(slot, ranked, AX.X, ALU.max)
                dve.tensor_scalar(spilt[:, L:L + 1], most, float(CAP), None, ALU.is_gt)
                dve.drain().then_inc(s_spilt, 1)
                for t in range(3):
                    n = TOKN[t]
                    dve.tensor_tensor(chosen[0:n, t], k_("slots", CAP, n).unsqueeze(1).broadcast_to([n, EG, CAP]),
                                      ranked[0:n, t, :].unsqueeze(2).broadcast_to([n, EG, CAP]), ALU.is_equal)
                dve.drain().then_inc(s_chosen, 1)
                dve.tensor_reduce(m1, el, AX.X, ALU.max)
                dve.drain()
                first_of(e1, el, m1, mt)
                dve.scalar_tensor_tensor(out=el, in0=e1, scalar=-1e30, in1=el, op0=ALU.mult, op1=ALU.add)
                dve.drain()
                dve.tensor_reduce(m2, el, AX.X, ALU.max)
                dve.drain()
                first_of(e2, el, m2, mt)
                dve.tensor_tensor(mt, m2, m1, ALU.subtract)
                dve.drain().then_inc(s_rv, 1)
                dve.wait_ge(s_ra, L + 1)
                dve.tensor_reduce(gden, gtmp, AX.X, ALU.add)
                dve.tensor_scalar(w1, mt, 1.0, None, ALU.add)
                dve.drain()
                dve.tensor_tensor(w1, w1, gden, ALU.mult)
                dve.drain()
                dve.reciprocal(w1, w1)
                dve.drain()
                dve.tensor_tensor(w2, w1, mt, ALU.mult)
                dve.tensor_tensor(e1, e1, w1.unsqueeze(2).broadcast_to([P, 3, EPG]), ALU.mult)
                dve.drain()
                dve.tensor_tensor(e2, e2, w2.unsqueeze(2).broadcast_to([P, 3, EPG]), ALU.mult)
                dve.drain()
                dve.tensor_tensor(e1, e1, e2, ALU.add)
                dve.drain().then_inc(s_chosen, 1)
                dve.tensor_scalar(over, slot, float(CAP), None, ALU.is_gt)
                dve.drain()
                dve.tensor_tensor(e2, e1, over.unsqueeze(2).broadcast_to([P, 3, EPG]), ALU.mult)
                dve.drain()
                for t in range(3):
                    dve.tensor_tensor(spilt_gates[:, t], gsel[:, t, :].unsqueeze(2).broadcast_to([P, EG, EPG]),
                                      e2[:, t, :].unsqueeze(1).broadcast_to([P, EG, EPG]), ALU.mult)
                for g in range(EG):
                    dve.wait_ge(s_ct, L * EG + g + 1)
                    dve.tensor_copy(chosen_t[:, g, :], psum[:, 6 + g % 2, 0:T]).then_inc(s_ctout, 1)
                dve.wait_ge(s_packout, (L + 1) * KD)
                dve.wait_ge(s_gsout, L + 1)
                dve.drain()
                with dve.Fori(0, EG) as g:
                    dve.tensor_copy(group_gates, slot_gates[:, g, :])
                    dve.drain()
                    for u in range(EPG):
                        seen = (L * E + g * EPG + u) * 2
                        for q in range(2):
                            dve.wait_ge(s_up, seen + q + 1)
                            dve.wait_ge(s_sg, seen + q + 1)
                            dve.tensor_tensor(hidden[:, 2 * q:2 * q + 2, :],
                                              silu_gate[:, q, :].rearrange("p (f c) -> p f c", f=2),
                                              psum[:, 2 + q, 0:2 * CAP].rearrange("p (f c) -> p f c", f=2), ALU.mult)\
                                .then_inc(s_hid, 1)
                        for half in range(2):
                            dve.wait_ge(s_down, seen + half + 1)
                            y = y_group[:, half * BANK:(half + 1) * BANK]
                            if u == 0:
                                ins = dve.tensor_scalar(y, psum[:, 4 + half, :], group_gates[:, 0:1], None, ALU.mult)
                            else:
                                ins = dve.scalar_tensor_tensor(out=y, in0=psum[:, 4 + half, :],
                                                               scalar=group_gates[:, u:u + 1], in1=y,
                                                               op0=ALU.mult, op1=ALU.add)
                            if u == EPG - 1:
                                ins.then_inc(s_yg, 1)
                    for j in range(KD):
                        dve.wait_ge(s_spread, (L * EG + g) * KD + j + 1)
                        dve.tensor_tensor(x[:, j, :], x[:, j, :], psum[:, 6 + j % 2, 0:T], ALU.add)\
                            .then_inc(s_added, 1)
                with dve.If(dve.value_load(spilt[0:1, L:L + 1], min_val=0, max_val=1) > 0):
                    dve.drain().then_inc(d_start, 1)
                    dve.wait_ge(d_grow, L + 1)
                    for e in range(E):
                        if e >= 2:
                            dve.wait_ge(d_gb, L * E + e - 1)
                        dve.tensor_scalar(one_row[0:E, e % 2, :], gate_row[0:E, :], ident[0:E, e:e + 1], None,
                                          ALU.mult).then_inc(d_orow, 1)
                    with dve.Fori(0, E) as e:
                        seen = (L * E + e) * FC
                        for f in range(FC):
                            dve.wait_ge(d_up, seen + f + 1)
                            dve.wait_ge(d_sg, seen + f + 1)
                            sg = all_silu[:, f % 2, :]
                            dve.tensor_tensor(sg, sg, psum[:, 2 + f % 2, 0:T], ALU.mult)
                            dve.drain()
                            dve.tensor_tensor(all_hidden[:, f, :], sg, all_gates[:, e, :], ALU.mult)\
                                .then_inc(d_hid, 1)
                        for j in range(KD):
                            dve.wait_ge(d_down, seen * 2 + j + 1)
                            dve.tensor_tensor(x[:, j, :], x[:, j, :], psum[:, 4 + j % 4, 0:T], ALU.add)\
                                .then_inc(d_added, 1)
                        dve.drain().then_inc(d_start, 1)
                with dve.Else():
                    for sm, n in ((d_start, E + 1), (d_orow, E), (d_hid, E * FC), (d_added, E * KD)):
                        dve.sem_inc(sm, n)
                dve.drain().then_inc(d_end, 1)

            dve.wait_ge(s_const, 48)
            for L in range(DEPTH):
                mixer(L)
                attention(L)
                moe(L)
            normed(DEPTH, 0, "norm_final")

        @block.gpsimd
        def _(pool):
            for L in range(DEPTH):
                pool.wait_ge(s_raw_free, L + 1)
                pool.dma_start(conv_out[L], conv_tail[:]).then_inc(s_tstore, 16)
                pool.wait_ge(s_csout, L * 2 + 2)
                pool.wait_ge(s_kvout, L * 2 + 2)
                pool.dma_start(st_out[L, 0], states_out[:, 0, :]).then_inc(s_store[0], 16)
                for b in range(DB):
                    pool.wait_ge(s_newst, L * DB + b + 1)
                    pool.dma_start(st_out[L, 1 + b], states_out[:, (b + 1) % 2, :]).then_inc(s_store[(b + 1) % 2], 16)
                pool.wait_ge(s_mkvout, L * 16 + 8)
                pool.dma_start(mk_out[L], k_mem[:]).then_inc(s_mkstore, 16)
                pool.wait_ge(s_mkvout, L * 16 + 16)
                pool.dma_start(mv_out[L], vt_mem[:]).then_inc(s_mvstore, 16)
                pool.wait_ge(s_wout, L * 16 + KD)
                pool.memset(q_own[:], 0.0).then_inc(s_qzero, 1)
                pool.wait_ge(s_mvstore, 16 * (L + 1))
                pool.wait_ge(s_vt, (L + 1) * 4)
                pool.memset(prob_own[:], 0.0).then_inc(s_pzero, 1)
            for i in range(2):
                c = slice(i * KD // 2, (i + 1) * KD // 2)
                pool.wait_ge(s_h, DEPTH * NNORM * KD + (i + 1) * KD // 2)
                pool.dma_start(y_out[:, c, :], h[:, c, :]).then_inc(s_ystore, 16)
            pool.wait_ge(s_ystore, 32)
            for i in range(2):
                pool.wait_ge(s_store[i], 16 * (5 - i) * DEPTH)
            pool.wait_ge(s_mkstore, 16 * DEPTH)
            pool.wait_ge(s_mvstore, 16 * DEPTH)
            pool.wait_ge(s_tstore, 16 * DEPTH)


def kernel(x_prompt, x_sample, mem_prompt, state_ssm, state_conv, state_ret, cache_mem_k, cache_mem_v,
           norm_mix, w_in, conv_w, conv_b, dt_bias, a_log, d_skip, ssd_gain, ret_gain, w_out,
           norm_mem, w_mq, w_mk, w_mv, w_mo, norm_ffn, w_rg, b_rg, w_re, b_re, w_gate, w_up, w_down,
           norm_final):
    import concourse.bacc as bacc
    from concourse.bass_utils import run_bass_kernel_spmd

    f = lambda a: np.asarray(a)

    def features(a):
        a = f(a)
        return np.moveaxis(a.reshape(*a.shape[:-2], a.shape[-2] // P, P, a.shape[-1]), -3, -2)

    def slabs(w):
        k, c = w.shape
        return w.reshape(k // P, P, c // P, P).transpose(2, 1, 0, 3)

    def quads(w):
        w = w.reshape(w.shape[0], P, -1)
        per = QUAD // w.shape[2]
        return w.reshape(-1, per, P, w.shape[2]).transpose(0, 2, 1, 3).reshape(-1, P, QUAD)

    w_in, w_out = f(w_in), f(w_out)
    w_gate, w_up, w_down = f(w_gate), f(w_up), f(w_down)
    offs = np.cumsum([0, D, CC * P, H, RH * DK, RH * DK, D, D])
    state_conv, state_ssm, state_ret = f(state_conv), f(state_ssm), f(state_ret)
    cache_mem_k, cache_mem_v = f(cache_mem_k), f(cache_mem_v)
    stream = np.zeros((DEPTH, QUADS, P, QUAD), np.float32)
    for l in range(DEPTH):
        z, xbc, dt, q, k, v, g = [w_in[l][:, offs[i]:offs[i + 1]] for i in range(7)]
        st = stream[l]
        for at, w in ((Q_V, v), (Q_K, k), (Q_Q, q), (Q_XBC, xbc), (Q_Z, z), (Q_G, g), (Q_OUT, w_out[l]),
                      (Q_MQ, f(w_mq)[l]), (Q_MO, f(w_mo)[l])):
            r = quads(slabs(w))
            st[at:at + len(r)] = r
        st[Q_DT, :, 0:KD * H] = dt.reshape(KD, P, H).transpose(1, 0, 2).reshape(P, -1)
        c = state_conv[l].reshape(DB, CW - 1, CC, P).transpose(3, 2, 0, 1)
        st[Q_DT, :, KD * H:KD * H + CC * DB * (CW - 1)] = c.reshape(P, -1)
        both = np.concatenate([state_ssm[l].transpose(0, 3, 1, 2).reshape(DB, P, 1024),
                               state_ret[l].transpose(0, 2, 1, 3).reshape(DB, P, 1024)], 2)
        st[Q_MEM] = quads(slabs(np.concatenate([f(w_mk)[l], f(w_mv)[l]], 1)))
        st[Q_STATE] = both.reshape(4, 2, P, 2048).transpose(0, 2, 1, 3).reshape(4, P, QUAD)
        kc = cache_mem_k[l].reshape(DB, M, KD, P).transpose(0, 3, 2, 1).reshape(DB, P, 2048)
        vc = cache_mem_v[l].reshape(DB, 2, P, D).transpose(0, 2, 1, 3).reshape(DB, P, 2048)
        st[Q_KC:Q_KC + 4] = kc.reshape(4, 2, P, 2048).transpose(0, 2, 1, 3).reshape(4, P, QUAD)
        st[Q_VC:Q_VC + 4] = vc.reshape(4, 2, P, 2048).transpose(0, 2, 1, 3).reshape(4, P, QUAD)
        for e in range(E):
            gs, us = slabs(w_gate[l, e]), slabs(w_up[l, e])
            gu = np.stack([gs, us], 1).reshape(2 * FC, P, SLAB)
            st[Q_MOE + 3 * e:Q_MOE + 3 * e + 2] = quads(gu)
            st[Q_MOE + 3 * e + 2] = w_down[l, e].reshape(FC, P, D).transpose(1, 0, 2).reshape(P, QUAD)

    params = np.zeros((DEPTH, P, PN), np.float32)

    def put(name, l, a):
        params[l, :a.shape[0], PAT[name]:PAT[name] + a.shape[1]] = a

    for l in range(DEPTH):
        for name, a in (("norm_mix", norm_mix), ("norm_mem", norm_mem), ("norm_ffn", norm_ffn),
                        ("ssd_gain", ssd_gain), ("ret_gain", ret_gain)):
            put(name, l, f(a)[l].reshape(KD, P).T)
        put("norm_final", l, f(norm_final).reshape(KD, P).T)
        put("d_skip", l, np.repeat(f(d_skip)[l], HD).reshape(KD, P).T)
        put("conv_b", l, f(conv_b)[l].reshape(CC, P).T)
        put("conv_w", l, f(conv_w)[l].reshape(CW, CC, P).transpose(2, 1, 0).reshape(P, -1))
        put("dt_bias", l, f(dt_bias)[l][:, None])
        put("a_log", l, f(a_log)[l][:, None])
        put("route_b", l, np.tile(np.concatenate([f(b_rg)[l], f(b_re)[l]])[None], (P, 1)))
        w = np.concatenate([f(w_rg)[l], f(w_re)[l]], 1)
        put("route_w", l, w.reshape(KD, P, EG + E).transpose(1, 0, 2).reshape(P, -1))

    tokens = np.concatenate([f(x_prompt).reshape(SEQ, D), f(x_sample).reshape(NS, D)], 0)
    ins = {
        "stream": stream.reshape(DEPTH * QUADS, P, QUAD),
        "params": params,
        "consts": constants(),
        "x_in": np.ascontiguousarray(features(tokens.T)),
        "mem_in": np.ascontiguousarray(features(f(mem_prompt)[0].T)),
    }
    outs = {"y_out": (P, KD, T), "st_out": (DEPTH, 1 + DB, P, 2048), "conv_out": (DEPTH, P, CC, (CW - 1) * (1 + DB)),
            "mk_out": (DEPTH, P, KD, M), "mv_out": (DEPTH, P, KD, M)}
    nc = bacc.Bacc("TRN2", target_bir_lowering=False, num_devices=1)
    aps = [nc.dram_tensor(n, a.shape, F32, kind="ExternalInput").ap() for n, a in ins.items()]
    aps += [nc.dram_tensor(n, s, F32, kind="ExternalOutput").ap() for n, s in outs.items()]
    build(nc, *aps)
    r = run_bass_kernel_spmd(nc, [ins], core_ids=[0]).results[0]

    y = np.asarray(r["y_out"]).transpose(2, 1, 0).reshape(T, D)
    st = np.asarray(r["st_out"])
    ssm = st[..., 0:1024].reshape(DEPTH, 1 + DB, N, H, HD).transpose(0, 1, 3, 4, 2)
    ret = st[..., 1024:].reshape(DEPTH, 1 + DB, DK, RH, DV).transpose(0, 1, 3, 2, 4)
    conv = np.asarray(r["conv_out"]).reshape(DEPTH, P, CC, 1 + DB, CW - 1).transpose(0, 3, 4, 2, 1)
    conv = conv.reshape(DEPTH, 1 + DB, CW - 1, CC * P)

    def memory(a):
        return np.asarray(a).transpose(0, 3, 2, 1).reshape(DEPTH, 1, M, XH, DV)

    c = np.ascontiguousarray
    return (c(y[:SEQ].reshape(1, SEQ, D)), c(y[SEQ:].reshape(DB, DS, D)), c(ssm[:, :1]), c(conv[:, :1]), c(ret[:, :1]),
            c(memory(r["mk_out"])), c(memory(r["mv_out"])), c(ssm[:, 1:]), c(conv[:, 1:]), c(ret[:, 1:]))
```
